# Optimizing a Trainium2 kernel written in Bass

```python
import math
import jax, jax.numpy as jnp
from jax import lax
import numpy as np

D_MODEL = 1024
BATCH = 1
SEQ = 512
DEPTH = 2
DEC_BATCH = 1
DEC_SEQ = 32
PAST_LEN = 256

CHUNK = 64
N_A_LAYERS = DEPTH // 2
N_B_LAYERS = DEPTH - N_A_LAYERS
CONV_CH = D_MODEL
CONV_WIDTH = 31
N_HEADS = 16
QK_NOPE = 64
QK_ROPE = 32
V_HEAD = 64
KV_LORA = 256
Q_LORA = 512
ROPE_THETA = 10000.0
QBLOCK = 128
NORM_EPS = 1e-6
ATTN_SCALE = 1.0 / math.sqrt(QK_NOPE + QK_ROPE)

kernel_name = 'yoco_conformer_conv_mla_stream_step'

def rmsnorm(x, g):
    xf = x.astype(jnp.float32)
    y = xf * lax.rsqrt(jnp.mean(xf * xf, axis=-1, keepdims=True) + NORM_EPS)
    return (y * g.astype(jnp.float32)).astype(x.dtype)

def layernorm(x, g, b):
    xf = x.astype(jnp.float32)
    mu = jnp.mean(xf, axis=-1, keepdims=True)
    xc = xf - mu
    y = xc * lax.rsqrt(jnp.mean(xc * xc, axis=-1, keepdims=True) + NORM_EPS)
    return (y * g.astype(jnp.float32) + b.astype(jnp.float32)).astype(x.dtype)

def rope(x, pos):
    half = x.shape[-1] // 2
    inv = ROPE_THETA ** (-jnp.arange(half, dtype=jnp.float32) / half)
    ang = pos.astype(jnp.float32)[:, None] * inv[None, :]
    shape = (1, pos.shape[0]) + (1,) * (x.ndim - 3) + (half,)
    cos = jnp.cos(ang).reshape(shape)
    sin = jnp.sin(ang).reshape(shape)
    xf = x.astype(jnp.float32)
    x1, x2 = xf[..., :half], xf[..., half:]
    return jnp.concatenate([x1 * cos - x2 * sin, x2 * cos + x1 * sin], axis=-1).astype(x.dtype)

def conv_module(u, buf, w_in, w_dw, b_dw, g_ln, b_ln, w_out):
    a, gl, z = jnp.split(u @ w_in, 3, axis=-1)
    v = a * jax.nn.sigmoid(gl)
    vp = jnp.concatenate([buf.astype(v.dtype), v], axis=1)
    y = lax.conv_general_dilated(vp, w_dw[:, None, :].astype(vp.dtype), window_strides=(1,),
                                 padding='VALID', dimension_numbers=('NWC', 'WIO', 'NWC'),
                                 feature_group_count=CONV_CH) + b_dw
    y = jax.nn.silu(layernorm(y, g_ln, b_ln))
    out = (y * jax.nn.silu(z)) @ w_out
    return out, vp[:, vp.shape[1] - (CONV_WIDTH - 1):]

def mla_kv_side(h, pos, g_kv_in, w_kv_a, g_kv_a):
    lat = rmsnorm(h, g_kv_in) @ w_kv_a
    c = rmsnorm(lat[..., :KV_LORA], g_kv_a)
    kr = rope(lat[..., KV_LORA:], pos)
    return c, kr

def latent_attention(q_nope, q_rope, q_pos, c, kr, k_pos, w_uk, w_uv):
    q_lat = jnp.einsum('bthn,chn->bthc', q_nope, w_uk)
    s = (jnp.einsum('bthc,bsc->bhts', q_lat, c).astype(jnp.float32)
         + jnp.einsum('bthr,bsr->bhts', q_rope, kr).astype(jnp.float32)) * ATTN_SCALE
    allowed = (k_pos[None, :] // CHUNK) <= (q_pos[:, None] // CHUNK)
    s = jnp.where(allowed[None, None], s, -jnp.inf)
    p = jax.nn.softmax(s, axis=-1).astype(c.dtype)
    o_lat = jnp.einsum('bhts,bsc->bthc', p, c)
    return jnp.einsum('bthc,chv->bthv', o_lat, w_uv)

def mla_mixer(u, pos, c, kr, k_pos, blocked, w_b_in, g_q_a, w_q_b, w_kv_b, w_b_out):
    B, T, _ = u.shape
    p = u @ w_b_in
    qa, z = p[..., :Q_LORA], p[..., Q_LORA:]
    q = (rmsnorm(qa, g_q_a) @ w_q_b).reshape(B, T, N_HEADS, QK_NOPE + QK_ROPE)
    q_nope = q[..., :QK_NOPE]
    q_rope = rope(q[..., QK_NOPE:], pos)
    w_kvb = w_kv_b.reshape(KV_LORA, N_HEADS, QK_NOPE + V_HEAD)
    w_uk, w_uv = w_kvb[..., :QK_NOPE], w_kvb[..., QK_NOPE:]
    if blocked:
        nb = T // QBLOCK
        split = lambda a: a.reshape((B, nb, QBLOCK) + a.shape[2:]).swapaxes(0, 1)
        def blk(args):
            qn, qr, qp = args
            return latent_attention(qn, qr, qp, c, kr, k_pos, w_uk, w_uv)
        o = lax.map(blk, (split(q_nope), split(q_rope), pos.reshape(nb, QBLOCK)))
        o = o.swapaxes(0, 1).reshape(B, T, N_HEADS, V_HEAD)
    else:
        o = latent_attention(q_nope, q_rope, pos, c, kr, k_pos, w_uk, w_uv)
    o = o.reshape(B, T, N_HEADS * V_HEAD)
    return (o * jax.nn.silu(z)) @ w_b_out

def trunk(x, pos, conv_bufs, past_c, past_kr, blocked,
          g_pre, g_post, w_a_in, w_a_dw, b_a_dw, g_a_ln, b_a_ln, w_a_out,
          g_kv_in, w_kv_a, g_kv_a, w_kv_b, w_b_in, g_q_a, w_q_b, w_b_out):
    h = x
    new_conv = []
    c_new = kr_new = None
    c_all = kr_all = k_pos = None
    for layer in range(DEPTH):
        u = rmsnorm(h, g_pre[layer])
        if layer < N_A_LAYERS:
            i = layer
            out, buf = conv_module(u, conv_bufs[i], w_a_in[i], w_a_dw[i], b_a_dw[i],
                                   g_a_ln[i], b_a_ln[i], w_a_out[i])
            new_conv.append(buf)
        else:
            if layer == N_A_LAYERS:
                c_new, kr_new = mla_kv_side(h, pos, g_kv_in, w_kv_a, g_kv_a)
                if past_c is None:
                    c_all, kr_all, k_pos = c_new, kr_new, pos
                else:
                    c_all = jnp.concatenate([past_c.astype(c_new.dtype), c_new], axis=1)
                    kr_all = jnp.concatenate([past_kr.astype(kr_new.dtype), kr_new], axis=1)
                    k_pos = jnp.arange(past_c.shape[1] + x.shape[1])
            j = layer - N_A_LAYERS
            out = mla_mixer(u, pos, c_all, kr_all, k_pos, blocked,
                            w_b_in[j], g_q_a[j], w_q_b[j], w_kv_b, w_b_out[j])
        h = h + rmsnorm(out, g_post[layer])
    return h, jnp.stack(new_conv, axis=0), c_new, kr_new

def setup_inputs(seed: int = 0) -> dict:
    key = jax.random.key(seed)
    ks = jax.random.split(key, 24)
    f32 = jnp.float32
    nrm = lambda k, shape, fan: jax.random.normal(k, shape, f32) * (fan ** -0.5)
    gain = lambda k, shape: 1.0 + 0.05 * jax.random.normal(k, shape, f32)
    small = lambda k, shape: 0.02 * jax.random.normal(k, shape, f32)
    return {
        'x_prompt': jax.random.normal(ks[0], (BATCH, SEQ, D_MODEL), f32),
        'x_sample': jax.random.normal(ks[1], (DEC_BATCH, DEC_SEQ, D_MODEL), f32),
        'state_conv': jax.random.normal(ks[2], (N_A_LAYERS, DEC_BATCH, CONV_WIDTH - 1, CONV_CH), f32),
        'cache_kv_latent': jax.random.normal(ks[3], (DEC_BATCH, PAST_LEN, KV_LORA), f32),
        'cache_k_rope': jax.random.normal(ks[4], (DEC_BATCH, PAST_LEN, QK_ROPE), f32),
        'g_pre': gain(ks[5], (DEPTH, D_MODEL)),
        'g_post': gain(ks[6], (DEPTH, D_MODEL)),
        'w_a_in': nrm(ks[7], (N_A_LAYERS, D_MODEL, 3 * CONV_CH), D_MODEL),
        'w_a_dw': nrm(ks[8], (N_A_LAYERS, CONV_WIDTH, CONV_CH), CONV_WIDTH),
        'b_a_dw': small(ks[9], (N_A_LAYERS, CONV_CH)),
        'g_a_ln': gain(ks[10], (N_A_LAYERS, CONV_CH)),
        'b_a_ln': small(ks[11], (N_A_LAYERS, CONV_CH)),
        'w_a_out': nrm(ks[12], (N_A_LAYERS, CONV_CH, D_MODEL), CONV_CH),
        'g_kv_in': gain(ks[13], (D_MODEL,)),
        'w_kv_a': nrm(ks[14], (D_MODEL, KV_LORA + QK_ROPE), D_MODEL),
        'g_kv_a': gain(ks[15], (KV_LORA,)),
        'w_kv_b': nrm(ks[16], (KV_LORA, N_HEADS * (QK_NOPE + V_HEAD)), KV_LORA),
        'w_b_in': nrm(ks[17], (N_B_LAYERS, D_MODEL, Q_LORA + N_HEADS * V_HEAD), D_MODEL),
        'g_q_a': gain(ks[18], (N_B_LAYERS, Q_LORA)),
        'w_q_b': nrm(ks[19], (N_B_LAYERS, Q_LORA, N_HEADS * (QK_NOPE + QK_ROPE)), Q_LORA),
        'w_b_out': nrm(ks[20], (N_B_LAYERS, N_HEADS * V_HEAD, D_MODEL), N_HEADS * V_HEAD),
    }

def reference(x_prompt, x_sample, state_conv, cache_kv_latent, cache_k_rope,
              g_pre, g_post, w_a_in, w_a_dw, b_a_dw, g_a_ln, b_a_ln, w_a_out,
              g_kv_in, w_kv_a, g_kv_a, w_kv_b, w_b_in, g_q_a, w_q_b, w_b_out):
    weights = (g_pre, g_post, w_a_in, w_a_dw, b_a_dw, g_a_ln, b_a_ln, w_a_out,
               g_kv_in, w_kv_a, g_kv_a, w_kv_b, w_b_in, g_q_a, w_q_b, w_b_out)
    pos_p = jnp.arange(x_prompt.shape[1])
    zero_bufs = jnp.zeros((N_A_LAYERS, x_prompt.shape[0], CONV_WIDTH - 1, CONV_CH), x_prompt.dtype)
    y_prompt, conv_state_prompt, kv_latent_prompt, k_rope_prompt = trunk(
        x_prompt, pos_p, zero_bufs, None, None, True, *weights)
    past_len = cache_kv_latent.shape[1]
    pos_s = past_len + jnp.arange(x_sample.shape[1])
    y_sample, conv_state_sample, kv_latent_sample, k_rope_sample = trunk(
        x_sample, pos_s, state_conv, cache_kv_latent, cache_k_rope, False, *weights)
    return (y_prompt, y_sample, conv_state_prompt, kv_latent_prompt, k_rope_prompt,
            conv_state_sample, kv_latent_sample, k_rope_sample)


_drawn_inputs = setup_inputs


def setup_inputs(seed=0):
    import zlib

    import numpy as np

    out = dict(_drawn_inputs(seed))
    spreads = {}
    factors = {}
    for name, (base, spread) in spreads.items():
        noise = np.random.default_rng([zlib.crc32(name.encode()), seed]).standard_normal(out[name].shape)
        drawn = base * np.exp(spread * noise) if base else spread * noise
        out[name] = __import__('jax').numpy.asarray(drawn.astype(out[name].dtype))
    for name, factor in factors.items():
        out[name] = (out[name] * factor).astype(out[name].dtype)
    return out
```

```python
from contextlib import ExitStack

import concourse.bass as bass
from concourse import mybir

F32 = mybir.dt.float32
F32R = mybir.dt.float32r
BF16 = mybir.dt.bfloat16
ALU = mybir.AluOpType
ACT = mybir.ActivationFunctionType
AX_X = mybir.AxisListType.X

P = 128
D = 1024
KD = D // P
SEQ, DEC, PAST = 512, 32, 256
T = SEQ + DEC
HB = T // 2
NB = 2
LORA = 256
KL = LORA // P
QL = 512
KQ = QL // P
HEADS, NOPE, ROPE, VH = 16, 64, 32, 64
GH = 4
NG = HEADS // GH
KEYS = T + PAST
SKEYS = KEYS - SEQ
WIDTH = 31
HIST = WIDTH - 1
VCOLS = HIST + SEQ + HIST + DEC
CCOLS = VCOLS - HIST
CHUNK = 64
EPS = 1e-6
SCALE = 1.0 / float(NOPE + ROPE) ** 0.5
NEG = -1e30

STAGES = 5
RING = 16
POOL_TAPS = 4
DVE_TAPS = WIDTH - POOL_TAPS

U_IN = 0
U_AO = U_IN + 8 * KD
U_KV = U_AO + 2 * KD
U_Q = U_KV + KD
U_Z = U_Q + KD
U_G = U_Z + 2 * KD
GU = KQ + KL
U_BO = U_G + NG * GU
UNITS = U_BO + 2 * KD

TASKS3 = ([("kv", m, 0) for m in range(3)] + [("q", m, 0) for m in range(KQ)]
          + [("kv", m, 1) for m in range(3)] + [("q", m, 1) for m in range(KQ)]
          + [("z", m, b) for m in range(KD) for b in range(2)])
SQUARED = [p for p, (kind, m, _) in enumerate(TASKS3) if kind == "q" or (kind == "kv" and m < KL)]
GTASKS = ([("rope", 2, b, "dve") for b in range(2)] + [("nope", m, b, "act") for m in range(2) for b in range(2)]
          + [("k", m, h, ("act", "dve")[h]) for m in range(2) for h in range(2)]
          + [("v", t, 0, ("dve", "act")[t % 2]) for t in range(7)])
NQTASK, NTASK = 6, len(GTASKS)
KT = 7
NS = 9
NITEM = NG * NS
FTASKS = [(m, b) for c in range(2) for b in range(2) for m in range(4 * c, 4 * c + 4)]


def evacs(eng, g, i):
    each = sum(t[3] == eng for t in GTASKS)
    return g * each + sum(t[3] == eng for t in GTASKS[:i + 1])


V_PRE0, V_PRE1, V_POST0, V_POST1 = 0, 8, 16, 24
V_DW = 32
V_BDW = V_DW + 8 * WIDTH
V_GLN, V_BLN, V_KVIN = V_BDW + 8, V_BDW + 16, V_BDW + 24
V_KVA = V_KVIN + 8
V_QA = V_KVA + 2
NVEC = V_QA + 4


def unit_cols(u):
    if u < U_AO:
        return 384
    if U_KV <= u < U_Q:
        return 320
    if U_G <= u < U_BO and (u - U_G) % GU < KQ:
        return 384
    return 512


def unit_gain(u):
    if U_KV <= u < U_Q:
        return V_KVIN + (u - U_KV)
    if U_Q <= u < U_G:
        return V_PRE1 + (u - U_Q) % KD
    return None


def build(nc, x_t, state_t, ckv_t, ckr_t, w_in, w_ao, w_kv, w_bi, w_qb, w_kb, w_bo, vecs_d, cc_d, ss_d, krs_d,
          y_out, conv_out, c_out, kr_out):
    ctx = ExitStack()
    with ctx:
        def sem(name):
            return ctx.enter_context(nc.semaphore(name))


        def keep(name, shape, dt=F32, side="left"):
            return ctx.enter_context(nc.sbuf_tensor(name, shape, dt, side=side))

        def region(side, *specs):
            st = ExitStack()
            return st, [st.enter_context(nc.sbuf_tensor(n, s, d, side=side)) for n, s, d in specs]

        xT = keep("xT", [P, KD, T])
        zs = keep("zs", [P, KD, T])
        rlow_hi = keep("rlow_hi", [P, 8, 512], F32R)
        rlow_lo = keep("rlow_lo", [P, 8, 512], F32R)
        stage = keep("stage", [P, STAGES, 512])
        cc = keep("cc", [P, T])
        ss = keep("ss", [P, T])
        kr = keep("kr", [P, KEYS])
        vecs = keep("vecs", [P, NVEC])
        ones = keep("ones", [P, P])
        mean_b = keep("mean_b", [P, T])
        rstd_b = keep("rstd_b", [P, T])
        var_b = keep("var_b", [P, T])
        early = keep("early", [1, P], BF16)
        neg = keep("neg", [1, CHUNK], BF16)
        negmax = keep("negmax", [P, 2, 2])
        rowmax = keep("rowmax", [P, 2, 2])
        rowsum = keep("rowsum", [P, 2, 2])
        rinv = keep("rinv", [P, 2, 2])
        sq = keep("sq", [P, 4, HB], F32, "right")

        left, (act_hi, act_lo, rtop_hi, rtop_lo) = region(
            "left", ("act_hi", [P, KD, T], F32R), ("act_lo", [P, KD, T], F32R),
            ("rtop_hi", [P, 8, 512], F32R), ("rtop_lo", [P, 8, 512], F32R))
        right, (y, v, sig, a_sb, prod, part, acc, state) = region(
            "right", ("y", [P, KD, T], F32), ("v", [P, 2, VCOLS], F32), ("sig", [P, T], F32),
            ("a_sb", [P, T], F32), ("prod", [P, 2, CCOLS], F32), ("part", [P, 2, CCOLS], F32),
            ("acc", [P, 4, CCOLS], F32), ("state", [P, KD, HIST], F32))
        right.close()
        qn_hi = keep("qn_hi", [P, KQ, T], F32R, "right")
        qn_lo = keep("qn_lo", [P, KQ, T], F32R, "right")
        c_hi = keep("c_hi", [P, KL, KEYS], F32R, "right")
        c_lo = keep("c_lo", [P, KL, KEYS], F32R, "right")
        right, (qa, cf, kr_ps) = region("right", ("qa", [P, KQ, T], F32), ("cf", [P, KL, KEYS], F32),
                                        ("kr_ps", [2 * ROPE, HB], F32))
        right.close()
        left.close()
        left, (kT, probs, qT, vt, ident) = region(
            "left", ("kT", [P, 2 * GH, KEYS], F32), ("probs", [P, 2, 2, 512], F32),
            ("qT", [P, 2 * GH, T], F32), ("vt", [P, 2 * KT, GH * VH], F32),
            ("ident", [P, P], F32))
        right, (pT, rope_a, rope_r) = region(
            "right", ("pT", [P, 2, 512], F32), ("rope_a", [P, 2, HB], F32), ("rope_r", [P, 2, T], F32))
        right.close()
        left.close()
        left, (o_hi, o_lo, btop_hi, btop_lo) = region(
            "left", ("o_hi", [P, KD, T], F32R), ("o_lo", [P, KD, T], F32R),
            ("btop_hi", [P, 8, 512], F32R), ("btop_lo", [P, 8, 512], F32R))
        left.close()

        ps = ctx.enter_context(nc.psum_tensor("ps", [P, 8, 512], F32))

        x_in = [sem(f"x_in{i}") for i in range(4)]
        vecs_in, tables_in, state_in = sem("vecs_in"), sem("tables_in"), sem("state_in")
        cache_in, c_stored = sem("cache_in"), sem("c_stored")
        stage_in = [sem(f"stage_in{i}") for i in range(STAGES)]
        conv_out_done, rope_moved, krows_in, outs_done = (
            sem("conv_out_done"), sem("rope_moved"), sem("krows_in"), sem("outs_done"))
        scaled, hi_done = sem("scaled"), sem("hi_done")
        xsq_done, uhi_done = sem("xsq_done"), sem("uhi_done")
        sqrt_done = sem("sqrt_done")
        mt_evac, sig_done, prod_done, ysq_done, gate_done = (
            sem("mt_evac"), sem("sig_done"), sem("prod_done"), sem("ysq_done"), sem("gate_done"))
        ln_silu, yz_hi = sem("ln_silu"), sem("yz_hi")
        o_evac, osq_done, hsq_done, xn_hi = sem("o_evac"), sem("osq_done"), sem("hsq_done"), sem("xn_hi")
        p_evac, psq_done, c_hi_done, qn_hi_done = sem("p_evac"), sem("psq_done"), sem("c_hi_done"), sem("qn_hi_done")
        g_evac_act, exp_done, pt_evac_act = sem("g_evac_act"), sem("exp_done"), sem("pt_evac_act")
        oo_hi, f_evac, fsq_done = sem("oo_hi"), sem("f_evac"), sem("fsq_done")
        const_set, dve_self, var_done, rstd_done = sem("const_set"), sem("dve_self"), sem("var_done"), sem("rstd_done")
        u_full, u_lo = sem("u_full"), sem("u_lo")
        tap_done, conv_done = sem("tap_done"), sem("conv_done")
        ln_norm, yz_full = sem("ln_norm"), sem("yz_full")
        h_done, xn_full = sem("h_done"), sem("xn_full")
        kr_done, c_full, qn_full = sem("kr_done"), sem("c_full"), sem("qn_full")
        g_evac_dve, rope_done, max_done, prob_done, pt_evac_dve, att_done = (
            sem("g_evac_dve"), sem("rope_done"), sem("max_done"), sem("prob_done"), sem("pt_evac_dve"), sem("att_done"))
        oo_lo, y_done = sem("oo_lo"), sem("y_done")
        pool_set, lo_done, state_set, v_done, padd_done, y_ready = (
            sem("pool_set"), sem("lo_done"), sem("state_set"), sem("v_done"), sem("padd_done"), sem("y_ready"))
        yz_lo, xn_lo, c_lo_done, qn_lo_done = sem("yz_lo"), sem("xn_lo"), sem("c_lo_done"), sem("qn_lo_done")
        xstat_done, mt_done, ystat_done, o_done, ostat_done, hstat_done = (
            sem("xstat_done"), sem("mt_done"), sem("ystat_done"), sem("o_done"), sem("ostat_done"), sem("hstat_done"))
        p_done, pstat_done, g_done = sem("p_done"), sem("pstat_done"), sem("g_done")
        scores_done, pt_done, pv_done, f_done, fstat_done = (
            sem("scores_done"), sem("pt_done"), sem("pv_done"), sem("f_done"), sem("fstat_done"))

        def blk(b):
            return slice(b * HB, (b + 1) * HB)

        def pair(b0):
            return ps[:, b0:b0 + 2, 0:HB]

        def two(ap):
            return ap.rearrange("p (b t) -> p b t", b=NB)

        def slot(u):
            n = unit_cols(u)
            if u >= U_G:
                m = u - U_G
                if m < NG * GU + KD:
                    return rlow_hi[:, m % 8, 0:n], rlow_lo[:, m % 8, 0:n]
                return btop_hi[:, m % 8, 0:n], btop_lo[:, m % 8, 0:n]
            s = u % RING
            if s < 8:
                return rlow_hi[:, s, 0:n], rlow_lo[:, s, 0:n]
            return rtop_hi[:, s - 8, 0:n], rtop_lo[:, s - 8, 0:n]

        def wait_slot(act, u):
            if u < RING:
                return
            if u < U_KV:
                act.wait_ge(mt_done, 3 * (u // 8 - 1))
            elif u < U_Q:
                act.wait_ge(o_done, 12)
            elif u < U_Z:
                act.wait_ge(o_done, 16)
            elif u < U_Z + KD:
                act.wait_ge(p_done, TASKS3.index(("kv", 2, 1)) + 1)
            elif u < U_G:
                act.wait_ge(p_done, TASKS3.index(("q", 3, 1)) + 1)
            elif u < U_G + 8:
                act.wait_ge(p_done, TASKS3.index(("z", 3, 1)) + 1)
            elif u < U_BO + KD:
                g, i = divmod(u - U_G - 8, GU)
                act.wait_ge(g_done, NTASK * g + (NQTASK if i < KQ else NTASK))
            else:
                act.wait_ge(pv_done, NITEM)

        def unit_src(u):
            n = unit_cols(u)
            for first, src in ((U_BO, w_bo), (U_Q, None), (U_KV, w_kv), (U_AO, w_ao), (U_IN, w_in)):
                if u >= first:
                    break
            if src is not None:
                return src[u - first]
            if u < U_G:
                return w_bi[u - U_Q]
            g, i = divmod(u - U_G, GU)
            return w_qb[g * KQ + i] if i < KQ else w_kb[g * KL + i - KQ]

        def hi(act, u):
            raw = stage[:, u % STAGES, 0:unit_cols(u)]
            act.wait_ge(stage_in[u % STAGES], 16 * (u // STAGES + 1))
            gain = unit_gain(u)
            if gain is not None:
                nc.scalar.activation(raw, raw, ACT.Copy, scale=vecs[:, gain:gain + 1]).then_inc(scaled, 1)
            wait_slot(act, u)
            if gain is not None:
                act.wait_ge(scaled, u - U_KV + 1)
            nc.scalar.activation(slot(u)[0], raw, ACT.Copy).then_inc(hi_done, 1)

        def lo(pool, u):
            pool.wait_ge(hi_done, u + 1)
            h, l = slot(u)
            nc.gpsimd.tensor_tensor(l, stage[:, u % STAGES, 0:unit_cols(u)], h.bitcast(F32),
                                    ALU.subtract).then_inc(lo_done, 1)

        def ready(pe, u):
            pe.wait_ge(lo_done, u + 1)

        def mm3(out, w, xh, xl, start, stop):
            wh, wl = w
            nc.tensor.matmul(out, wh, xh, start=start, stop=False)
            nc.tensor.matmul(out, wh, xl, start=False, stop=False)
            return nc.tensor.matmul(out, wl, xh, start=False, stop=stop)

        def cols(w, c, n=P):
            return w[0][:, c:c + n], w[1][:, c:c + n]

        block = ctx.enter_context(nc.Block())

        @block.sync
        def _(sp):
            def load(u):
                if u >= STAGES:
                    sp.wait_ge(lo_done, u - STAGES + 1)
                sp.dma_start(stage[:, u % STAGES, 0:unit_cols(u)], unit_src(u)).then_inc(stage_in[u % STAGES], 16)

            sp.dma_start(vecs[:], vecs_d).then_inc(vecs_in, 16)
            for i in range(4):
                sp.dma_start(xT[:, 2 * i:2 * i + 2, :], x_t[:, 2 * i:2 * i + 2, :]).then_inc(x_in[i], 16)
            for u in range(8):
                load(u)
                if u == 2:
                    sp.dma_start(state[:], state_t).then_inc(state_in, 16)
            for j in range(KD):
                for u in range(8 * (j + 1), 8 * (j + 2)):
                    load(u)
                sp.wait_ge(v_done, j + 1)
                sp.dma_start(conv_out[:, j, 0:HIST], v[:, j % 2, SEQ:SEQ + HIST]).then_inc(conv_out_done, 16)
                sp.dma_start(conv_out[:, j, HIST:2 * HIST], v[:, j % 2, VCOLS - HIST:VCOLS]).then_inc(conv_out_done, 16)
            for u in range(U_AO + KD, U_KV):
                load(u)
            sp.dma_start(cc[:], cc_d).then_inc(tables_in, 16)
            sp.dma_start(ss[:], ss_d).then_inc(tables_in, 16)
            sp.dma_start(kr[ROPE:2 * ROPE, 0:T], krs_d).then_inc(tables_in, 16)
            sp.dma_start(kr[2 * ROPE:3 * ROPE, T:KEYS], ckr_t).then_inc(cache_in, 16)
            for u in range(U_KV, U_KV + 4):
                load(u)
            sp.wait_ge(yz_lo, 2 * KD)
            sp.dma_start(cf[:, :, T:KEYS], ckv_t).then_inc(cache_in, 16)
            for u in range(U_KV + 4, U_G + GU):
                load(u)
            sp.wait_ge(c_full, KL)
            sp.dma_start(c_out, cf[:, :, 0:T]).then_inc(c_stored, 16)
            sp.wait_ge(kr_done, 2)
            sp.dma_start(kr_out, kr[2 * ROPE:3 * ROPE, 0:T]).then_inc(outs_done, 16)
            sp.wait_ge(p_done, len(TASKS3))
            for h in range(2 * GH):
                sp.dma_start(kT[2 * ROPE:3 * ROPE, h, :], kr[2 * ROPE:3 * ROPE, :]).then_inc(krows_in, 16)
            for g in range(NG):
                sp.wait_ge(rope_done, 2 * (g + 1))
                for i in range(GH):
                    h = GH * (g % 2) + i
                    for half in range(2):
                        sp.dma_start(qT[NOPE + 16 * half:NOPE + 16 * half + 16, h, :],
                                     rope_r[64 * half + 16 * i:64 * half + 16 * i + 16, g % 2, :]).then_inc(rope_moved, 16)
                first = U_G + GU * (g + 1)
                for u in range(first, first + GU if g + 1 < NG else UNITS):
                    load(u)
            for n in range(2 * KD):
                b, m = divmod(n, KD)
                sp.wait_ge(y_done, n + 1)
                sp.dma_start(y_out[:, m, blk(b)], xT[:, m, blk(b)]).then_inc(outs_done, 16)
            sp.wait_ge(outs_done, 16 * (1 + 2 * KD))
            sp.wait_ge(c_stored, 16)
            sp.wait_ge(conv_out_done, 32 * KD)

        @block.scalar
        def _(act):
            act.wait_ge(vecs_in, 16)
            for k in range(KD):
                if k % 2 == 0:
                    act.wait_ge(x_in[k // 2], 16)
                if k >= 2:
                    act.wait_ge(xstat_done, k - 1)
                nc.scalar.activation(sq[:, 2 * (k % 2):2 * (k % 2) + 2, :], two(xT[:, k, :]), ACT.Square).then_inc(xsq_done, 1)
            for u in range(0, 4):
                hi(act, u)

            def sqrt_of(n, b=None):
                s = slice(0, T) if b is None else blk(b)
                act.wait_ge(var_done, n + 1)
                nc.scalar.activation(var_b[:, s], var_b[:, s], ACT.Sqrt).then_inc(sqrt_done, 1)

            sqrt_of(0)
            for k in range(KD):
                act.wait_ge(u_full, k + 1)
                nc.scalar.activation(act_hi[:, k, :], y[:, k, :], ACT.Copy).then_inc(uhi_done, 1)
                if k % 2:
                    hi(act, 4 + k // 2)

            def ysquare(j):
                act.wait_ge(y_ready, j + 1)
                if j >= 2:
                    act.wait_ge(ystat_done, j - 1)
                elif j == 0:
                    act.wait_ge(xstat_done, KD)
                nc.scalar.activation(sq[:, 2 * (j % 2):2 * (j % 2) + 2, :], two(y[:, j, :]), ACT.Square).then_inc(ysq_done, 1)

            for j in range(KD):
                nxt = 8 * (j + 1)
                for u in range(4):
                    hi(act, nxt + u)
                act.wait_ge(mt_done, 3 * j + 1)
                if j >= 1:
                    act.wait_ge(v_done, j)
                nc.scalar.activation(two(sig[:]), pair(2 * ((3 * j) % 2)), ACT.Sigmoid).then_inc(mt_evac, 1)
                for u in range(4, 6):
                    hi(act, nxt + u)
                act.wait_ge(mt_done, 3 * j + 2)
                nc.scalar.activation(two(a_sb[:]), pair(2 * ((3 * j + 1) % 2)), ACT.Copy).then_inc(mt_evac, 1)
                for u in range(6, 8):
                    hi(act, nxt + u)
                for i in range(POOL_TAPS):
                    w, n = DVE_TAPS + i, POOL_TAPS * j + i
                    act.wait_ge(v_done, j + 1)
                    adds = 3 * j + (1 if i >= 2 else i - 1)
                    if adds > 0:
                        act.wait_ge(padd_done, adds)
                    nc.scalar.activation(prod[:, n % 2, :], v[:, j % 2, w:w + CCOLS], ACT.Copy,
                                         scale=vecs[:, V_DW + WIDTH * j + w:V_DW + WIDTH * j + w + 1]).then_inc(prod_done, 1)
                act.wait_ge(mt_done, 3 * j + 3)
                nc.scalar.activation(two(zs[:, j, :]), pair(2 * ((3 * j + 2) % 2)), ACT.Copy).then_inc(mt_evac, 1)
                if j >= 2:
                    ysquare(j - 2)
            ysquare(KD - 2)
            act.wait_ge(mt_evac, 3 * KD)
            for j in range(KD):
                nc.scalar.activation(zs[:, j, :], zs[:, j, :], ACT.Silu).then_inc(gate_done, 1)
                hi(act, U_AO + KD + j)
            ysquare(KD - 1)

            def split_yz(n):
                b, k = divmod(n, KD)
                act.wait_ge(yz_full, n + 1)
                nc.scalar.activation(act_hi[:, k, blk(b)], y[:, k, blk(b)], ACT.Copy).then_inc(yz_hi, 1)

            sqrt_of(1)
            for n in range(2 * KD):
                b, k = divmod(n, KD)
                act.wait_ge(ln_norm, n + 1)
                nc.scalar.activation(y[:, k, blk(b)], y[:, k, blk(b)], ACT.Silu, bias=vecs[:, V_BLN + k:V_BLN + k + 1],
                                     scale=vecs[:, V_GLN + k:V_GLN + k + 1]).then_inc(ln_silu, 1)
                if n >= 1:
                    split_yz(n - 1)
            split_yz(2 * KD - 1)

            def evac_o(n):
                b, m = divmod(n, KD)
                act.wait_ge(o_done, n + 1)
                if n >= 2:
                    act.wait_ge(ostat_done, n - 1)
                nc.scalar.activation(sq[:, n % 2, :], ps[:, n % 4, 0:HB], ACT.Square).then_inc(osq_done, 1)
                nc.scalar.activation(zs[:, m, blk(b)], ps[:, n % 4, 0:HB], ACT.Copy).then_inc(o_evac, 1)

            def hsquare(n):
                b, m = divmod(n, KD)
                act.wait_ge(h_done, n + 1)
                if n >= 2:
                    act.wait_ge(hstat_done, n - 1)
                nc.scalar.activation(sq[:, 2 + n % 2, :], xT[:, m, blk(b)], ACT.Square).then_inc(hsq_done, 1)

            def xn_split(n):
                b, m = divmod(n, KD)
                act.wait_ge(xn_full, n + 1)
                nc.scalar.activation(act_hi[:, m, blk(b)], zs[:, m, blk(b)], ACT.Copy).then_inc(xn_hi, 1)

            def evac_p(p):
                kind, m, b = TASKS3[p]
                src = ps[:, p % 4, 0:HB]
                act.wait_ge(p_done, p + 1)
                if p in SQUARED:
                    i = SQUARED.index(p)
                    if i >= 2:
                        act.wait_ge(pstat_done, i - 1)
                    else:
                        act.wait_ge(ostat_done, 2 * KD - 1 + i)
                    nc.scalar.activation(sq[:, i % 2, :], src, ACT.Square).then_inc(psq_done, 1)
                if kind == "z":
                    nc.scalar.activation(zs[:, m, blk(b)], src, ACT.Silu).then_inc(p_evac, 1)
                elif kind == "q":
                    nc.scalar.activation(qa[:, m, blk(b)], src, ACT.Copy).then_inc(p_evac, 1)
                elif m < KL:
                    nc.scalar.activation(cf[:, m, blk(b)], src, ACT.Copy).then_inc(p_evac, 1)
                else:
                    if b:
                        act.wait_ge(kr_done, 1)
                    nc.scalar.activation(kr_ps[:], ps[0:2 * ROPE, p % 4, 0:HB], ACT.Copy).then_inc(p_evac, 1)

            for n in range(2 * KD):
                evac_o(n)
                if n == 9:
                    sqrt_of(2, 0)
                if 10 <= n < 14:
                    for i in ((0, 1), (2, 3), (4, 5, 6), (7,))[n - 10]:
                        hsquare(i)
                if n == 13:
                    sqrt_of(3, 0)
                if n >= 14:
                    for i in range(4 * (n - 14), 4 * (n - 14) + 4):
                        xn_split(i)
                if n >= 12:
                    for i in range(2):
                        hi(act, U_KV + 2 * (n - 12) + i)
            for p in range(len(TASKS3)):
                if p < 4:
                    for i in range(2):
                        hi(act, U_Q + 2 * p + i)
                evac_p(p)
                if p == 1:
                    sqrt_of(4, 1)
                if 2 <= p < 6:
                    for i in ((8, 9), (10, 11), (12, 13, 14), (15,))[p - 2]:
                        hsquare(i)
                if p == 5:
                    sqrt_of(5, 1)
                    for i in range(KD, 2 * KD):
                        xn_split(i)
                if p == 6:
                    act.wait_ge(cache_in, 32)
                    for k in range(KL):
                        nc.scalar.activation(c_hi[:, k, T:KEYS], cf[:, k, T:KEYS], ACT.Copy).then_inc(c_hi_done, 1)
                if 9 <= p < 13:
                    for i in range(2):
                        hi(act, U_Z + 2 * (p - 9) + i)
                if p == 11:
                    sqrt_of(6)
                if p == 13:
                    for k in range(KL):
                        act.wait_ge(c_full, k + 1)
                        nc.scalar.activation(c_hi[:, k, 0:T], cf[:, k, 0:T], ACT.Copy).then_inc(c_hi_done, 1)
                if p == 15:
                    sqrt_of(7)
                if p == 17:
                    for k in range(KQ):
                        act.wait_ge(qn_full, k + 1)
                        nc.scalar.activation(qn_hi[:, k, :], qa[:, k, :], ACT.Copy).then_inc(qn_hi_done, 1)
                if 14 <= p < 22:
                    hi(act, U_Z + KD + p - 14)
                if 22 <= p < 22 + GU:
                    hi(act, U_G + p - 22)

            def gevac(g, i):
                kind, m, half, eng = GTASKS[i]
                if eng != "act":
                    return
                bank = 4 + i % 4 if g == 0 else 7
                act.wait_ge(g_done, NTASK * g + i + 1)
                slot0 = GH * (g % 2) + 2 * m
                if kind == "nope":
                    for e in range(2):
                        last = nc.scalar.activation(qT[0:NOPE, slot0 + e, blk(half)], ps[64 * e:64 * e + 64, bank, 0:HB], ACT.Copy)
                elif kind == "k":
                    for e in range(2):
                        last = nc.scalar.activation(kT[0:NOPE, slot0 + e, 400 * half:400 * half + 400],
                                                    ps[64 * e:64 * e + 64, bank, 0:400], ACT.Copy)
                else:
                    n = min(P, KEYS - P * m)
                    last = nc.scalar.activation(vt[0:n, KT * (g % 2) + m, :], ps[0:n, bank, 0:GH * VH], ACT.Copy)
                last.then_inc(g_evac_act, 1)

            for i in range(NTASK):
                gevac(0, i)
                if i == 5:
                    for u in range(U_G + GU, U_G + 2 * GU):
                        hi(act, u)

            def exps(i):
                s = i % NS
                act.wait_ge(max_done, i + 1)
                if i >= 2:
                    act.wait_ge(pt_done, i - 1)
                n, heads = (P * (s % 4 + 1), 2) if s < 8 else (SKEYS, 1)
                for e in range(heads):
                    last = nc.scalar.activation(probs[:, i % 2, e, 0:n], ps[:, 2 * (i % 2) + e, 0:n], ACT.Exp,
                                                bias=negmax[:, i % 2, e:e + 1], scale=SCALE,
                                                accum_out=rowsum[:, i % 2, e:e + 1])
                last.then_inc(exp_done, 1)

            def pt_evac(i):
                s = i % NS
                n = P * (s % 4 + 1) if s < 8 else 2 * P
                act.wait_ge(pt_done, i + 1)
                nc.scalar.activation(pT[:, 0, 0:n], ps[:, 4, 0:n], ACT.Copy).then_inc(pt_evac_act, 1)

            for i in range(NITEM + 1):
                g, s = divmod(i, NS)
                if i >= 1:
                    pt_evac(i - 1)
                if i == NITEM:
                    break
                exps(i)
                if g + 1 < NG:
                    for t in range(2 * s, min(2 * s + 2, NTASK)):
                        gevac(g + 1, t)
                ahead = {1: 0, 2: 1, 4: 2, 5: 3, 6: 4, 7: 5}.get(s)
                if ahead is not None and U_G + GU * (g + 2) + ahead < U_BO + KD:
                    hi(act, U_G + GU * (g + 2) + ahead)

            def oo_split(n):
                b, k = divmod(n, KD)
                nc.scalar.activation(o_hi[:, k, blk(b)], zs[:, k, blk(b)], ACT.Copy).then_inc(oo_hi, 1)

            def evac_f(n):
                m, b = FTASKS[n]
                act.wait_ge(f_done, n + 1)
                if n >= 2:
                    act.wait_ge(fstat_done, n - 1)
                nc.scalar.activation(sq[:, n % 2, :], ps[:, n % 4, 0:HB], ACT.Square).then_inc(fsq_done, 1)
                nc.scalar.activation(zs[:, m, blk(b)], ps[:, n % 4, 0:HB], ACT.Copy).then_inc(f_evac, 1)

            act.wait_ge(att_done, NITEM)
            for n in range(2 * KD):
                oo_split(n)
            for i in range(KD):
                hi(act, U_BO + KD + i)
            for n in range(2 * KD):
                evac_f(n)
                if n == 13:
                    sqrt_of(8, 0)
            sqrt_of(9, 1)

        @block.vector
        def _(dve):
            self_count = [0]

            def link(ins):
                self_count[0] += 1
                ins.then_inc(dve_self, 1)
                return self_count[0]

            nc.vector.memset(neg[:], NEG)
            nc.vector.memset(early[:, CHUNK:P], 0.0)
            nc.vector.memset(early[:, 0:CHUNK], 1.0)
            nc.vector.memset(ones[:], 1.0).then_inc(const_set, 1)

            def variance(n, src, count, b=None):
                s = slice(0, T) if b is None else blk(b)
                dst = var_b[:, s] if b is not None else two(var_b[:])
                nc.vector.tensor_scalar(dst, src, 1.0 / count, EPS, ALU.mult, ALU.add).then_inc(var_done, 1)

            def inverse(n, dst, b=None):
                s = slice(0, T) if b is None else blk(b)
                dve.wait_ge(sqrt_done, n + 1)
                nc.vector.reciprocal(dst[:, s], var_b[:, s]).then_inc(rstd_done, 1)
                dve.wait_ge(rstd_done, n + 1)

            dve.wait_ge(xstat_done, KD)
            variance(0, pair(4), D)
            inverse(0, rstd_b)

            def u_split(k):
                dve.wait_ge(uhi_done, k + 1)
                nc.vector.tensor_tensor(act_lo[:, k, :], y[:, k, :], act_hi[:, k, :].bitcast(F32),
                                        ALU.subtract).then_inc(u_lo, 1)

            dve.wait_ge(vecs_in, 16)
            for k in range(KD):
                nc.vector.scalar_tensor_tensor(out=y[:, k, :], in0=xT[:, k, :], scalar=vecs[:, V_PRE0 + k:V_PRE0 + k + 1],
                                               in1=rstd_b[:], op0=ALU.mult, op1=ALU.mult).then_inc(u_full, 1)
                if k:
                    u_split(k - 1)
            u_split(KD - 1)

            per_tile = DVE_TAPS + 1
            for j in range(KD):
                dve.wait_ge(v_done, j + 1)
                for w in range(DVE_TAPS):
                    dst = acc[:, 2 * (j % 2) + w % 2, :]
                    src = v[:, j % 2, w:w + CCOLS]
                    tap = vecs[:, V_DW + WIDTH * j + w:V_DW + WIDTH * j + w + 1]
                    if w == 0:
                        ins = nc.vector.tensor_scalar(dst, src, tap, vecs[:, V_BDW + j:V_BDW + j + 1], ALU.mult, ALU.add)
                    elif w == 1:
                        ins = nc.vector.tensor_scalar(dst, src, tap, None, ALU.mult)
                    else:
                        dve.wait_ge(tap_done, per_tile * j + w - 1)
                        ins = nc.vector.scalar_tensor_tensor(out=dst, in0=src, scalar=tap, in1=dst,
                                                             op0=ALU.mult, op1=ALU.add)
                    ins.then_inc(tap_done, 1)
                dve.wait_ge(tap_done, per_tile * j + DVE_TAPS)
                dst = acc[:, 2 * (j % 2), :]
                nc.vector.tensor_tensor(dst, dst, acc[:, 2 * (j % 2) + 1, :], ALU.add).then_inc(tap_done, 1)
                dve.wait_ge(tap_done, per_tile * (j + 1))
                dve.sem_inc(conv_done, 1)

            dve.wait_ge(ystat_done, KD)
            n = link(nc.vector.tensor_scalar(two(mean_b[:]), pair(4), 1.0 / D, None, ALU.mult))
            dve.wait_ge(dve_self, n)
            n = link(nc.vector.tensor_tensor(rstd_b[:], mean_b[:], mean_b[:], ALU.mult))
            dve.wait_ge(dve_self, n)
            n = link(nc.vector.scalar_tensor_tensor(out=two(var_b[:]), in0=pair(6), scalar=1.0 / D, in1=two(rstd_b[:]),
                                                    op0=ALU.mult, op1=ALU.subtract))
            dve.wait_ge(dve_self, n)
            n = link(nc.vector.tensor_scalar(var_b[:], var_b[:], 0.0, EPS, ALU.max, ALU.add))
            dve.wait_ge(dve_self, n)
            dve.sem_inc(var_done, 1)
            inverse(1, rstd_b)

            def centre(n):
                b, k = divmod(n, KD)
                return link(nc.vector.tensor_tensor(y[:, k, blk(b)], y[:, k, blk(b)], mean_b[:, blk(b)], ALU.subtract))

            def gate(n):
                b, k = divmod(n, KD)
                dve.wait_ge(ln_silu, n + 1)
                dve.wait_ge(gate_done, k + 1)
                nc.vector.tensor_tensor(y[:, k, blk(b)], y[:, k, blk(b)], zs[:, k, blk(b)], ALU.mult).then_inc(yz_full, 1)

            centred = centre(0)
            for n in range(2 * KD):
                b, k = divmod(n, KD)
                following = centre(n + 1) if n + 1 < 2 * KD else 0
                dve.wait_ge(dve_self, centred)
                nc.vector.tensor_tensor(y[:, k, blk(b)], y[:, k, blk(b)], rstd_b[:, blk(b)], ALU.mult).then_inc(ln_norm, 1)
                centred = following
                if n >= 1:
                    gate(n - 1)
            gate(2 * KD - 1)

            def residual(norm, b, gain, evacuated, count, done, order=0):
                def scale(m):
                    if evacuated is not None:
                        dve.wait_ge(evacuated, count)
                    return link(nc.vector.scalar_tensor_tensor(
                        out=zs[:, m, blk(b)], in0=zs[:, m, blk(b)], scalar=vecs[:, gain + m:gain + m + 1],
                        in1=rstd_b[:, blk(b)], op0=ALU.mult, op1=ALU.mult))
                scaled_at = scale(0)
                for m in range(KD):
                    following = scale(m + 1) if m + 1 < KD else 0
                    dve.wait_ge(dve_self, scaled_at)
                    nc.vector.tensor_tensor(xT[:, m, blk(b)], xT[:, m, blk(b)], zs[:, m, blk(b)], ALU.add).then_inc(done, 1)
                    scaled_at = following

            for b in range(NB):
                dve.wait_ge(ostat_done, KD * (b + 1))
                variance(2 + 2 * b, ps[:, 4 + b, 0:HB], D, b)
                inverse(2 + 2 * b, rstd_b, b)
                residual(2 + 2 * b, b, V_POST0, o_evac, KD * (b + 1), h_done)
                dve.wait_ge(hstat_done, KD * (b + 1))
                variance(3 + 2 * b, ps[:, 6 + b, 0:HB], D, b)
                inverse(3 + 2 * b, mean_b, b)
                dve.wait_ge(h_done, KD * (b + 1))
                for m in range(KD):
                    nc.vector.tensor_tensor(zs[:, m, blk(b)], xT[:, m, blk(b)], mean_b[:, blk(b)], ALU.mult).then_inc(xn_full, 1)

            def rotate_keys(b):
                dve.wait_ge(p_evac, TASKS3.index(("kv", 2, b)) + 1)
                if b == 0:
                    dve.wait_ge(tables_in, 48)
                dst = kr[2 * ROPE:3 * ROPE, blk(b)]
                tmp = var_b[2 * ROPE:3 * ROPE, blk(b)]
                nc.vector.tensor_tensor(dst, kr_ps[0:ROPE, :], cc[0:ROPE, blk(b)], ALU.mult)
                n = link(nc.vector.tensor_tensor(tmp, kr_ps[ROPE:2 * ROPE, :], kr[ROPE:2 * ROPE, blk(b)], ALU.mult))
                dve.wait_ge(dve_self, n)
                nc.vector.tensor_tensor(dst, dst, tmp, ALU.add).then_inc(kr_done, 1)

            rotate_keys(0)
            rotate_keys(1)
            dve.wait_ge(pstat_done, 8)
            dve.wait_ge(kr_done, 2)
            variance(6, pair(4), LORA)
            inverse(6, rstd_b)
            for k in range(KL):
                nc.vector.scalar_tensor_tensor(out=cf[:, k, 0:T], in0=cf[:, k, 0:T], scalar=vecs[:, V_KVA + k:V_KVA + k + 1],
                                               in1=rstd_b[:], op0=ALU.mult, op1=ALU.mult).then_inc(c_full, 1)
            dve.wait_ge(pstat_done, len(SQUARED))
            variance(7, pair(6), QL)
            inverse(7, rstd_b)
            for k in range(KQ):
                nc.vector.scalar_tensor_tensor(out=qa[:, k, :], in0=qa[:, k, :], scalar=vecs[:, V_QA + k:V_QA + k + 1],
                                               in1=rstd_b[:], op0=ALU.mult, op1=ALU.mult).then_inc(qn_full, 1)

            def gevac(g, i):
                kind, m, half, eng = GTASKS[i]
                if eng != "dve":
                    return
                bank = 4 + i % 4 if g == 0 else 7
                dve.wait_ge(g_done, NTASK * g + i + 1)
                if kind == "rope":
                    src = ps[:, bank, 0:HB]
                    if g >= 2 and half == 0:
                        dve.wait_ge(rope_moved, 128 * (g - 1))
                    if g or half:
                        dve.wait_ge(rope_done, 2 * g + half)
                    nc.vector.tensor_tensor(rope_a[:, 0, :], src, cc[:, blk(half)], ALU.mult)
                    nc.vector.tensor_tensor(rope_a[0:64, 1, :], src[64:128], ss[64:128, blk(half)], ALU.mult)
                    n = link(nc.vector.tensor_tensor(rope_a[64:128, 1, :], src[0:64], ss[0:64, blk(half)], ALU.mult))
                    last_read = n
                    dve.wait_ge(dve_self, n)
                    nc.vector.tensor_tensor(rope_r[:, g % 2, blk(half)], rope_a[:, 0, :], rope_a[:, 1, :],
                                            ALU.add).then_inc(rope_done, 1)
                    dve.wait_ge(rope_done, 2 * g + half + 1)
                    dve.sem_inc(g_evac_dve, 1)
                    return
                if kind == "k":
                    slot0 = GH * (g % 2) + 2 * m
                    for e in range(2):
                        last = nc.vector.tensor_copy(kT[0:NOPE, slot0 + e, 400 * half:400 * half + 400],
                                                     ps[64 * e:64 * e + 64, bank, 0:400])
                else:
                    n = min(P, KEYS - P * m)
                    last = nc.vector.tensor_copy(vt[0:n, KT * (g % 2) + m, :], ps[0:n, bank, 0:GH * VH])
                last.then_inc(g_evac_dve, 1)

            def maxima(i):
                s = i % NS
                dve.wait_ge(scores_done, i + 1)
                n, heads = (P * (s % 4 + 1), 2) if s < 8 else (SKEYS, 1)
                for e in range(heads):
                    at = link(nc.vector.reduce_max(rowmax[:, i % 2, e:e + 1], ps[:, 2 * (i % 2) + e, 0:n], axis=AX_X))
                if i >= 2:
                    dve.wait_ge(exp_done, i - 1)
                dve.wait_ge(dve_self, at)
                nc.vector.tensor_scalar(negmax[:, i % 2, 0:heads], rowmax[:, i % 2, 0:heads], -SCALE, None,
                                        ALU.mult).then_inc(max_done, 1)

            def pt_evac(i):
                s = i % NS
                dve.wait_ge(pt_done, i + 1)
                if s < 8:
                    n = P * (s % 4 + 1)
                    nc.vector.tensor_copy(pT[:, 1, 0:n], ps[:, 5, 0:n]).then_inc(pt_evac_dve, 1)
                else:
                    nc.vector.tensor_copy(pT[0:SKEYS - 2 * P, 1, 0:P], ps[0:SKEYS - 2 * P, 5, 0:P]).then_inc(pt_evac_dve, 1)

            def normalise(i):
                s = i % NS
                n, heads = (P * (s % 4 + 1), 2) if s < 8 else (SKEYS, 1)
                dve.wait_ge(exp_done, i + 1)
                at = link(nc.vector.reciprocal(rinv[:, i % 2, 0:heads], rowsum[:, i % 2, 0:heads]))
                dve.wait_ge(dve_self, at)
                for e in range(heads):
                    last = nc.vector.tensor_scalar(probs[:, i % 2, e, 0:n], probs[:, i % 2, e, 0:n],
                                                   rinv[:, i % 2, e:e + 1], None, ALU.mult)
                last.then_inc(prob_done, 1)

            def gated(i):
                g, s = divmod(i, NS)
                dve.wait_ge(pv_done, i + 1)
                if s < 8:
                    m, q = 2 * g + s // 4, P * (s % 4)
                    nc.vector.tensor_tensor(zs[:, m, q:q + P], ps[:, 6, 0:P], zs[:, m, q:q + P], ALU.mult).then_inc(att_done, 1)
                else:
                    dst = zs[:, 2 * g:2 * g + 2, SEQ:T]
                    nc.vector.tensor_tensor(dst, ps[:, 6, 0:2 * DEC].rearrange("p (m q) -> p m q", m=2), dst,
                                            ALU.mult).then_inc(att_done, 1)

            dve.wait_ge(c_stored, 16)
            for i in range(NTASK):
                gevac(0, i)
            dve.wait_ge(p_evac, len(TASKS3))
            for i in range(NITEM + 1):
                g, s = divmod(i, NS)
                if i < NITEM:
                    maxima(i)
                if i >= 1:
                    pt_evac(i - 1)
                if i < NITEM and g + 1 < NG:
                    for t in range(2 * s, min(2 * s + 2, NTASK)):
                        gevac(g + 1, t)
                if i < NITEM:
                    normalise(i)
                if i >= 1:
                    gated(i - 1)

            for n in range(2 * KD):
                b, k = divmod(n, KD)
                dve.wait_ge(oo_hi, n + 1)
                nc.vector.tensor_tensor(o_lo[:, k, blk(b)], zs[:, k, blk(b)], o_hi[:, k, blk(b)].bitcast(F32),
                                        ALU.subtract).then_inc(oo_lo, 1)
            for b in range(NB):
                dve.wait_ge(fstat_done, (12, 16)[b])
                variance(8 + b, ps[:, 4 + b, 0:HB], D, b)
                inverse(8 + b, rstd_b, b)
                residual(8 + b, b, V_POST1, f_evac, (12, 16)[b], y_done)

        @block.gpsimd
        def _(pool):
            nc.gpsimd.memset(v[:, :, 0:HIST], 0.0)
            for u in range(8):
                lo(pool, u)

            def merge(j):
                pool.wait_ge(conv_done, j + 1)
                a, b = acc[:, 2 * (j % 2), :], part[:, j % 2, :]
                pool.wait_ge(padd_done, 3 * (j + 1))
                nc.gpsimd.tensor_tensor(y[:, j, 0:SEQ], a[:, 0:SEQ], b[:, 0:SEQ], ALU.add)
                nc.gpsimd.tensor_tensor(y[:, j, SEQ:T], a[:, SEQ + HIST:CCOLS], b[:, SEQ + HIST:CCOLS],
                                        ALU.add).then_inc(y_ready, 1)

            pool.wait_ge(state_in, 16)
            pool.wait_ge(u_lo, KD)
            for j in range(KD):
                for u in range(8 * (j + 1), 8 * (j + 2)):
                    lo(pool, u)
                if j >= 2:
                    merge(j - 2)
                    pool.wait_ge(conv_out_done, 32 * (j - 1))
                nc.gpsimd.tensor_copy(v[:, j % 2, HIST + SEQ:2 * HIST + SEQ], state[:, j, :])
                pool.wait_ge(mt_evac, 3 * j + 2)
                nc.gpsimd.tensor_tensor(v[:, j % 2, HIST:HIST + SEQ], a_sb[:, 0:SEQ], sig[:, 0:SEQ], ALU.mult)
                nc.gpsimd.tensor_tensor(v[:, j % 2, 2 * HIST + SEQ:VCOLS], a_sb[:, SEQ:T], sig[:, SEQ:T],
                                        ALU.mult).then_inc(v_done, 1)
                for i in range(1, POOL_TAPS):
                    pool.wait_ge(prod_done, POOL_TAPS * j + i + 1)
                    p = part[:, j % 2, :]
                    if i >= 2:
                        pool.wait_ge(padd_done, 3 * j + i - 1)
                    nc.gpsimd.tensor_tensor(p, prod[:, i % 2, :], prod[:, 0, :] if i == 1 else p,
                                            ALU.add).then_inc(padd_done, 1)
            merge(KD - 2)
            for u in range(U_AO + KD, U_KV):
                lo(pool, u)
            merge(KD - 1)

            def rest(full, half, low, n, done, got):
                pool.wait_ge(got, n)
                nc.gpsimd.tensor_tensor(low, full, half.bitcast(F32), ALU.subtract).then_inc(done, 1)

            for n in range(2 * KD):
                b, k = divmod(n, KD)
                rest(y[:, k, blk(b)], act_hi[:, k, blk(b)], act_lo[:, k, blk(b)], n + 1, yz_lo, yz_hi)

            def xn_rest(n):
                b, m = divmod(n, KD)
                rest(zs[:, m, blk(b)], act_hi[:, m, blk(b)], act_lo[:, m, blk(b)], n + 1, xn_lo, xn_hi)

            for u in range(U_KV, U_KV + 4):
                lo(pool, u)
            for i in range(2):
                for n in range(4 * i, 4 * i + 4):
                    xn_rest(n)
                for u in range(U_KV + 4 + 2 * i, U_KV + 6 + 2 * i):
                    lo(pool, u)
            for u in range(U_Q, U_Z):
                lo(pool, u)
            for n in range(KD, 2 * KD):
                xn_rest(n)
            for k in range(KL):
                rest(cf[:, k, T:KEYS], c_hi[:, k, T:KEYS], c_lo[:, k, T:KEYS], k + 1, c_lo_done, c_hi_done)
            for u in range(U_Z, U_Z + KD):
                lo(pool, u)
            for k in range(KL):
                rest(cf[:, k, 0:T], c_hi[:, k, 0:T], c_lo[:, k, 0:T], KL + k + 1, c_lo_done, c_hi_done)
            for u in range(U_Z + KD, U_Z + KD + 3):
                lo(pool, u)
            for k in range(KQ):
                rest(qa[:, k, :], qn_hi[:, k, :], qn_lo[:, k, :], k + 1, qn_lo_done, qn_hi_done)
            for u in range(U_Z + KD + 3, U_G + GU):
                lo(pool, u)
            pool.wait_ge(p_done, len(TASKS3))
            nc.gpsimd.memset(ident[:], 0.0).then_inc(pool_set, 1)
            pool.wait_ge(pool_set, 1)
            nc.gpsimd.affine_select(out=ident[:], in_=ident[:], compare_op=ALU.not_equal, fill=1.0, base=0,
                                    pattern=[[-1, P]], channel_multiplier=1).then_inc(pool_set, 1)
            for u in range(U_G + GU, UNITS):
                lo(pool, u)

        @block.tensor
        def _(pe):
            def sums(banks, src, first, last):
                for b in range(NB):
                    ins = nc.tensor.matmul(ps[:, banks + b, 0:HB], ones[:], src[:, b, :], start=first, stop=last)
                return ins

            pe.wait_ge(const_set, 1)
            for k in range(KD):
                pe.wait_ge(xsq_done, k + 1)
                sums(4, sq[:, 2 * (k % 2):2 * (k % 2) + 2, :], k == 0, k == KD - 1).then_inc(xstat_done, 1)

            def ystats(j):
                pe.wait_ge(ysq_done, j + 1)
                sums(4, two(y[:, j, :]), j == 0, j == KD - 1)
                sums(6, sq[:, 2 * (j % 2):2 * (j % 2) + 2, :], j == 0, j == KD - 1).then_inc(ystat_done, 1)

            pe.wait_ge(var_done, 1)
            for j in range(KD):
                for i in range(3):
                    t = 3 * j + i
                    if t >= 2:
                        pe.wait_ge(mt_evac, t - 1)
                    for k in range(KD):
                        if i == 0:
                            ready(pe, 8 * j + k)
                            if j == 0:
                                pe.wait_ge(u_lo, k + 1)
                        w = cols(slot(8 * j + k), P * i)
                        for b in range(NB):
                            last = mm3(ps[:, 2 * (t % 2) + b, 0:HB], w, act_hi[:, k, blk(b)], act_lo[:, k, blk(b)],
                                       k == 0, k == KD - 1)
                    last.then_inc(mt_done, 1)
                if j >= 2:
                    ystats(j - 2)
            ystats(KD - 2)
            ystats(KD - 1)

            def product(bank, units, m, b, kts):
                for k in kts:
                    last = mm3(ps[:, bank, 0:HB], cols(slot(units + k), P * m), act_hi[:, k, blk(b)],
                               act_lo[:, k, blk(b)], k == 0, k == KD - 1)
                return last

            def one_sum(bank, src, first, last):
                return nc.tensor.matmul(ps[:, bank, 0:HB], ones[:], src, start=first, stop=last)

            def ostat(n):
                b, m = divmod(n, KD)
                pe.wait_ge(osq_done, n + 1)
                one_sum(4 + b, sq[:, n % 2, :], m == 0, m == KD - 1).then_inc(ostat_done, 1)

            def hstat(n):
                b, m = divmod(n, KD)
                pe.wait_ge(hsq_done, n + 1)
                one_sum(6 + b, sq[:, 2 + n % 2, :], m == 0, m == KD - 1).then_inc(hstat_done, 1)

            pe.wait_ge(mt_evac, 3 * KD)
            for k in range(KD):
                ready(pe, U_AO + k)
                pe.wait_ge(yz_lo, k + 1)
                for m in range(4):
                    last = product(m, U_AO, m, 0, [k])
                    if k == KD - 1:
                        last.then_inc(o_done, 1)
            for n in range(4, 2 * KD):
                b, m = divmod(n, KD)
                pe.wait_ge(o_evac, n - 3)
                if n == 4:
                    ready(pe, U_KV - 1)
                if n == KD:
                    pe.wait_ge(yz_lo, 2 * KD)
                product(n % 4, U_AO + 8 * (m // 4), m % 4, b, range(KD)).then_inc(o_done, 1)
                if n == 4:
                    ostat(0)
                    ostat(1)
                ostat(n - 2)
                if 11 <= n < 14:
                    for i in ((0, 1), (2, 3, 4), (5, 6, 7))[n - 11]:
                        hstat(i)

            def pstat(i):
                kind, m, b = TASKS3[SQUARED[i]]
                tiles = KL if kind == "kv" else KQ
                pe.wait_ge(psq_done, i + 1)
                one_sum((4 if kind == "kv" else 6) + b, sq[:, i % 2, :], m == 0, m == tiles - 1).then_inc(pstat_done, 1)

            for p, (kind, m, b) in enumerate(TASKS3):
                if p >= 4:
                    pe.wait_ge(p_evac, p - 3)
                else:
                    pe.wait_ge(o_evac, 13 + p)
                units, col = {"kv": (U_KV, m), "q": (U_Q, m), "z": (U_Z + 8 * (m // 4), m % 4)}[kind]
                ready(pe, units + KD - 1)
                if kind == "kv" and m == 0:
                    pe.wait_ge(xn_lo, KD * (b + 1))
                if kind == "kv" and m == KL:
                    for k in range(KD):
                        last = mm3(ps[0:2 * ROPE, p % 4, 0:HB], cols(slot(U_KV + k), LORA, 2 * ROPE),
                                   act_hi[:, k, blk(b)], act_lo[:, k, blk(b)], k == 0, k == KD - 1)
                    last.then_inc(p_done, 1)
                else:
                    product(p % 4, units, col, b, range(KD)).then_inc(p_done, 1)
                if p < 2:
                    ostat(14 + p)
                if p - 2 in SQUARED:
                    pstat(SQUARED.index(p - 2))
                if 3 <= p < 6:
                    for i in ((8, 9), (10, 11, 12), (13, 14, 15))[p - 3]:
                        hstat(i)

            def gtask(g, i):
                kind, m, half, _ = GTASKS[i]
                bank = 4 + i % 4 if g == 0 else 7
                prev = i - 4 if g == 0 else i - 1
                if prev >= 0:
                    eng = GTASKS[prev][3]
                    pe.wait_ge(g_evac_act if eng == "act" else g_evac_dve, evacs(eng, g, prev))
                elif g > 0:
                    pe.wait_ge(g_evac_act, evacs("act", g, -1))
                    pe.wait_ge(g_evac_dve, evacs("dve", g, -1))
                base = U_G + GU * g
                if i == 0:
                    ready(pe, base + KQ - 1)
                    if g == 0:
                        pe.wait_ge(qn_lo_done, KQ)
                if i == NQTASK:
                    ready(pe, base + GU - 1)
                    if g == 0:
                        pe.wait_ge(c_lo_done, 2 * KL)
                if kind in ("rope", "nope"):
                    for k in range(KQ):
                        last = mm3(ps[:, bank, 0:HB], cols(slot(base + k), P * m), qn_hi[:, k, blk(half)],
                                   qn_lo[:, k, blk(half)], k == 0, k == KQ - 1)
                elif kind == "k":
                    keys = slice(400 * half, 400 * half + 400)
                    for k in range(KL):
                        last = mm3(ps[:, bank, 0:400], cols(slot(base + KQ + k), P * m), c_hi[:, k, keys],
                                   c_lo[:, k, keys], k == 0, k == KL - 1)
                else:
                    n = min(P, KEYS - P * m)
                    keys = slice(P * m, P * m + n)
                    for k in range(KL):
                        wh, wl = cols(slot(base + KQ + k), GH * NOPE, GH * VH)
                        out = ps[0:n, bank, 0:GH * VH]
                        nc.tensor.matmul(out, c_hi[:, k, keys], wh, start=k == 0, stop=False)
                        nc.tensor.matmul(out, c_hi[:, k, keys], wl, start=False, stop=False)
                        last = nc.tensor.matmul(out, c_lo[:, k, keys], wh, start=False, stop=k == KL - 1)
                last.then_inc(g_done, 1)

            for i in range(NTASK):
                gtask(0, i)

            def scores(i):
                g, s = divmod(i, NS)
                if i >= 2:
                    pe.wait_ge(exp_done, i - 1)
                if i == 0:
                    pe.wait_ge(p_evac, len(TASKS3))
                    pe.wait_ge(krows_in, 16 * 2 * GH)
                if s == 0:
                    pe.wait_ge(g_evac_act, evacs("act", g, NTASK - 1))
                    pe.wait_ge(g_evac_dve, evacs("dve", g, NTASK - 1))
                    pe.wait_ge(rope_moved, 128 * (g + 1))
                if s < 8:
                    q, n = P * (s % 4), P * (s % 4 + 1)
                    for e in range(2):
                        h = GH * (g % 2) + 2 * (s // 4) + e
                        bank = 2 * (i % 2) + e
                        nc.tensor.matmul(ps[:, bank, 0:n], qT[0:NOPE + ROPE, h, q:q + P], kT[0:NOPE + ROPE, h, 0:n],
                                         start=True, stop=True)
                        last = nc.tensor.matmul(ps[:, bank, n - CHUNK:n], early[:], neg[:], start=False, stop=True,
                                                skip_group_check=True)
                else:
                    for e in range(GH):
                        h = GH * (g % 2) + e
                        last = nc.tensor.matmul(ps[DEC * e:DEC * e + DEC, 2 * (i % 2), 0:SKEYS],
                                                qT[0:NOPE + ROPE, h, SEQ:T], kT[0:NOPE + ROPE, h, SEQ:KEYS],
                                                start=True, stop=True)
                last.then_inc(scores_done, 1)

            def transposes(i):
                s = i % NS
                pe.wait_ge(prob_done, i + 1)
                if i >= 1:
                    pe.wait_ge(pt_evac_act, i)
                    pe.wait_ge(pt_evac_dve, i)
                if s < 8:
                    for e in range(2):
                        for t in range(s % 4 + 1):
                            last = nc.tensor.transpose(ps[:, 4 + e, P * t:P * t + P], probs[:, i % 2, e, P * t:P * t + P], ident[:])
                else:
                    for t in range(3):
                        n = min(P, SKEYS - P * t)
                        last = nc.tensor.transpose(ps[0:n, 4 + t // 2, P * (t % 2):P * (t % 2) + P],
                                                   probs[:, i % 2, 0, P * t:P * t + n], ident[:])
                last.then_inc(pt_done, 1)

            def values(i):
                g, s = divmod(i, NS)
                pe.wait_ge(pt_evac_act, i + 1)
                pe.wait_ge(pt_evac_dve, i + 1)
                if i >= 1:
                    pe.wait_ge(att_done, i)
                v0 = KT * (g % 2)
                if s < 8:
                    for t in range(s % 4 + 1):
                        for e in range(2):
                            col = VH * (2 * (s // 4) + e)
                            last = nc.tensor.matmul(ps[64 * e:64 * e + 64, 6, 0:P], vt[:, v0 + t, col:col + VH],
                                                    pT[:, e, P * t:P * t + P], start=t == 0, stop=t == s % 4)
                else:
                    for m in range(2):
                        for t in range(3):
                            n = min(P, SKEYS - P * t)
                            for e in range(2):
                                h = 2 * m + e
                                last = nc.tensor.matmul(ps[64 * e:64 * e + 64, 6, DEC * m:DEC * m + DEC],
                                                        vt[0:n, v0 + 4 + t, VH * h:VH * h + VH],
                                                        pT[0:n, t // 2, P * (t % 2) + DEC * h:P * (t % 2) + DEC * h + DEC],
                                                        start=t == 0, stop=t == 2)
                last.then_inc(pv_done, 1)

            pe.wait_ge(pool_set, 2)
            for i in range(NITEM + 1):
                g, s = divmod(i, NS)
                if i < NITEM:
                    scores(i)
                if i >= 1:
                    transposes(i - 1)
                if i < NITEM and g + 1 < NG:
                    for t in range(2 * s, min(2 * s + 2, NTASK)):
                        gtask(g + 1, t)
                if i >= 1:
                    values(i - 1)

            def fstat(n):
                m, b = FTASKS[n]
                pe.wait_ge(fsq_done, n + 1)
                one_sum(4 + b, sq[:, n % 2, :], m == 0, m == KD - 1).then_inc(fstat_done, 1)

            def fproduct(n, kts):
                m, b = FTASKS[n]
                for k in kts:
                    last = mm3(ps[:, n % 4, 0:HB], cols(slot(U_BO + 8 * (m // 4) + k), P * (m % 4)), o_hi[:, k, blk(b)],
                               o_lo[:, k, blk(b)], k == 0, k == KD - 1)
                return last

            ready(pe, U_BO + KD - 1)
            for k in range(KD):
                pe.wait_ge(oo_lo, k + 1)
                for n in range(4):
                    last = fproduct(n, [k])
                    if k == KD - 1:
                        last.then_inc(f_done, 1)
            for n in range(4, 2 * KD):
                pe.wait_ge(f_evac, n - 3)
                if n == 4:
                    pe.wait_ge(oo_lo, 2 * KD)
                if n == 8:
                    ready(pe, UNITS - 1)
                fproduct(n, range(KD)).then_inc(f_done, 1)
                if n == 4:
                    fstat(0)
                    fstat(1)
                fstat(n - 2)
            fstat(14)
            fstat(15)


def kernel(x_prompt, x_sample, state_conv, cache_kv_latent, cache_k_rope,
           g_pre, g_post, w_a_in, w_a_dw, b_a_dw, g_a_ln, b_a_ln, w_a_out,
           g_kv_in, w_kv_a, g_kv_a, w_kv_b, w_b_in, g_q_a, w_q_b, w_b_out):
    import numpy as np
    import concourse.bacc as bacc
    from concourse import mybir as mb
    from concourse.bass_utils import run_bass_kernel_spmd

    f = lambda a: np.asarray(a)

    def tiles(a):
        return f(a).reshape(-1, P, a.shape[-1])

    def columns(a):
        return f(a).reshape(-1, P).T

    def rows(a):
        return f(a).T.reshape(-1, P, a.shape[0]).transpose(1, 0, 2)

    x = np.concatenate([f(x_prompt)[0], f(x_sample)[0]], axis=0)
    win = tiles(w_a_in[0]).reshape(KD, P, 3, KD, P)
    win = win[:, :, [1, 0, 2]].transpose(3, 0, 1, 2, 4).reshape(KD * KD, P, 3 * P)

    def chunks(a, n=512):
        t = tiles(a)
        return t.reshape(t.shape[0], P, -1, n).transpose(2, 0, 1, 3).reshape(-1, P, n)

    wkv = tiles(w_kv_a)
    half = ROPE // 2
    wkv = np.concatenate([wkv, wkv[..., LORA + half:], wkv[..., LORA:LORA + half]], axis=-1)
    wqb = tiles(w_q_b[0]).reshape(KQ, P, NG, GH, NOPE + ROPE)
    nope = wqb[..., :NOPE].reshape(KQ, P, NG, GH * NOPE)
    rope = wqb[..., NOPE:].reshape(KQ, P, NG, GH, 2, half).transpose(0, 1, 2, 4, 3, 5).reshape(KQ, P, NG, GH * ROPE)
    wqb = np.concatenate([nope, rope], axis=-1).transpose(2, 0, 1, 3).reshape(NG * KQ, P, 3 * P)
    wkb = tiles(w_kv_b).reshape(KL, P, NG, GH, 2, NOPE).transpose(2, 0, 1, 4, 3, 5).reshape(NG * KL, P, 2 * GH * NOPE)

    vec = np.concatenate(
        [columns(g_pre[0]), columns(g_pre[1]), columns(g_post[0]), columns(g_post[1]),
         f(w_a_dw)[0].T.reshape(KD, P, WIDTH).transpose(1, 0, 2).reshape(P, KD * WIDTH),
         columns(b_a_dw[0]), columns(g_a_ln[0]), columns(b_a_ln[0]), columns(g_kv_in), columns(g_kv_a),
         columns(g_q_a[0])], axis=1)

    pos = np.concatenate([np.arange(SEQ), PAST + np.arange(DEC)]).astype(np.float32)
    inv = (np.float32(10000.0) ** (-np.arange(half, dtype=np.float32) / np.float32(half))).astype(np.float32)
    ang = inv[:, None] * pos[None, :]
    cos, sin = np.cos(ang).astype(np.float32), np.sin(ang).astype(np.float32)
    cc = np.tile(cos, (8, 1))
    ss = np.concatenate([np.tile(sin, (4, 1)), -np.tile(sin, (4, 1))], axis=0)
    krs = np.concatenate([-sin, sin], axis=0)

    arrays = {
        "x_t": rows(x), "state_t": rows(f(state_conv)[0, 0]), "ckv_t": rows(f(cache_kv_latent)[0]),
        "ckr_t": f(cache_k_rope)[0].T, "w_in": win, "w_ao": chunks(w_a_out[0]), "w_kv": wkv,
        "w_bi": chunks(w_b_in[0]), "w_qb": wqb, "w_kb": wkb, "w_bo": chunks(w_b_out[0]),
        "vecs_d": vec, "cc_d": cc, "ss_d": ss, "krs_d": krs,
    }
    arrays = {k: np.ascontiguousarray(a) for k, a in arrays.items()}
    outs = {"y_out": (P, KD, T), "conv_out": (P, KD, 2 * HIST), "c_out": (P, KL, T), "kr_out": (ROPE, T)}

    nc = bacc.Bacc("TRN2", target_bir_lowering=False, num_devices=1)
    args = [nc.dram_tensor(k, a.shape, mb.dt.from_np(a.dtype), kind="ExternalInput").ap() for k, a in arrays.items()]
    args += [nc.dram_tensor(k, s, mb.dt.float32, kind="ExternalOutput").ap() for k, s in outs.items()]
    build(nc, *args)
    r = run_bass_kernel_spmd(nc, [arrays], core_ids=[0]).results[0]

    def tokens(a):
        a = np.asarray(a)
        return np.ascontiguousarray(a.transpose(2, 1, 0).reshape(a.shape[2], -1))

    yt, ct, cv, krt = tokens(r["y_out"]), tokens(r["c_out"]), tokens(r["conv_out"]), np.asarray(r["kr_out"]).T
    return (yt[None, :SEQ], yt[None, SEQ:], cv[None, None, :HIST], ct[None, :SEQ], np.ascontiguousarray(krt[None, :SEQ]),
            cv[None, None, HIST:], ct[None, SEQ:], np.ascontiguousarray(krt[None, SEQ:]))
```

```python
from contextlib import ExitStack

import concourse.bass as bass
from concourse import mybir

F32 = mybir.dt.float32
F32R = mybir.dt.float32r
BF16 = mybir.dt.bfloat16
ALU = mybir.AluOpType
ACT = mybir.ActivationFunctionType
AX_X = mybir.AxisListType.X

P = 128
D = 1024
KD = D // P
SEQ, DEC, PAST = 512, 32, 256
T = SEQ + DEC
HB = T // 2
NB = 2
LORA = 256
KL = LORA // P
QL = 512
KQ = QL // P
HEADS, NOPE, ROPE, VH = 16, 64, 32, 64
GH = 4
NG = HEADS // GH
KEYS = T + PAST
SKEYS = KEYS - SEQ
WIDTH = 31
HIST = WIDTH - 1
VCOLS = HIST + SEQ + HIST + DEC
CCOLS = VCOLS - HIST
CHUNK = 64
EPS = 1e-6
SCALE = 1.0 / float(NOPE + ROPE) ** 0.5
NEG = -1e30

STAGES = 5
RING = 16
POOL_TAPS = 7
DVE_TAPS = WIDTH - POOL_TAPS
PADDS = POOL_TAPS - 1
PRODS = 4

U_IN = 0
U_AO = U_IN + 8 * KD
U_KV = U_AO + 2 * KD
U_Q = U_KV + KD
U_Z = U_Q + KD
U_G = U_Z + 2 * KD
GU = KQ + KL
U_BO = U_G + NG * GU
UNITS = U_BO + 2 * KD

TASKS3 = ([("kv", m, 0) for m in range(3)] + [("q", m, 0) for m in range(KQ)]
          + [("kv", m, 1) for m in range(3)] + [("q", m, 1) for m in range(KQ)]
          + [("z", m, b) for m in range(KD) for b in range(2)])
ZTASK = TASKS3.index(("z", 0, 0))
N_IN, N_LN, N_O, N_H, N_KV, N_Q, N_F = 0, 1, (3, 5), (4, 6), 7, 8, 9
GTASKS = ([("rope", 2, b, "dve") for b in range(2)] + [("nope", m, b, "act") for m in range(2) for b in range(2)]
          + [("k", m, h, ("act", "dve")[h]) for m in range(2) for h in range(2)]
          + [("v", t, 0, ("dve", "act")[t % 2]) for t in range(7)])
NQTASK, NTASK = 6, len(GTASKS)
KT = 7
NS = 9
NITEM = NG * NS
FTASKS = [(m, b) for c in range(2) for b in range(2) for m in range(4 * c, 4 * c + 4)]


def evacs(eng, g, i):
    each = sum(t[3] == eng for t in GTASKS)
    return g * each + sum(t[3] == eng for t in GTASKS[:i + 1])


V_PRE0, V_PRE1, V_POST0, V_POST1 = 0, 8, 16, 24
V_DW = 32
V_BDW = V_DW + 8 * WIDTH
V_GLN, V_BLN, V_KVIN = V_BDW + 8, V_BDW + 16, V_BDW + 24
V_KVA = V_KVIN + 8
V_QA = V_KVA + 2
NVEC = V_QA + 4


def unit_cols(u):
    if u < U_AO:
        return 384
    if U_KV <= u < U_Q:
        return 320
    if U_G <= u < U_BO and (u - U_G) % GU < KQ:
        return 384
    return 512


def unit_gain(u):
    if U_KV <= u < U_Q:
        return V_KVIN + (u - U_KV)
    if U_Q <= u < U_G:
        return V_PRE1 + (u - U_Q) % KD
    return None


def build(nc, x_t, state_t, ckv_t, ckr_t, w_in, w_ao, w_kv, w_bi, w_qb, w_kb, w_bo, vecs_d, cc_d, ss_d, krs_d,
          y_out, conv_out, c_out, kr_out):
    ctx = ExitStack()
    with ctx:
        def sem(name):
            return ctx.enter_context(nc.semaphore(name))


        def keep(name, shape, dt=F32, side="left"):
            return ctx.enter_context(nc.sbuf_tensor(name, shape, dt, side=side))

        def region(side, *specs):
            st = ExitStack()
            return st, [st.enter_context(nc.sbuf_tensor(n, s, d, side=side)) for n, s, d in specs]

        xT = keep("xT", [P, KD, T])
        zs = keep("zs", [P, KD, T])
        rlow_hi = keep("rlow_hi", [P, 8, 512], F32R)
        rlow_lo = keep("rlow_lo", [P, 8, 512], F32R)
        stage = keep("stage", [P, STAGES, 512])
        cc = keep("cc", [P, T])
        ss = keep("ss", [P, T])
        kr = keep("kr", [P, KEYS])
        vecs = keep("vecs", [P, NVEC])
        ones = keep("ones", [P, P])
        warm = keep("warm", [1, 1])
        mean_b = keep("mean_b", [P, T])
        rstd_b = keep("rstd_b", [P, T])
        var_b = keep("var_b", [P, T])
        early = keep("early", [1, P], BF16)
        neg = keep("neg", [1, CHUNK], BF16)
        negmax = keep("negmax", [P, 2, 2])
        rowmax = keep("rowmax", [P, 2, 2])
        rowsum = keep("rowsum", [P, 2, 2])
        rinv = keep("rinv", [P, 2, 2])
        sq = keep("sq", [P, 4, HB], F32, "right")

        left, (act_hi, act_lo, rtop_hi, rtop_lo) = region(
            "left", ("act_hi", [P, KD, T], F32R), ("act_lo", [P, KD, T], F32R),
            ("rtop_hi", [P, 8, 512], F32R), ("rtop_lo", [P, 8, 512], F32R))
        right, (y, v, sig, a_sb, prod, part, acc, state) = region(
            "right", ("y", [P, KD, T], F32), ("v", [P, 2, VCOLS], F32), ("sig", [P, T], F32),
            ("a_sb", [P, T], F32), ("prod", [P, PRODS, CCOLS], F32), ("part", [P, 2, CCOLS], F32),
            ("acc", [P, 2, CCOLS], F32), ("state", [P, KD, HIST], F32))
        right.close()
        qn_hi = keep("qn_hi", [P, KQ, T], F32R, "right")
        qn_lo = keep("qn_lo", [P, KQ, T], F32R, "right")
        c_hi = keep("c_hi", [P, KL, KEYS], F32R, "right")
        c_lo = keep("c_lo", [P, KL, KEYS], F32R, "right")
        right, (qa, cf, kr_ps) = region("right", ("qa", [P, KQ, T], F32), ("cf", [P, KL, KEYS], F32),
                                        ("kr_ps", [2 * ROPE, HB], F32))
        right.close()
        left.close()
        left, (kT, probs, qT, vt, ident) = region(
            "left", ("kT", [P, 2 * GH, KEYS], F32), ("probs", [P, 2, 2, 512], F32),
            ("qT", [P, 2 * GH, T], F32), ("vt", [P, 2 * KT, GH * VH], F32),
            ("ident", [P, P], F32))
        right, (pT, rope_a, rope_r) = region(
            "right", ("pT", [P, 2, 512], F32), ("rope_a", [P, 2, HB], F32), ("rope_r", [P, 2, T], F32))
        right.close()
        left.close()
        right, (fsq,) = region("right", ("fsq", [P, NB, 6, HB], F32))
        right.close()
        left, (o_hi, o_lo, btop_hi, btop_lo) = region(
            "left", ("o_hi", [P, KD, T], F32R), ("o_lo", [P, KD, T], F32R),
            ("btop_hi", [P, 8, 512], F32R), ("btop_lo", [P, 8, 512], F32R))
        left.close()

        ps = ctx.enter_context(nc.psum_tensor("ps", [P, 8, 512], F32))

        x_in = [sem(f"x_in{i}") for i in range(4)]
        vecs_in, tables_in, state_in = sem("vecs_in"), sem("tables_in"), sem("state_in")
        cache_in, c_stored = sem("cache_in"), sem("c_stored")
        stage_in = [sem(f"stage_in{i}") for i in range(STAGES)]
        conv_out_done, rope_moved, krows_in, outs_done = (
            sem("conv_out_done"), sem("rope_moved"), sem("krows_in"), sem("outs_done"))
        scaled, hi_done = sem("scaled"), sem("hi_done")
        xsq_done, uhi_done = sem("xsq_done"), sem("uhi_done")
        sqrt_done = sem("sqrt_done")
        mt_evac, sig_done, prod_done, ysq_done, gate_done = (
            sem("mt_evac"), sem("sig_done"), sem("prod_done"), sem("ysq_done"), sem("gate_done"))
        ln_silu, yz_hi = sem("ln_silu"), sem("yz_hi")
        o_evac, osq_done, hsq_done, xn_hi = sem("o_evac"), sem("osq_done"), sem("hsq_done"), sem("xn_hi")
        p_evac, psq_done, c_hi_done, qn_hi_done = sem("p_evac"), sem("psq_done"), sem("c_hi_done"), sem("qn_hi_done")
        g_evac_act, exp_done, pt_evac_act = sem("g_evac_act"), sem("exp_done"), sem("pt_evac_act")
        oo_hi, f_evac, fsq_done = sem("oo_hi"), sem("f_evac"), sem("fsq_done")
        const_set, dve_self, var_done, rstd_done = sem("const_set"), sem("dve_self"), sem("var_done"), sem("rstd_done")
        u_full, u_lo = sem("u_full"), sem("u_lo")
        tap_done, y_ready = sem("tap_done"), sem("y_ready")
        ln_norm, yz_full = sem("ln_norm"), sem("yz_full")
        h_done, xn_full = sem("h_done"), sem("xn_full")
        osum_done, hsum_done, qsum_done, fsum_done = sem("osum_done"), sem("hsum_done"), sem("qsum_done"), sem("fsum_done")
        kr_done, c_full, qn_full = sem("kr_done"), sem("c_full"), sem("qn_full")
        g_evac_dve, rope_done, max_done, prob_done, pt_evac_dve, att_done = (
            sem("g_evac_dve"), sem("rope_done"), sem("max_done"), sem("prob_done"), sem("pt_evac_dve"), sem("att_done"))
        oo_lo, y_done = sem("oo_lo"), sem("y_done")
        pool_set, lo_done, v_done, padd_done = sem("pool_set"), sem("lo_done"), sem("v_done"), sem("padd_done")
        yz_lo, xn_lo, c_lo_done, qn_lo_done = sem("yz_lo"), sem("xn_lo"), sem("c_lo_done"), sem("qn_lo_done")
        xstat_done, mt_done, ystat_done, o_done, ostat_done, hstat_done = (
            sem("xstat_done"), sem("mt_done"), sem("ystat_done"), sem("o_done"), sem("ostat_done"), sem("hstat_done"))
        p_done, pstat_done, g_done = sem("p_done"), sem("pstat_done"), sem("g_done")
        scores_done, pt_done, pv_done, f_done, fstat_done = (
            sem("scores_done"), sem("pt_done"), sem("pv_done"), sem("f_done"), sem("fstat_done"))

        def blk(b):
            return slice(b * HB, (b + 1) * HB)

        def pair(b0):
            return ps[:, b0:b0 + 2, 0:HB]

        def two(ap):
            return ap.rearrange("p (b t) -> p b t", b=NB)

        def slot(u):
            n = unit_cols(u)
            if u >= U_G:
                m = u - U_G
                if m < NG * GU + KD:
                    return rlow_hi[:, m % 8, 0:n], rlow_lo[:, m % 8, 0:n]
                return btop_hi[:, m % 8, 0:n], btop_lo[:, m % 8, 0:n]
            s = u % RING
            if s < 8:
                return rlow_hi[:, s, 0:n], rlow_lo[:, s, 0:n]
            return rtop_hi[:, s - 8, 0:n], rtop_lo[:, s - 8, 0:n]

        def wait_slot(act, u):
            if u < RING:
                return
            if u < U_KV:
                act.wait_ge(mt_done, 3 * (u // 8 - 1))
            elif u < U_Q:
                act.wait_ge(o_done, 12)
            elif u < U_Z:
                act.wait_ge(o_done, 16)
            elif u < U_Z + KD:
                act.wait_ge(p_done, TASKS3.index(("kv", 2, 1)) + 1)
            elif u < U_G:
                act.wait_ge(p_done, TASKS3.index(("q", 3, 1)) + 1)
            elif u < U_G + 8:
                act.wait_ge(p_done, TASKS3.index(("z", 3, 1)) + 1)
            elif u < U_BO + KD:
                g, i = divmod(u - U_G - 8, GU)
                act.wait_ge(g_done, NTASK * g + (NQTASK if i < KQ else NTASK))
            else:
                act.wait_ge(pv_done, NITEM)

        def unit_src(u):
            n = unit_cols(u)
            for first, src in ((U_BO, w_bo), (U_Q, None), (U_KV, w_kv), (U_AO, w_ao), (U_IN, w_in)):
                if u >= first:
                    break
            if src is not None:
                return src[u - first]
            if u < U_G:
                return w_bi[u - U_Q]
            g, i = divmod(u - U_G, GU)
            return w_qb[g * KQ + i] if i < KQ else w_kb[g * KL + i - KQ]

        def hi(act, u):
            raw = stage[:, u % STAGES, 0:unit_cols(u)]
            act.wait_ge(stage_in[u % STAGES], 16 * (u // STAGES + 1))
            gain = unit_gain(u)
            if gain is not None:
                nc.scalar.activation(raw, raw, ACT.Copy, scale=vecs[:, gain:gain + 1]).then_inc(scaled, 1)
            wait_slot(act, u)
            if gain is not None:
                act.wait_ge(scaled, u - U_KV + 1)
            nc.scalar.activation(slot(u)[0], raw, ACT.Copy).then_inc(hi_done, 1)

        def lo(pool, u):
            pool.wait_ge(hi_done, u + 1)
            h, l = slot(u)
            nc.gpsimd.tensor_tensor(l, stage[:, u % STAGES, 0:unit_cols(u)], h.bitcast(F32),
                                    ALU.subtract).then_inc(lo_done, 1)

        def ready(pe, u):
            pe.wait_ge(lo_done, u + 1)

        def mm3(out, w, xh, xl, start, stop):
            wh, wl = w
            nc.tensor.matmul(out, wh, xh, start=start, stop=False)
            nc.tensor.matmul(out, wh, xl, start=False, stop=False)
            return nc.tensor.matmul(out, wl, xh, start=False, stop=stop)

        def cols(w, c, n=P):
            return w[0][:, c:c + n], w[1][:, c:c + n]

        block = ctx.enter_context(nc.Block())

        @block.sync
        def _(sp):
            def load(u):
                if u >= STAGES:
                    sp.wait_ge(lo_done, u - STAGES + 1)
                sp.dma_start(stage[:, u % STAGES, 0:unit_cols(u)], unit_src(u)).then_inc(stage_in[u % STAGES], 16)

            sp.dma_start(vecs[:], vecs_d).then_inc(vecs_in, 16)
            for i in range(4):
                sp.dma_start(xT[:, 2 * i:2 * i + 2, :], x_t[:, 2 * i:2 * i + 2, :]).then_inc(x_in[i], 16)
            for u in range(8):
                load(u)
                if u == 2:
                    sp.dma_start(state[:], state_t).then_inc(state_in, 16)
            for j in range(KD):
                for u in range(8 * (j + 1), 8 * (j + 2)):
                    load(u)
                sp.wait_ge(v_done, j + 1)
                sp.dma_start(conv_out[:, j, 0:HIST], v[:, j % 2, SEQ:SEQ + HIST]).then_inc(conv_out_done, 16)
                sp.dma_start(conv_out[:, j, HIST:2 * HIST], v[:, j % 2, VCOLS - HIST:VCOLS]).then_inc(conv_out_done, 16)
            for u in range(U_AO + KD, U_KV):
                load(u)
            sp.dma_start(cc[:], cc_d).then_inc(tables_in, 16)
            sp.dma_start(ss[:], ss_d).then_inc(tables_in, 16)
            sp.dma_start(kr[ROPE:2 * ROPE, 0:T], krs_d).then_inc(tables_in, 16)
            sp.dma_start(kr[2 * ROPE:3 * ROPE, T:KEYS], ckr_t).then_inc(cache_in, 16)
            for u in range(U_KV, U_KV + 4):
                load(u)
            sp.wait_ge(yz_lo, 2 * KD)
            sp.dma_start(cf[:, :, T:KEYS], ckv_t).then_inc(cache_in, 16)
            for u in range(U_KV + 4, U_G + GU):
                load(u)
            sp.wait_ge(c_full, KL)
            sp.dma_start(c_out, cf[:, :, 0:T]).then_inc(c_stored, 16)
            sp.wait_ge(kr_done, 2)
            sp.dma_start(kr_out, kr[2 * ROPE:3 * ROPE, 0:T]).then_inc(outs_done, 16)
            for u in range(U_G + GU, U_G + 2 * GU):
                load(u)
            sp.wait_ge(p_done, len(TASKS3))
            for h in range(2 * GH):
                sp.dma_start(kT[2 * ROPE:3 * ROPE, h, :], kr[2 * ROPE:3 * ROPE, :]).then_inc(krows_in, 16)
            for g in range(NG):
                sp.wait_ge(rope_done, 2 * (g + 1))
                for i in range(GH):
                    h = GH * (g % 2) + i
                    for half in range(2):
                        sp.dma_start(qT[NOPE + 16 * half:NOPE + 16 * half + 16, h, :],
                                     rope_r[64 * half + 16 * i:64 * half + 16 * i + 16, g % 2, :]).then_inc(rope_moved, 16)
                first = U_G + GU * (g + 2)
                for u in range(first, first + GU if g + 1 < NG else UNITS):
                    load(u)
            for n in range(2 * KD):
                b, m = divmod(n, KD)
                sp.wait_ge(y_done, n + 1)
                sp.dma_start(y_out[:, m, blk(b)], xT[:, m, blk(b)]).then_inc(outs_done, 16)
            sp.wait_ge(outs_done, 16 * (1 + 2 * KD))
            sp.wait_ge(c_stored, 16)
            sp.wait_ge(conv_out_done, 32 * KD)

        @block.scalar
        def _(act):
            act.wait_ge(vecs_in, 16)
            for k in range(KD):
                if k % 2 == 0:
                    act.wait_ge(x_in[k // 2], 16)
                if k >= 2:
                    act.wait_ge(xstat_done, k - 1)
                nc.scalar.activation(sq[:, 2 * (k % 2):2 * (k % 2) + 2, :], two(xT[:, k, :]), ACT.Square).then_inc(xsq_done, 1)
            for u in range(0, 4):
                hi(act, u)

            def sqrt_of(n, b=None):
                s = slice(0, T) if b is None else blk(b)
                act.wait_ge(var_done, n + 1)
                nc.scalar.activation(var_b[:, s], var_b[:, s], ACT.Sqrt).then_inc(sqrt_done, 1)

            sqrt_of(N_IN)
            for k in range(KD):
                act.wait_ge(u_full, k + 1)
                nc.scalar.activation(act_hi[:, k, :], y[:, k, :], ACT.Copy).then_inc(uhi_done, 1)
                if k % 2:
                    hi(act, 4 + k // 2)

            def load_table(func):
                nc.scalar.activation(warm[:], ones[0:1, 0:1], func)

            def ysquare(j):
                act.wait_ge(y_ready, j + 1)
                if j >= 2:
                    act.wait_ge(ystat_done, j - 1)
                elif j == 0:
                    act.wait_ge(xstat_done, KD)
                nc.scalar.activation(sq[:, 2 * (j % 2):2 * (j % 2) + 2, :], two(y[:, j, :]), ACT.Square).then_inc(ysq_done, 1)

            def tap_product(j, i):
                w, after = DVE_TAPS + i, i + PRODS
                act.wait_ge(v_done, j + 1)
                if i >= PRODS:
                    act.wait_ge(padd_done, PADDS * j + max(1, i - PRODS))
                elif j:
                    act.wait_ge(padd_done, PADDS * (j - 1) + (after if after < POOL_TAPS else max(1, i)))
                nc.scalar.activation(prod[:, i % PRODS, :], v[:, j % 2, w:w + CCOLS], ACT.Copy,
                                     scale=vecs[:, V_DW + WIDTH * j + w:V_DW + WIDTH * j + w + 1]).then_inc(prod_done, 1)

            for j in range(KD):
                nxt = 8 * (j + 1)
                act.wait_ge(mt_done, 3 * j + 1)
                if j >= 1:
                    act.wait_ge(v_done, j)
                nc.scalar.activation(two(sig[:]), pair(2 * ((3 * j) % 2)), ACT.Sigmoid).then_inc(mt_evac, 1)
                for u in range(4):
                    hi(act, nxt + u)
                if j >= 2:
                    ysquare(j - 2)
                act.wait_ge(mt_done, 3 * j + 2)
                nc.scalar.activation(two(a_sb[:]), pair(2 * ((3 * j + 1) % 2)), ACT.Copy).then_inc(mt_evac, 1)
                for i in range(POOL_TAPS):
                    if i < 4:
                        hi(act, nxt + 4 + i)
                    tap_product(j, i)
                    if i == 3:
                        act.wait_ge(mt_done, 3 * j + 3)
                        nc.scalar.activation(two(zs[:, j, :]), pair(2 * ((3 * j + 2) % 2)), ACT.Copy).then_inc(mt_evac, 1)
            ysquare(KD - 2)
            act.wait_ge(mt_evac, 3 * KD)
            for j in range(KD):
                nc.scalar.activation(zs[:, j, :], zs[:, j, :], ACT.Silu).then_inc(gate_done, 1)
                hi(act, U_AO + KD + j)
            load_table(ACT.Sqrt)
            ysquare(KD - 1)

            def split_yz(n):
                b, k = divmod(n, KD)
                act.wait_ge(yz_full, n + 1)
                nc.scalar.activation(act_hi[:, k, blk(b)], y[:, k, blk(b)], ACT.Copy).then_inc(yz_hi, 1)

            for b in range(NB):
                sqrt_of(N_LN + b, b)
            load_table(ACT.Silu)
            for n in range(2 * KD):
                b, k = divmod(n, KD)
                act.wait_ge(ln_norm, n + 1)
                nc.scalar.activation(y[:, k, blk(b)], y[:, k, blk(b)], ACT.Silu, bias=vecs[:, V_BLN + k:V_BLN + k + 1],
                                     scale=vecs[:, V_GLN + k:V_GLN + k + 1]).then_inc(ln_silu, 1)
                if n >= 1:
                    split_yz(n - 1)
            split_yz(2 * KD - 1)

            def evac_o(n):
                b, m = divmod(n, KD)
                act.wait_ge(o_done, n + 1)
                nc.scalar.activation(y[:, m, blk(b)], ps[:, n % 4, 0:HB], ACT.Square).then_inc(osq_done, 1)
                nc.scalar.activation(zs[:, m, blk(b)], ps[:, n % 4, 0:HB], ACT.Copy).then_inc(o_evac, 1)

            def hsquare(n):
                b, m = divmod(n, KD)
                act.wait_ge(h_done, n + 1)
                nc.scalar.activation(y[:, m, blk(b)], xT[:, m, blk(b)], ACT.Square).then_inc(hsq_done, 1)

            def xn_split(n):
                b, m = divmod(n, KD)
                act.wait_ge(xn_full, n + 1)
                nc.scalar.activation(act_hi[:, m, blk(b)], zs[:, m, blk(b)], ACT.Copy).then_inc(xn_hi, 1)

            def evac_p(p):
                kind, m, b = TASKS3[p]
                src = ps[:, p % 4, 0:HB]
                act.wait_ge(p_done, p + 1)
                if kind == "z":
                    nc.scalar.activation(zs[:, m, blk(b)], src, ACT.Silu).then_inc(p_evac, 1)
                elif kind == "q":
                    nc.scalar.activation(y[:, KL + m, blk(b)], src, ACT.Square).then_inc(psq_done, 1)
                    nc.scalar.activation(qa[:, m, blk(b)], src, ACT.Copy).then_inc(p_evac, 1)
                elif m < KL:
                    nc.scalar.activation(y[:, m, blk(b)], src, ACT.Square).then_inc(psq_done, 1)
                    nc.scalar.activation(cf[:, m, blk(b)], src, ACT.Copy).then_inc(p_evac, 1)
                else:
                    if b:
                        act.wait_ge(kr_done, 1)
                    nc.scalar.activation(kr_ps[:], ps[0:2 * ROPE, p % 4, 0:HB], ACT.Copy).then_inc(p_evac, 1)

            for n in range(9):
                evac_o(n)
            sqrt_of(N_O[0], 0)
            for n, tiles in ((9, (0, 1, 2)), (10, (3, 4, 5)), (11, (6, 7))):
                evac_o(n)
                for i in tiles:
                    hsquare(i)
            for u in range(U_KV, U_KV + 3):
                hi(act, u)
            evac_o(12)
            sqrt_of(N_H[0], 0)
            hi(act, U_KV + 3)
            evac_o(13)
            for i in range(4):
                xn_split(i)
            hi(act, U_KV + 4)
            evac_o(14)
            for i in range(4, KD):
                xn_split(i)
            for u in range(U_KV + 5, U_Q):
                hi(act, u)
            evac_o(15)
            for u in range(U_Q, U_Q + 3):
                hi(act, u)
            evac_p(0)
            sqrt_of(N_O[1], 1)
            for u in range(U_Q + 3, U_Q + 5):
                hi(act, u)
            evac_p(1)
            hi(act, U_Q + 5)
            for i in range(KD, KD + 2):
                hsquare(i)
            hi(act, U_Q + 6)
            evac_p(2)
            for i in range(KD + 2, KD + 5):
                hsquare(i)
            hi(act, U_Q + 7)
            evac_p(3)
            for i in range(KD + 5, 2 * KD):
                hsquare(i)
            evac_p(4)
            sqrt_of(N_H[1], 1)
            evac_p(5)
            for i in range(KD, 2 * KD):
                xn_split(i)
            evac_p(6)
            act.wait_ge(cache_in, 32)
            for k in range(KL):
                nc.scalar.activation(c_hi[:, k, T:KEYS], cf[:, k, T:KEYS], ACT.Copy).then_inc(c_hi_done, 1)
            evac_p(7)
            evac_p(8)
            evac_p(9)
            for p in range(10, ZTASK):
                for i in range(2):
                    hi(act, U_Z + 2 * (p - 10) + i)
                evac_p(p)
            sqrt_of(N_KV)
            for k in range(KL):
                act.wait_ge(c_full, k + 1)
                nc.scalar.activation(c_hi[:, k, 0:T], cf[:, k, 0:T], ACT.Copy).then_inc(c_hi_done, 1)
            sqrt_of(N_Q)
            for p in range(ZTASK, len(TASKS3)):
                evac_p(p)
                if p == ZTASK:
                    for k in range(KQ):
                        act.wait_ge(qn_full, k + 1)
                        nc.scalar.activation(qn_hi[:, k, :], qa[:, k, :], ACT.Copy).then_inc(qn_hi_done, 1)
                i = p - ZTASK
                if i < KD:
                    hi(act, U_Z + KD + i)
                else:
                    hi(act, U_G + i - KD)

            def gevac(g, i):
                kind, m, half, eng = GTASKS[i]
                if eng != "act":
                    return
                bank = 4 + i % 4 if g == 0 else 6 + i % 2
                act.wait_ge(g_done, NTASK * g + i + 1)
                slot0 = GH * (g % 2) + 2 * m
                if kind == "nope":
                    for e in range(2):
                        last = nc.scalar.activation(qT[0:NOPE, slot0 + e, blk(half)], ps[64 * e:64 * e + 64, bank, 0:HB], ACT.Copy)
                elif kind == "k":
                    for e in range(2):
                        last = nc.scalar.activation(kT[0:NOPE, slot0 + e, 400 * half:400 * half + 400],
                                                    ps[64 * e:64 * e + 64, bank, 0:400], ACT.Copy)
                else:
                    n = min(P, KEYS - P * m)
                    last = nc.scalar.activation(vt[0:n, KT * (g % 2) + m, :], ps[0:n, bank, 0:GH * VH], ACT.Copy)
                last.then_inc(g_evac_act, 1)

            for i in range(NTASK):
                gevac(0, i)
                if i in (8, 10, 12, 14):
                    hi(act, U_G + KD + (i - 8) // 2)

            def exps(i):
                s = i % NS
                act.wait_ge(max_done, i + 1)
                if i >= 2:
                    act.wait_ge(pt_done, i - 1)
                n, heads = (P * (s % 4 + 1), 2) if s < 8 else (SKEYS, 1)
                for e in range(heads):
                    last = nc.scalar.activation(probs[:, i % 2, e, 0:n], ps[:, 2 * (i % 2) + e, 0:n], ACT.Exp,
                                                bias=negmax[:, i % 2, e:e + 1], scale=SCALE,
                                                accum_out=rowsum[:, i % 2, e:e + 1])
                last.then_inc(exp_done, 1)

            def pt_evac(i):
                s = i % NS
                n = P * (s % 4 + 1) if s < 8 else 2 * P
                act.wait_ge(pt_done, i + 1)
                nc.scalar.activation(pT[:, 0, 0:n], ps[:, 4, 0:n], ACT.Copy).then_inc(pt_evac_act, 1)

            for i in range(NITEM + 1):
                g, s = divmod(i, NS)
                if g + 1 < NG:
                    gevac(g + 1, 2 * s)
                if i >= 1:
                    pt_evac(i - 1)
                if i == NITEM:
                    break
                exps(i)
                if g + 1 < NG and 2 * s + 1 < NTASK:
                    gevac(g + 1, 2 * s + 1)
                ahead = {1: 0, 2: 1, 4: 2, 5: 3, 6: 4, 7: 5}.get(s)
                if ahead is not None and U_G + GU * (g + 2) + ahead < U_BO + KD:
                    hi(act, U_G + GU * (g + 2) + ahead)

            def oo_split(n):
                b, k = divmod(n, KD)
                nc.scalar.activation(o_hi[:, k, blk(b)], zs[:, k, blk(b)], ACT.Copy).then_inc(oo_hi, 1)

            def evac_f(n):
                m, b = FTASKS[n]
                act.wait_ge(f_done, n + 1)
                if m >= 6:
                    act.wait_ge(fsum_done, 1 + b)
                nc.scalar.activation(fsq[:, b, m if m < 6 else m - 4, :], ps[:, n % 4, 0:HB], ACT.Square).then_inc(fsq_done, 1)
                nc.scalar.activation(zs[:, m, blk(b)], ps[:, n % 4, 0:HB], ACT.Copy).then_inc(f_evac, 1)

            act.wait_ge(att_done, NITEM)
            for n in range(2 * KD):
                oo_split(n)
            for i in range(KD):
                hi(act, U_BO + KD + i)
            for n in range(2 * KD):
                evac_f(n)
                if n == 12:
                    sqrt_of(N_F, 0)
            sqrt_of(N_F + 1, 1)

        @block.vector
        def _(dve):
            self_count = [0]

            def link(ins):
                self_count[0] += 1
                ins.then_inc(dve_self, 1)
                return self_count[0]

            nc.vector.memset(neg[:], NEG)
            nc.vector.memset(early[:, CHUNK:P], 0.0)
            nc.vector.memset(early[:, 0:CHUNK], 1.0)
            nc.vector.memset(ones[:], 1.0).then_inc(const_set, 1)

            def fold(sums, more, got, count, done, after=0):
                dve.wait_ge(got, count)
                if after:
                    dve.wait_ge(done, after)
                nc.vector.tensor_tensor(sums, sums, more, ALU.add).then_inc(done, 1)

            def variance(n, src, count, b=None):
                s = slice(0, T) if b is None else blk(b)
                dst = var_b[:, s] if b is not None else two(var_b[:])
                nc.vector.tensor_scalar(dst, src, 1.0 / count, EPS, ALU.mult, ALU.add).then_inc(var_done, 1)

            def inverse(n, dst, b=None):
                s = slice(0, T) if b is None else blk(b)
                dve.wait_ge(sqrt_done, n + 1)
                nc.vector.reciprocal(dst[:, s], var_b[:, s]).then_inc(rstd_done, 1)
                dve.wait_ge(rstd_done, n + 1)

            dve.wait_ge(xstat_done, KD)
            variance(N_IN, pair(4), D)
            inverse(N_IN, rstd_b)

            def u_split(k):
                dve.wait_ge(uhi_done, k + 1)
                nc.vector.tensor_tensor(act_lo[:, k, :], y[:, k, :], act_hi[:, k, :].bitcast(F32),
                                        ALU.subtract).then_inc(u_lo, 1)

            dve.wait_ge(vecs_in, 16)
            for k in range(KD):
                nc.vector.scalar_tensor_tensor(out=y[:, k, :], in0=xT[:, k, :], scalar=vecs[:, V_PRE0 + k:V_PRE0 + k + 1],
                                               in1=rstd_b[:], op0=ALU.mult, op1=ALU.mult).then_inc(u_full, 1)
                if k:
                    u_split(k - 1)
            u_split(KD - 1)

            taps_issued = 0
            LATE = 8
            for j in range(KD):
                late = j < LATE
                dve.wait_ge(v_done, j + 1)
                if j:
                    dve.wait_ge(y_ready, j)
                for w in range(DVE_TAPS):
                    dst = acc[:, w % 2, :]
                    src = v[:, j % 2, w:w + CCOLS]
                    tap = vecs[:, V_DW + WIDTH * j + w:V_DW + WIDTH * j + w + 1]
                    if w == 0:
                        ins = nc.vector.tensor_scalar(dst, src, tap, vecs[:, V_BDW + j:V_BDW + j + 1], ALU.mult, ALU.add)
                    elif w == 1 and late:
                        ins = nc.vector.tensor_scalar(dst, src, tap, None, ALU.mult)
                    else:
                        other = dst
                        if w == 1:
                            other = part[:, j % 2, :]
                            dve.wait_ge(padd_done, PADDS * (j + 1))
                        else:
                            dve.wait_ge(tap_done, taps_issued - 1)
                        ins = nc.vector.scalar_tensor_tensor(out=dst, in0=src, scalar=tap, in1=other,
                                                             op0=ALU.mult, op1=ALU.add)
                    ins.then_inc(tap_done, 1)
                    taps_issued += 1
                dve.wait_ge(tap_done, taps_issued)
                if late:
                    nc.vector.tensor_tensor(acc[:, 0, :], acc[:, 0, :], acc[:, 1, :], ALU.add).then_inc(tap_done, 1)
                    taps_issued += 1
                    dve.wait_ge(tap_done, taps_issued)
                    dve.wait_ge(padd_done, PADDS * (j + 1))
                other = part[:, j % 2, :] if late else acc[:, 1, :]
                nc.vector.tensor_tensor(y[:, j, 0:SEQ], acc[:, 0, 0:SEQ], other[:, 0:SEQ], ALU.add)
                nc.vector.tensor_tensor(y[:, j, SEQ:T], acc[:, 0, SEQ + HIST:CCOLS], other[:, SEQ + HIST:CCOLS],
                                        ALU.add).then_inc(y_ready, 1)

            for b in range(NB):
                dve.wait_ge(ystat_done, KD + b)
                s = blk(b)
                n = link(nc.vector.tensor_scalar(mean_b[:, s], ps[:, 4 + b, 0:HB], 1.0 / D, None, ALU.mult))
                dve.wait_ge(dve_self, n)
                n = link(nc.vector.tensor_tensor(rstd_b[:, s], mean_b[:, s], mean_b[:, s], ALU.mult))
                dve.wait_ge(dve_self, n)
                n = link(nc.vector.scalar_tensor_tensor(out=var_b[:, s], in0=ps[:, 6 + b, 0:HB], scalar=1.0 / D,
                                                        in1=rstd_b[:, s], op0=ALU.mult, op1=ALU.subtract))
                dve.wait_ge(dve_self, n)
                nc.vector.tensor_scalar(var_b[:, s], var_b[:, s], 0.0, EPS, ALU.max, ALU.add).then_inc(var_done, 1)
            for b in range(NB):
                inverse(N_LN + b, rstd_b, b)

            def centre(n):
                b, k = divmod(n, KD)
                return link(nc.vector.tensor_tensor(y[:, k, blk(b)], y[:, k, blk(b)], mean_b[:, blk(b)], ALU.subtract))

            def gate(n):
                b, k = divmod(n, KD)
                dve.wait_ge(ln_silu, n + 1)
                dve.wait_ge(gate_done, k + 1)
                nc.vector.tensor_tensor(y[:, k, blk(b)], y[:, k, blk(b)], zs[:, k, blk(b)], ALU.mult).then_inc(yz_full, 1)

            centred = centre(0)
            for n in range(2 * KD):
                b, k = divmod(n, KD)
                following = centre(n + 1) if n + 1 < 2 * KD else 0
                dve.wait_ge(dve_self, centred)
                nc.vector.tensor_tensor(y[:, k, blk(b)], y[:, k, blk(b)], rstd_b[:, blk(b)], ALU.mult).then_inc(ln_norm, 1)
                centred = following
                if n >= 1:
                    gate(n - 1)
            gate(2 * KD - 1)

            def residual(b, gain, evacuated, count, done, between=None):
                def scale(m):
                    dve.wait_ge(evacuated, count)
                    return link(nc.vector.scalar_tensor_tensor(
                        out=zs[:, m, blk(b)], in0=zs[:, m, blk(b)], scalar=vecs[:, gain + m:gain + m + 1],
                        in1=rstd_b[:, blk(b)], op0=ALU.mult, op1=ALU.mult))
                scaled_at = scale(0)
                for m in range(KD):
                    following = scale(m + 1) if m + 1 < KD else 0
                    dve.wait_ge(dve_self, scaled_at)
                    nc.vector.tensor_tensor(xT[:, m, blk(b)], xT[:, m, blk(b)], zs[:, m, blk(b)], ALU.add).then_inc(done, 1)
                    scaled_at = following
                    if between is not None:
                        between(m)

            def rotate_keys(b):
                dve.wait_ge(p_evac, TASKS3.index(("kv", 2, b)) + 1)
                if b == 0:
                    dve.wait_ge(tables_in, 48)
                dst = kr[2 * ROPE:3 * ROPE, blk(b)]
                tmp = mean_b[2 * ROPE:3 * ROPE, blk(b)]
                nc.vector.tensor_tensor(dst, kr_ps[0:ROPE, :], cc[0:ROPE, blk(b)], ALU.mult)
                n = link(nc.vector.tensor_tensor(tmp, kr_ps[ROPE:2 * ROPE, :], kr[ROPE:2 * ROPE, blk(b)], ALU.mult))
                dve.wait_ge(dve_self, n)
                nc.vector.tensor_tensor(dst, dst, tmp, ALU.add).then_inc(kr_done, 1)

            def ofold(b, i):
                fold(y[:, 0:2, blk(b)], y[:, 2 * i:2 * i + 2, blk(b)], osq_done, KD * b + 2 * i + 2, osum_done,
                     3 * b + i - 1 if i > 1 else 0)

            def hfold(b, i):
                fold(y[:, 0:2, blk(b)], y[:, 2 * i:2 * i + 2, blk(b)], hsq_done, KD * b + 2 * i + 2, hsum_done,
                     3 * b + i - 1 if i > 1 else 0)

            for i in range(1, 4):
                ofold(0, i)
            for b in range(NB):
                dve.wait_ge(ostat_done, b + 1)
                variance(N_O[b], ps[:, 4 + b, 0:HB], D, b)
                inverse(N_O[b], rstd_b, b)
                residual(b, V_POST0, o_evac, KD * (b + 1), h_done,
                         lambda m: hfold(b, 1) if m == 5 else hfold(b, 2) if m == KD - 1 else None)
                hfold(b, 3)
                if b == 0:
                    ofold(1, 1)
                else:
                    rotate_keys(0)
                dve.wait_ge(hstat_done, b + 1)
                variance(N_H[b], ps[:, 6 + b, 0:HB], D, b)
                inverse(N_H[b], mean_b, b)
                dve.wait_ge(h_done, KD * (b + 1))
                for m in range(KD):
                    nc.vector.tensor_tensor(zs[:, m, blk(b)], xT[:, m, blk(b)], mean_b[:, blk(b)], ALU.mult).then_inc(xn_full, 1)
                if b == 0:
                    ofold(1, 2)
                    ofold(1, 3)

            def qfold(b):
                fold(y[:, KL:KL + 2, blk(b)], y[:, KL + 2:KL + 4, blk(b)], psq_done,
                     (KL + KQ) * (b + 1), qsum_done)

            qfold(0)
            dve.wait_ge(xn_full, 2 * KD)
            rotate_keys(1)
            qfold(1)
            dve.wait_ge(pstat_done, 1)
            variance(N_KV, pair(4), LORA)
            inverse(N_KV, rstd_b)
            for k in range(KL):
                nc.vector.scalar_tensor_tensor(out=cf[:, k, 0:T], in0=cf[:, k, 0:T], scalar=vecs[:, V_KVA + k:V_KVA + k + 1],
                                               in1=rstd_b[:], op0=ALU.mult, op1=ALU.mult).then_inc(c_full, 1)
            dve.wait_ge(pstat_done, 2)
            variance(N_Q, pair(6), QL)
            dve.wait_ge(c_full, KL)
            inverse(N_Q, rstd_b)
            for k in range(KQ):
                nc.vector.scalar_tensor_tensor(out=qa[:, k, :], in0=qa[:, k, :], scalar=vecs[:, V_QA + k:V_QA + k + 1],
                                               in1=rstd_b[:], op0=ALU.mult, op1=ALU.mult).then_inc(qn_full, 1)

            def gevac(g, i):
                kind, m, half, eng = GTASKS[i]
                if eng != "dve":
                    return
                bank = 4 + i % 4 if g == 0 else 6 + i % 2
                dve.wait_ge(g_done, NTASK * g + i + 1)
                if kind == "rope":
                    src = ps[:, bank, 0:HB]
                    if g >= 2 and half == 0:
                        dve.wait_ge(rope_moved, 128 * (g - 1))
                    if g or half:
                        dve.wait_ge(rope_done, 2 * g + half)
                    nc.vector.tensor_tensor(rope_a[:, 0, :], src, cc[:, blk(half)], ALU.mult)
                    nc.vector.tensor_tensor(rope_a[0:64, 1, :], src[64:128], ss[64:128, blk(half)], ALU.mult)
                    n = link(nc.vector.tensor_tensor(rope_a[64:128, 1, :], src[0:64], ss[0:64, blk(half)], ALU.mult))
                    dve.wait_ge(dve_self, n)
                    nc.vector.tensor_tensor(rope_r[:, g % 2, blk(half)], rope_a[:, 0, :], rope_a[:, 1, :],
                                            ALU.add).then_inc(rope_done, 1)
                    dve.wait_ge(rope_done, 2 * g + half + 1)
                    dve.sem_inc(g_evac_dve, 1)
                    return
                if kind == "k":
                    slot0 = GH * (g % 2) + 2 * m
                    for e in range(2):
                        last = nc.vector.tensor_copy(kT[0:NOPE, slot0 + e, 400 * half:400 * half + 400],
                                                     ps[64 * e:64 * e + 64, bank, 0:400])
                else:
                    n = min(P, KEYS - P * m)
                    last = nc.vector.tensor_copy(vt[0:n, KT * (g % 2) + m, :], ps[0:n, bank, 0:GH * VH])
                last.then_inc(g_evac_dve, 1)

            def maxima(i):
                s = i % NS
                n, heads = (P * (s % 4 + 1), 2) if s < 8 else (SKEYS, 1)
                for e in range(heads):
                    dve.wait_ge(scores_done, 2 * i + (e + 1 if heads == 2 else 2))
                    at = link(nc.vector.reduce_max(rowmax[:, i % 2, e:e + 1], ps[:, 2 * (i % 2) + e, 0:n], axis=AX_X))
                if i >= 2:
                    dve.wait_ge(exp_done, i - 1)
                dve.wait_ge(dve_self, at)
                nc.vector.tensor_scalar(negmax[:, i % 2, 0:heads], rowmax[:, i % 2, 0:heads], -SCALE, None,
                                        ALU.mult).then_inc(max_done, 1)

            def pt_evac(i):
                s = i % NS
                dve.wait_ge(pt_done, i + 1)
                if s < 8:
                    n = P * (s % 4 + 1)
                    nc.vector.tensor_copy(pT[:, 1, 0:n], ps[:, 5, 0:n]).then_inc(pt_evac_dve, 1)
                else:
                    nc.vector.tensor_copy(pT[0:SKEYS - 2 * P, 1, 0:P], ps[0:SKEYS - 2 * P, 5, 0:P]).then_inc(pt_evac_dve, 1)

            def normalise(i):
                s = i % NS
                n, heads = (P * (s % 4 + 1), 2) if s < 8 else (SKEYS, 1)
                dve.wait_ge(exp_done, i + 1)
                at = link(nc.vector.reciprocal(rinv[:, i % 2, 0:heads], rowsum[:, i % 2, 0:heads]))
                dve.wait_ge(dve_self, at)
                for e in range(heads):
                    last = nc.vector.tensor_scalar(probs[:, i % 2, e, 0:n], probs[:, i % 2, e, 0:n],
                                                   rinv[:, i % 2, e:e + 1], None, ALU.mult)
                last.then_inc(prob_done, 1)

            def gated(i):
                g, s = divmod(i, NS)
                dve.wait_ge(pv_done, i + 1)
                if s < 8:
                    m, q = 2 * g + s // 4, P * (s % 4)
                    nc.vector.tensor_tensor(zs[:, m, q:q + P], ps[:, 2 * (i % 2) + 1, 0:P], zs[:, m, q:q + P], ALU.mult).then_inc(att_done, 1)
                else:
                    dst = zs[:, 2 * g:2 * g + 2, SEQ:T]
                    nc.vector.tensor_tensor(dst, ps[:, 2 * (i % 2) + 1, 0:2 * DEC].rearrange("p (m q) -> p m q", m=2), dst,
                                            ALU.mult).then_inc(att_done, 1)

            dve.wait_ge(c_stored, 16)
            for i in range(NTASK):
                gevac(0, i)
            dve.wait_ge(p_evac, len(TASKS3))
            for i in range(NITEM + 1):
                g, s = divmod(i, NS)
                if g + 1 < NG:
                    gevac(g + 1, 2 * s)
                if i < NITEM:
                    maxima(i)
                if i >= 1:
                    pt_evac(i - 1)
                if g + 1 < NG and 2 * s + 1 < NTASK:
                    gevac(g + 1, 2 * s + 1)
                if i < NITEM:
                    normalise(i)
                if i >= 1:
                    gated(i - 1)

            for n in range(2 * KD):
                b, k = divmod(n, KD)
                dve.wait_ge(oo_hi, n + 1)
                nc.vector.tensor_tensor(o_lo[:, k, blk(b)], zs[:, k, blk(b)], o_hi[:, k, blk(b)].bitcast(F32),
                                        ALU.subtract).then_inc(oo_lo, 1)
            for b, more, count in ((0, 2, 4), (1, 2, 8), (0, 4, 10), (0, 2, 12)):
                fold(fsq[:, b, 0:2, :], fsq[:, b, more:more + 2, :], fsq_done, count, fsum_done, {10: 1, 12: 3}.get(count, 0))
            for b in range(NB):
                dve.wait_ge(fstat_done, b + 1)
                variance(N_F + b, ps[:, 4 + b, 0:HB], D, b)
                inverse(N_F + b, rstd_b, b)

                def between(m):
                    if b == 0 and m in (3, 7):
                        more, count, after = ((4, 14, 2), (2, 16, 5))[m // 4]
                        fold(fsq[:, 1, 0:2, :], fsq[:, 1, more:more + 2, :], fsq_done, count, fsum_done, after)

                residual(b, V_POST1, f_evac, (12, 16)[b], y_done, between)

        @block.gpsimd
        def _(pool):
            nc.gpsimd.memset(v[:, :, 0:HIST], 0.0)
            for u in range(8):
                lo(pool, u)

            pool.wait_ge(state_in, 16)
            for j in range(KD):
                nxt = 8 * (j + 1)
                for u in range(4):
                    lo(pool, nxt + u)
                if j >= 2:
                    pool.wait_ge(y_ready, j - 1)
                    pool.wait_ge(conv_out_done, 32 * (j - 1))
                nc.gpsimd.tensor_copy(v[:, j % 2, HIST + SEQ:2 * HIST + SEQ], state[:, j, :])
                pool.wait_ge(mt_evac, 3 * j + 2)
                nc.gpsimd.tensor_tensor(v[:, j % 2, HIST:HIST + SEQ], a_sb[:, 0:SEQ], sig[:, 0:SEQ], ALU.mult)
                nc.gpsimd.tensor_tensor(v[:, j % 2, 2 * HIST + SEQ:VCOLS], a_sb[:, SEQ:T], sig[:, SEQ:T],
                                        ALU.mult).then_inc(v_done, 1)
                lo(pool, nxt + 4)
                for i in range(1, POOL_TAPS):
                    if i < 4:
                        lo(pool, nxt + 4 + i)
                    pool.wait_ge(prod_done, POOL_TAPS * j + i + 1)
                    p = part[:, j % 2, :]
                    if i >= 2:
                        pool.wait_ge(padd_done, PADDS * j + i - 1)
                    nc.gpsimd.tensor_tensor(p, prod[:, i % PRODS, :], prod[:, 0, :] if i == 1 else p,
                                            ALU.add).then_inc(padd_done, 1)
            for u in range(U_AO + KD, U_KV):
                lo(pool, u)

            def rest(full, half, low, n, done, got):
                pool.wait_ge(got, n)
                nc.gpsimd.tensor_tensor(low, full, half.bitcast(F32), ALU.subtract).then_inc(done, 1)

            for n in range(2 * KD):
                b, k = divmod(n, KD)
                rest(y[:, k, blk(b)], act_hi[:, k, blk(b)], act_lo[:, k, blk(b)], n + 1, yz_lo, yz_hi)

            def xn_rest(n):
                b, m = divmod(n, KD)
                rest(zs[:, m, blk(b)], act_hi[:, m, blk(b)], act_lo[:, m, blk(b)], n + 1, xn_lo, xn_hi)

            for u in range(U_KV, U_KV + 4):
                lo(pool, u)
            for i in range(2):
                for n in range(4 * i, 4 * i + 4):
                    xn_rest(n)
                for u in range(U_KV + 4 + 2 * i, U_KV + 6 + 2 * i):
                    lo(pool, u)
            for u in range(U_Q, U_Z):
                lo(pool, u)
            for n in range(KD, 2 * KD):
                xn_rest(n)
            for k in range(KL):
                rest(cf[:, k, T:KEYS], c_hi[:, k, T:KEYS], c_lo[:, k, T:KEYS], k + 1, c_lo_done, c_hi_done)
            for u in range(U_Z, U_Z + KD):
                lo(pool, u)
            for k in range(KL):
                rest(cf[:, k, 0:T], c_hi[:, k, 0:T], c_lo[:, k, 0:T], KL + k + 1, c_lo_done, c_hi_done)
            for u in range(U_Z + KD, U_Z + KD + 3):
                lo(pool, u)
            for k in range(KQ):
                rest(qa[:, k, :], qn_hi[:, k, :], qn_lo[:, k, :], k + 1, qn_lo_done, qn_hi_done)
            for u in range(U_Z + KD + 3, U_G + GU):
                lo(pool, u)
            pool.wait_ge(p_done, len(TASKS3))
            nc.gpsimd.memset(ident[:], 0.0).then_inc(pool_set, 1)
            pool.wait_ge(pool_set, 1)
            nc.gpsimd.affine_select(out=ident[:], in_=ident[:], compare_op=ALU.not_equal, fill=1.0, base=0,
                                    pattern=[[-1, P]], channel_multiplier=1).then_inc(pool_set, 1)
            for u in range(U_G + GU, UNITS):
                lo(pool, u)

        @block.tensor
        def _(pe):
            def sums(banks, src, first, last):
                for b in range(NB):
                    ins = nc.tensor.matmul(ps[:, banks + b, 0:HB], ones[:], src[:, b, :], start=first, stop=last)
                return ins

            pe.wait_ge(const_set, 1)
            for k in range(KD):
                pe.wait_ge(xsq_done, k + 1)
                sums(4, sq[:, 2 * (k % 2):2 * (k % 2) + 2, :], k == 0, k == KD - 1).then_inc(xstat_done, 1)

            def ystats(j):
                pe.wait_ge(ysq_done, j + 1)
                for b in range(NB):
                    nc.tensor.matmul(ps[:, 4 + b, 0:HB], ones[:], y[:, j, blk(b)], start=j == 0, stop=j == KD - 1)
                    last = nc.tensor.matmul(ps[:, 6 + b, 0:HB], ones[:], sq[:, 2 * (j % 2) + b, :], start=j == 0, stop=j == KD - 1)
                    if b or j == KD - 1:
                        last.then_inc(ystat_done, 1)

            pe.wait_ge(var_done, 1)
            for j in range(KD):
                for i in range(3):
                    t = 3 * j + i
                    if t >= 2:
                        pe.wait_ge(mt_evac, t - 1)
                    for k in range(KD):
                        if i == 0:
                            ready(pe, 8 * j + k)
                            if j == 0:
                                pe.wait_ge(u_lo, k + 1)
                        w = cols(slot(8 * j + k), P * i)
                        for b in range(NB):
                            last = mm3(ps[:, 2 * (t % 2) + b, 0:HB], w, act_hi[:, k, blk(b)], act_lo[:, k, blk(b)],
                                       k == 0, k == KD - 1)
                    last.then_inc(mt_done, 1)
                if j >= 2:
                    ystats(j - 2)
            ystats(KD - 2)
            ystats(KD - 1)

            def product(bank, units, m, b, kts):
                for k in kts:
                    if m == 0 and b == 0:
                        ready(pe, units + k)
                    last = mm3(ps[:, bank, 0:HB], cols(slot(units + k), P * m), act_hi[:, k, blk(b)],
                               act_lo[:, k, blk(b)], k == 0, k == KD - 1)
                return last

            def square_sums(bank, src, tiles=2):
                for i in range(tiles):
                    last = nc.tensor.matmul(ps[:, bank, 0:HB], ones[:], src[:, i, :], start=i == 0, stop=i == tiles - 1)
                return last

            def ostat(b):
                pe.wait_ge(osum_done, 3 * (b + 1))
                square_sums(4 + b, y[:, 0:2, blk(b)]).then_inc(ostat_done, 1)

            def hstat(b):
                pe.wait_ge(hsum_done, 3 * (b + 1))
                square_sums(6 + b, y[:, 0:2, blk(b)]).then_inc(hstat_done, 1)

            pe.wait_ge(mt_evac, 3 * KD)
            for k in range(KD):
                pe.wait_ge(yz_lo, k + 1)
                for m in range(4):
                    last = product(m, U_AO, m, 0, [k])
                    if k == KD - 1:
                        last.then_inc(o_done, 1)
            for n in range(4, 2 * KD):
                b, m = divmod(n, KD)
                pe.wait_ge(o_evac, n - 3)
                if n == KD:
                    pe.wait_ge(yz_lo, 2 * KD)
                product(n % 4, U_AO + 8 * (m // 4), m % 4, b, range(KD)).then_inc(o_done, 1)
                if n == 8:
                    ostat(0)
                if n == 12:
                    hstat(0)

            for p, (kind, m, b) in enumerate(TASKS3):
                if p >= 4:
                    pe.wait_ge(p_evac, p - 3)
                else:
                    pe.wait_ge(o_evac, 13 + p)
                units, col = {"kv": (U_KV, m), "q": (U_Q, m), "z": (U_Z + 8 * (m // 4), m % 4)}[kind]
                if kind == "kv" and m == 0:
                    pe.wait_ge(xn_lo, KD * (b + 1))
                if kind == "kv" and m == KL:
                    for k in range(KD):
                        last = mm3(ps[0:2 * ROPE, p % 4, 0:HB], cols(slot(U_KV + k), LORA, 2 * ROPE),
                                   act_hi[:, k, blk(b)], act_lo[:, k, blk(b)], k == 0, k == KD - 1)
                    last.then_inc(p_done, 1)
                else:
                    product(p % 4, units, col, b, range(KD)).then_inc(p_done, 1)
                if p == 0:
                    ostat(1)
                if p == 4:
                    hstat(1)
                if p == 10:
                    pe.wait_ge(psq_done, 2 * KL + KQ)
                    for b2 in range(NB):
                        last = square_sums(4 + b2, y[:, 0:KL, blk(b2)], KL)
                    last.then_inc(pstat_done, 1)
                if p == ZTASK:
                    pe.wait_ge(qsum_done, 2)
                    for b2 in range(NB):
                        last = square_sums(6 + b2, y[:, KL:KL + 2, blk(b2)])
                    last.then_inc(pstat_done, 1)

            def gtask(g, i):
                kind, m, half, _ = GTASKS[i]
                bank = 4 + i % 4 if g == 0 else 6 + i % 2
                prev = i - 4 if g == 0 else i - 2
                if prev >= 0:
                    eng = GTASKS[prev][3]
                    pe.wait_ge(g_evac_act if eng == "act" else g_evac_dve, evacs(eng, g, prev))
                elif g > 0:
                    pe.wait_ge(g_evac_act, evacs("act", g, -1))
                    pe.wait_ge(g_evac_dve, evacs("dve", g, -1))
                base = U_G + GU * g
                if i == 0:
                    ready(pe, base + KQ - 1)
                    if g == 0:
                        pe.wait_ge(qn_lo_done, KQ)
                if i == NQTASK:
                    ready(pe, base + GU - 1)
                    if g == 0:
                        pe.wait_ge(c_lo_done, 2 * KL)
                if kind in ("rope", "nope"):
                    for k in range(KQ):
                        last = mm3(ps[:, bank, 0:HB], cols(slot(base + k), P * m), qn_hi[:, k, blk(half)],
                                   qn_lo[:, k, blk(half)], k == 0, k == KQ - 1)
                elif kind == "k":
                    keys = slice(400 * half, 400 * half + 400)
                    for k in range(KL):
                        last = mm3(ps[:, bank, 0:400], cols(slot(base + KQ + k), P * m), c_hi[:, k, keys],
                                   c_lo[:, k, keys], k == 0, k == KL - 1)
                else:
                    n = min(P, KEYS - P * m)
                    keys = slice(P * m, P * m + n)
                    for k in range(KL):
                        wh, wl = cols(slot(base + KQ + k), GH * NOPE, GH * VH)
                        out = ps[0:n, bank, 0:GH * VH]
                        nc.tensor.matmul(out, c_hi[:, k, keys], wh, start=k == 0, stop=False)
                        nc.tensor.matmul(out, c_hi[:, k, keys], wl, start=False, stop=False)
                        last = nc.tensor.matmul(out, c_lo[:, k, keys], wh, start=False, stop=k == KL - 1)
                last.then_inc(g_done, 1)

            for i in range(NTASK):
                gtask(0, i)

            def scores(i):
                g, s = divmod(i, NS)
                if i >= 2:
                    pe.wait_ge(exp_done, i - 1)
                if i == 0:
                    pe.wait_ge(p_evac, len(TASKS3))
                    pe.wait_ge(krows_in, 16 * 2 * GH)
                if s == 0:
                    pe.wait_ge(g_evac_act, evacs("act", g, NTASK - 1))
                    pe.wait_ge(g_evac_dve, evacs("dve", g, NTASK - 1))
                    pe.wait_ge(rope_moved, 128 * (g + 1))
                if s < 8:
                    q, n = P * (s % 4), P * (s % 4 + 1)
                    for e in range(2):
                        h = GH * (g % 2) + 2 * (s // 4) + e
                        bank = 2 * (i % 2) + e
                        if e == 1 and i >= 2:
                            pe.wait_ge(att_done, i - 1)
                        nc.tensor.matmul(ps[:, bank, 0:n], qT[0:NOPE + ROPE, h, q:q + P], kT[0:NOPE + ROPE, h, 0:n],
                                         start=True, stop=True)
                        nc.tensor.matmul(ps[:, bank, n - CHUNK:n], early[:], neg[:], start=False, stop=True,
                                         skip_group_check=True).then_inc(scores_done, 1)
                else:
                    for e in range(GH):
                        h = GH * (g % 2) + e
                        last = nc.tensor.matmul(ps[DEC * e:DEC * e + DEC, 2 * (i % 2), 0:SKEYS],
                                                qT[0:NOPE + ROPE, h, SEQ:T], kT[0:NOPE + ROPE, h, SEQ:KEYS],
                                                start=True, stop=True)
                    last.then_inc(scores_done, 2)

            def transposes(i):
                s = i % NS
                pe.wait_ge(prob_done, i + 1)
                if i >= 1:
                    pe.wait_ge(pt_evac_act, i)
                    pe.wait_ge(pt_evac_dve, i)
                if s < 8:
                    for e in range(2):
                        for t in range(s % 4 + 1):
                            last = nc.tensor.transpose(ps[:, 4 + e, P * t:P * t + P], probs[:, i % 2, e, P * t:P * t + P], ident[:])
                else:
                    for t in range(3):
                        n = min(P, SKEYS - P * t)
                        last = nc.tensor.transpose(ps[0:n, 4 + t // 2, P * (t % 2):P * (t % 2) + P],
                                                   probs[:, i % 2, 0, P * t:P * t + n], ident[:])
                last.then_inc(pt_done, 1)

            def values(i):
                g, s = divmod(i, NS)
                pe.wait_ge(pt_evac_act, i + 1)
                pe.wait_ge(pt_evac_dve, i + 1)
                v0 = KT * (g % 2)
                if s < 8:
                    for t in range(s % 4 + 1):
                        for e in range(2):
                            col = VH * (2 * (s // 4) + e)
                            last = nc.tensor.matmul(ps[64 * e:64 * e + 64, 2 * (i % 2) + 1, 0:P], vt[:, v0 + t, col:col + VH],
                                                    pT[:, e, P * t:P * t + P], start=t == 0, stop=t == s % 4)
                else:
                    for m in range(2):
                        for t in range(3):
                            n = min(P, SKEYS - P * t)
                            for e in range(2):
                                h = 2 * m + e
                                last = nc.tensor.matmul(ps[64 * e:64 * e + 64, 2 * (i % 2) + 1, DEC * m:DEC * m + DEC],
                                                        vt[0:n, v0 + 4 + t, VH * h:VH * h + VH],
                                                        pT[0:n, t // 2, P * (t % 2) + DEC * h:P * (t % 2) + DEC * h + DEC],
                                                        start=t == 0, stop=t == 2)
                last.then_inc(pv_done, 1)

            pe.wait_ge(pool_set, 2)
            for i in range(NITEM + 1):
                g, s = divmod(i, NS)
                if g + 1 < NG:
                    gtask(g + 1, 2 * s)
                if i < NITEM:
                    scores(i)
                if i >= 1:
                    transposes(i - 1)
                if g + 1 < NG and 2 * s + 1 < NTASK:
                    gtask(g + 1, 2 * s + 1)
                if i >= 1:
                    values(i - 1)

            def fstat(b):
                pe.wait_ge(fsum_done, (4, 6)[b])
                square_sums(4 + b, fsq[:, b, 0:2, :]).then_inc(fstat_done, 1)

            def fproduct(n, kts):
                m, b = FTASKS[n]
                for k in kts:
                    last = mm3(ps[:, n % 4, 0:HB], cols(slot(U_BO + 8 * (m // 4) + k), P * (m % 4)), o_hi[:, k, blk(b)],
                               o_lo[:, k, blk(b)], k == 0, k == KD - 1)
                return last

            ready(pe, U_BO + KD - 1)
            for k in range(KD):
                pe.wait_ge(oo_lo, k + 1)
                for n in range(4):
                    last = fproduct(n, [k])
                    if k == KD - 1:
                        last.then_inc(f_done, 1)
            for n in range(4, 2 * KD):
                pe.wait_ge(f_evac, n - 3)
                if n == 4:
                    pe.wait_ge(oo_lo, 2 * KD)
                if n == 8:
                    ready(pe, UNITS - 1)
                fproduct(n, range(KD)).then_inc(f_done, 1)
                if n == 12:
                    fstat(0)
            fstat(1)


def kernel(x_prompt, x_sample, state_conv, cache_kv_latent, cache_k_rope,
           g_pre, g_post, w_a_in, w_a_dw, b_a_dw, g_a_ln, b_a_ln, w_a_out,
           g_kv_in, w_kv_a, g_kv_a, w_kv_b, w_b_in, g_q_a, w_q_b, w_b_out):
    import numpy as np
    import concourse.bacc as bacc
    from concourse import mybir as mb
    from concourse.bass_utils import run_bass_kernel_spmd

    f = lambda a: np.asarray(a)

    def tiles(a):
        return f(a).reshape(-1, P, a.shape[-1])

    def columns(a):
        return f(a).reshape(-1, P).T

    def rows(a):
        return f(a).T.reshape(-1, P, a.shape[0]).transpose(1, 0, 2)

    x = np.concatenate([f(x_prompt)[0], f(x_sample)[0]], axis=0)
    win = tiles(w_a_in[0]).reshape(KD, P, 3, KD, P)
    win = win[:, :, [1, 0, 2]].transpose(3, 0, 1, 2, 4).reshape(KD * KD, P, 3 * P)

    def chunks(a, n=512):
        t = tiles(a)
        return t.reshape(t.shape[0], P, -1, n).transpose(2, 0, 1, 3).reshape(-1, P, n)

    wkv = tiles(w_kv_a)
    half = ROPE // 2
    wkv = np.concatenate([wkv, wkv[..., LORA + half:], wkv[..., LORA:LORA + half]], axis=-1)
    wqb = tiles(w_q_b[0]).reshape(KQ, P, NG, GH, NOPE + ROPE)
    nope = wqb[..., :NOPE].reshape(KQ, P, NG, GH * NOPE)
    rope = wqb[..., NOPE:].reshape(KQ, P, NG, GH, 2, half).transpose(0, 1, 2, 4, 3, 5).reshape(KQ, P, NG, GH * ROPE)
    wqb = np.concatenate([nope, rope], axis=-1).transpose(2, 0, 1, 3).reshape(NG * KQ, P, 3 * P)
    wkb = tiles(w_kv_b).reshape(KL, P, NG, GH, 2, NOPE).transpose(2, 0, 1, 4, 3, 5).reshape(NG * KL, P, 2 * GH * NOPE)

    vec = np.concatenate(
        [columns(g_pre[0]), columns(g_pre[1]), columns(g_post[0]), columns(g_post[1]),
         f(w_a_dw)[0].T.reshape(KD, P, WIDTH).transpose(1, 0, 2).reshape(P, KD * WIDTH),
         columns(b_a_dw[0]), columns(g_a_ln[0]), columns(b_a_ln[0]), columns(g_kv_in), columns(g_kv_a),
         columns(g_q_a[0])], axis=1)

    pos = np.concatenate([np.arange(SEQ), PAST + np.arange(DEC)]).astype(np.float32)
    inv = (np.float32(10000.0) ** (-np.arange(half, dtype=np.float32) / np.float32(half))).astype(np.float32)
    ang = inv[:, None] * pos[None, :]
    cos, sin = np.cos(ang).astype(np.float32), np.sin(ang).astype(np.float32)
    cc = np.tile(cos, (8, 1))
    ss = np.concatenate([np.tile(sin, (4, 1)), -np.tile(sin, (4, 1))], axis=0)
    krs = np.concatenate([-sin, sin], axis=0)

    arrays = {
        "x_t": rows(x), "state_t": rows(f(state_conv)[0, 0]), "ckv_t": rows(f(cache_kv_latent)[0]),
        "ckr_t": f(cache_k_rope)[0].T, "w_in": win, "w_ao": chunks(w_a_out[0]), "w_kv": wkv,
        "w_bi": chunks(w_b_in[0]), "w_qb": wqb, "w_kb": wkb, "w_bo": chunks(w_b_out[0]),
        "vecs_d": vec, "cc_d": cc, "ss_d": ss, "krs_d": krs,
    }
    arrays = {k: np.ascontiguousarray(a) for k, a in arrays.items()}
    outs = {"y_out": (P, KD, T), "conv_out": (P, KD, 2 * HIST), "c_out": (P, KL, T), "kr_out": (ROPE, T)}

    nc = bacc.Bacc("TRN2", target_bir_lowering=False, num_devices=1)
    args = [nc.dram_tensor(k, a.shape, mb.dt.from_np(a.dtype), kind="ExternalInput").ap() for k, a in arrays.items()]
    args += [nc.dram_tensor(k, s, mb.dt.float32, kind="ExternalOutput").ap() for k, s in outs.items()]
    build(nc, *args)
    r = run_bass_kernel_spmd(nc, [arrays], core_ids=[0]).results[0]

    def tokens(a):
        a = np.asarray(a)
        return np.ascontiguousarray(a.transpose(2, 1, 0).reshape(a.shape[2], -1))

    yt, ct, cv, krt = tokens(r["y_out"]), tokens(r["c_out"]), tokens(r["conv_out"]), np.asarray(r["kr_out"]).T
    return (yt[None, :SEQ], yt[None, SEQ:], cv[None, None, :HIST], ct[None, :SEQ], np.ascontiguousarray(krt[None, :SEQ]),
            cv[None, None, HIST:], ct[None, SEQ:], np.ascontiguousarray(krt[None, SEQ:]))
```

```python
from contextlib import ExitStack

import concourse.bass as bass
from concourse import mybir

F32 = mybir.dt.float32
F32R = mybir.dt.float32r
BF16 = mybir.dt.bfloat16
ALU = mybir.AluOpType
ACT = mybir.ActivationFunctionType
AX_X = mybir.AxisListType.X

P = 128
D = 1024
KD = D // P
SEQ, DEC, PAST = 512, 32, 256
T = SEQ + DEC
HB = T // 2
NB = 2
LORA = 256
KL = LORA // P
QL = 512
KQ = QL // P
HEADS, NOPE, ROPE, VH = 16, 64, 32, 64
GH = 4
NG = HEADS // GH
KEYS = T + PAST
SKEYS = KEYS - SEQ
WIDTH = 31
HIST = WIDTH - 1
VCOLS = HIST + SEQ + HIST + DEC
CCOLS = VCOLS - HIST
CHUNK = 64
EPS = 1e-6
SCALE = 1.0 / float(NOPE + ROPE) ** 0.5
NEG = -1e30

STAGES = 5
RING = 16
POOL_TAPS = 7
PADDS = POOL_TAPS - 1
LAST_DVE_TAPS, PE_TAPS = 13, 10


def tap_split(j):
    return (LAST_DVE_TAPS, LAST_DVE_TAPS + PE_TAPS) if j == KD - 1 else (WIDTH - POOL_TAPS, WIDTH - POOL_TAPS)


PRODS = 4

U_IN = 0
U_AO = U_IN + 8 * KD
U_KV = U_AO + 2 * KD
U_Q = U_KV + KD
U_Z = U_Q + KD
U_G = U_Z + 2 * KD
GU = KQ + KL
U_BO = U_G + NG * GU
UNITS = U_BO + 2 * KD
POOL_FINAL = 5
AO_AFTER = (1, 2, 3, 4, 5, 6, 7, 8)

TASKS3 = ([("kv", m, 0) for m in range(3)] + [("q", m, 0) for m in range(KQ)]
          + [("kv", m, 1) for m in range(3)] + [("q", m, 1) for m in range(KQ)]
          + [("z", m, b) for m in range(KD) for b in range(2)])
ZTASK = TASKS3.index(("z", 0, 0))
C_AT, Q_AT = 4, 6
N_IN, N_LN, N_O, N_H, N_KV, N_Q, N_F = 0, 2, (4, 6), (5, 7), 8, 9, 10


def group_task(kind, m, half=0):
    eng = {"rope": "dve", "nope": "act", "k": ("act", "dve")[half], "v": ("dve", "act")[m % 2]}[kind]
    return kind, m, half, eng


GTASKS = [group_task(*t) for t in (
    ("rope", 2, 0), ("rope", 2, 1), ("nope", 0, 0), ("k", 0, 0), ("v", 0), ("nope", 0, 1), ("v", 1), ("nope", 1, 0),
    ("nope", 1, 1), ("v", 2), ("k", 0, 1), ("v", 3), ("k", 1, 0), ("v", 4), ("k", 1, 1), ("v", 5), ("v", 6))]
NTASK = len(GTASKS)
QTASKS = max(i for i, t in enumerate(GTASKS) if t[0] in ("rope", "nope")) + 1
KT = 7
NS = 9
NITEM = NG * NS
PROLOGUE = 12
STEPS = NITEM + 2
STEP_TASKS = []
for i in range(STEPS):
    n = PROLOGUE + sum(map(len, STEP_TASKS))
    STEP_TASKS.append([t for t in range(n, n + (1 if i % 4 == 3 else 2)) if t < NG * NTASK])
ACT_PT = NITEM - 5
AHEAD = {0: (10,), 1: (11,), 6: (12,), 7: (13,), 9: (14,), 10: (15,), 11: (16, 17), 15: (18,), 16: (19,), 19: (20,), 20: (21,), 21: (22, 23),
         24: (24,), 25: (25,), 28: (26,), 29: (27,), 30: (28,), 31: (29,), 33: (30,), 34: (31,)}
FTASKS = [(m, b) for c in range(2) for b in range(2) for m in range(4 * c, 4 * c + 4)]


def evacs(eng, n):
    return sum(GTASKS[t % NTASK][3] == eng for t in range(n + 1))


def task_bank(n):
    return 4 + n % 4 if n < PROLOGUE else 6 + n % 2


def out_bank(i):
    return 2 * ((i + 1) % 2) + 1


def tasks_needed(i):
    g, s = divmod(i, NS)
    m, q = divmod(s, 4)
    if s == NS - 1:
        return NTASK * (g + 1)
    reads = [("rope", 2, 1), ("nope", m, q // 2), ("k", m, q // 3), ("v", q, 0)]
    return NTASK * g + max(n for n, t in enumerate(GTASKS) if t[:3] in reads) + 1


V_PRE0, V_PRE1, V_POST0, V_POST1 = 0, 8, 16, 24
V_DW = 32
V_BDW = V_DW + 8 * WIDTH
V_GLN, V_BLN, V_KVIN = V_BDW + 8, V_BDW + 16, V_BDW + 24
V_KVA = V_KVIN + 8
V_QA = V_KVA + 2
NVEC = V_QA + 4


def unit_cols(u):
    if u < U_AO:
        return 384
    if U_KV <= u < U_Q:
        return 320
    if U_G <= u < U_BO and (u - U_G) % GU < KQ:
        return 384
    return 512


def unit_gain(u):
    if U_KV <= u < U_Q:
        return V_KVIN + (u - U_KV)
    if U_Q <= u < U_G:
        return V_PRE1 + (u - U_Q) % KD
    return None


def build(nc, x_t, state_t, ckv_t, ckr_t, w_in, w_ao, w_kv, w_bi, w_qb, w_kb, w_bo, vecs_d, cc_d, ss_d, krs_d,
          y_out, conv_out, c_out, kr_out):
    ctx = ExitStack()
    with ctx:
        def sem(name):
            return ctx.enter_context(nc.semaphore(name))

        def keep(name, shape, dt=F32, side="left"):
            return ctx.enter_context(nc.sbuf_tensor(name, shape, dt, side=side))

        def region(side, *specs):
            st = ExitStack()
            return st, [st.enter_context(nc.sbuf_tensor(n, s, d, side=side)) for n, s, d in specs]

        xT = keep("xT", [P, KD, T])
        zs = keep("zs", [P, KD, T])
        rlow_hi = keep("rlow_hi", [P, 8, 512], F32R)
        rlow_lo = keep("rlow_lo", [P, 8, 512], F32R)
        stage = keep("stage", [P, STAGES, 512])
        cc = keep("cc", [P, T])
        ss = keep("ss", [P, T])
        kr = keep("kr", [P, KEYS])
        vecs = keep("vecs", [P, NVEC])
        ones = keep("ones", [P, P])
        warm = keep("warm", [1, 1])
        mean_b = keep("mean_b", [P, T])
        rstd_b = keep("rstd_b", [P, T])
        var_b = keep("var_b", [P, T])
        early = keep("early", [1, P], BF16)
        neg = keep("neg", [1, CHUNK], BF16)
        negmax = keep("negmax", [P, 2, 2])
        rowmax = keep("rowmax", [P, 2, 2])
        rowsum = keep("rowsum", [P, 2, 2])
        rinv = keep("rinv", [P, 2, 2])
        sq = keep("sq", [P, 4, HB], F32, "right")

        left, (act_hi, act_lo, rtop_hi, rtop_lo) = region(
            "left", ("act_hi", [P, KD, T], F32R), ("act_lo", [P, KD, T], F32R),
            ("rtop_hi", [P, 8, 512], F32R), ("rtop_lo", [P, 8, 512], F32R))
        right, (y, v, sig, a_sb, prod, part, acc, state) = region(
            "right", ("y", [P, KD, T], F32), ("v", [P, 2, VCOLS], F32), ("sig", [P, T], F32),
            ("a_sb", [P, T], F32), ("prod", [P, PRODS, CCOLS], F32), ("part", [P, 2, CCOLS], F32),
            ("acc", [P, 2, CCOLS], F32), ("state", [P, KD, HIST], F32))
        right.close()
        qn_hi = keep("qn_hi", [P, KQ, T], F32R, "right")
        qn_lo = keep("qn_lo", [P, KQ, T], F32R, "right")
        c_hi = keep("c_hi", [P, KL, KEYS], F32R, "right")
        c_lo = keep("c_lo", [P, KL, KEYS], F32R, "right")
        right, (qa, cf, kr_ps) = region("right", ("qa", [P, KQ, T], F32), ("cf", [P, KL, KEYS], F32),
                                        ("kr_ps", [2 * ROPE, HB], F32))
        right.close()
        left.close()
        left, (kT, probs, qT, vt, ident) = region(
            "left", ("kT", [P, 2 * GH, KEYS], F32), ("probs", [P, 2, 2, 512], F32),
            ("qT", [P, 2 * GH, T], F32), ("vt", [P, 2 * KT, GH * VH], F32),
            ("ident", [P, P], F32))
        right, (pT, rope_a, rope_r) = region(
            "right", ("pT", [P, 2, 512], F32), ("rope_a", [P, 2, HB], F32), ("rope_r", [P, 2, T], F32))
        right.close()
        left.close()
        right, (fsq,) = region("right", ("fsq", [P, NB, 6, HB], F32))
        right.close()
        left, (o_hi, o_lo, btop_hi, btop_lo) = region(
            "left", ("o_hi", [P, KD, T], F32R), ("o_lo", [P, KD, T], F32R),
            ("btop_hi", [P, 8, 512], F32R), ("btop_lo", [P, 8, 512], F32R))
        left.close()

        diags = [cc[:, P * i:P * i + P] for i in range(4)] + [kr[:, P * i:P * i + P] for i in range(6)]
        eye = mean_b[:, 0:P]

        ps = ctx.enter_context(nc.psum_tensor("ps", [P, 8, 512], F32))

        x_in = [sem(f"x_in{i}") for i in range(4)]
        vecs_in, tables_in, state_in = sem("vecs_in"), sem("tables_in"), sem("state_in")
        cache_in, c_stored = sem("cache_in"), sem("c_stored")
        stage_in = [sem(f"stage_in{i}") for i in range(STAGES)]
        conv_out_done, rope_moved, krows_in, outs_done = (
            sem("conv_out_done"), sem("rope_moved"), sem("krows_in"), sem("outs_done"))
        hi_done = sem("hi_done")
        xsq_done, uhi_done = sem("xsq_done"), sem("uhi_done")
        sqrt_done = sem("sqrt_done")
        mt_evac, prod_done, ysq_done, gate_done = sem("mt_evac"), sem("prod_done"), sem("ysq_done"), sem("gate_done")
        diag_done = sem("diag_done")
        ln_silu, yz_hi = sem("ln_silu"), sem("yz_hi")
        o_evac, osq_done, hsq_done, xn_hi = sem("o_evac"), sem("osq_done"), sem("hsq_done"), sem("xn_hi")
        p_evac, psq_done, c_hi_done, qn_hi_done = sem("p_evac"), sem("psq_done"), sem("c_hi_done"), sem("qn_hi_done")
        g_evac_act, exp_done, pt_evac_act = sem("g_evac_act"), sem("exp_done"), sem("pt_evac_act")
        oo_hi, f_evac, fsq_done = sem("oo_hi"), sem("f_evac"), sem("fsq_done")
        const_set, dve_self, var_done, rstd_done = sem("const_set"), sem("dve_self"), sem("var_done"), sem("rstd_done")
        scaled = sem("scaled")
        u_full, u_lo = sem("u_full"), sem("u_lo")
        tap_done, y_ready = sem("tap_done"), sem("y_ready")
        ln_norm, yz_full = sem("ln_norm"), sem("yz_full")
        h_done, xn_full, xn_lo_dve = sem("h_done"), sem("xn_full"), sem("xn_lo_dve")
        xsum_done = sem("xsum_done")
        osum_done, hsum_done, qsum_done, fsum_done = sem("osum_done"), sem("hsum_done"), sem("qsum_done"), sem("fsum_done")
        kr_done, c_full, qn_full = sem("kr_done"), sem("c_full"), sem("qn_full")
        g_evac_dve, rope_done, max_done, prob_done, pt_evac_dve, att_done = (
            sem("g_evac_dve"), sem("rope_done"), sem("max_done"), sem("prob_done"), sem("pt_evac_dve"), sem("att_done"))
        oo_lo, y_done = sem("oo_lo"), sem("y_done")
        pool_self, y_done_pool = sem("pool_self"), sem("y_done_pool")
        pool_set, lo_done, v_done, padd_done = sem("pool_set"), sem("lo_done"), sem("v_done"), sem("padd_done")
        yz_lo, xn_lo, c_lo_done, qn_lo_done = sem("yz_lo"), sem("xn_lo"), sem("c_lo_done"), sem("qn_lo_done")
        xstat_done, mt_done, ystat_done, ymean_done, o_done, ostat_done, hstat_done = (
            sem("xstat_done"), sem("mt_done"), sem("ystat_done"), sem("ymean_done"), sem("o_done"), sem("ostat_done"), sem("hstat_done"))
        ptap_done = sem("ptap_done")
        p_done, pstat_done, g_done = sem("p_done"), sem("pstat_done"), sem("g_done")
        scores_done, pt_done, pv_done, f_done, fstat_done = (
            sem("scores_done"), sem("pt_done"), sem("pv_done"), sem("f_done"), sem("fstat_done"))

        def blk(b):
            return slice(b * HB, (b + 1) * HB)

        def pair(b0):
            return ps[:, b0:b0 + 2, 0:HB]

        def two(ap):
            return ap.rearrange("p (b t) -> p b t", b=NB)

        def slot(u):
            n = unit_cols(u)
            if u >= U_G:
                m = u - U_G
                if m < NG * GU + KD:
                    return rlow_hi[:, m % 8, 0:n], rlow_lo[:, m % 8, 0:n]
                return btop_hi[:, m % 8, 0:n], btop_lo[:, m % 8, 0:n]
            s = u % RING
            if s < 8:
                return rlow_hi[:, s, 0:n], rlow_lo[:, s, 0:n]
            return rtop_hi[:, s - 8, 0:n], rtop_lo[:, s - 8, 0:n]

        def wait_slot(act, u):
            if u < RING:
                return
            if u < U_KV:
                act.wait_ge(mt_done, 3 * (u // 8 - 1))
            elif u < U_Q:
                act.wait_ge(o_done, 12)
            elif u < U_Z:
                act.wait_ge(o_done, 16)
            elif u < U_Z + KD:
                act.wait_ge(p_done, TASKS3.index(("kv", 2, 1)) + 1)
            elif u < U_G:
                act.wait_ge(p_done, TASKS3.index(("q", 3, 1)) + 1)
            elif u < U_G + 8:
                act.wait_ge(p_done, TASKS3.index(("z", 3, 1)) + 1)
            elif u < U_BO + KD:
                g, i = divmod(u - U_G - 8, GU)
                act.wait_ge(g_done, NTASK * g + (QTASKS if i < KQ else NTASK))
            else:
                act.wait_ge(pv_done, NITEM)

        def unit_src(u):
            n = unit_cols(u)
            for first, src in ((U_BO, w_bo), (U_Q, None), (U_KV, w_kv), (U_AO, w_ao), (U_IN, w_in)):
                if u >= first:
                    break
            if src is not None:
                return src[u - first]
            if u < U_G:
                return w_bi[u - U_Q]
            g, i = divmod(u - U_G, GU)
            return w_qb[g * KQ + i] if i < KQ else w_kb[g * KL + i - KQ]

        def scale_unit(dve, u):
            raw = stage[:, u % STAGES, 0:unit_cols(u)]
            gain = unit_gain(u)
            dve.wait_ge(stage_in[u % STAGES], 16 * (u // STAGES + 1))
            nc.vector.tensor_scalar(raw, raw, vecs[:, gain:gain + 1], None, ALU.mult).then_inc(scaled, 1)

        def hi(act, u):
            act.wait_ge(stage_in[u % STAGES], 16 * (u // STAGES + 1))
            wait_slot(act, u)
            if unit_gain(u) is not None:
                act.wait_ge(scaled, u - U_KV + 1)
            nc.scalar.activation(slot(u)[0], stage[:, u % STAGES, 0:unit_cols(u)], ACT.Copy).then_inc(hi_done, 1)

        def lo(pool, u):
            pool.wait_ge(hi_done, u + 1)
            h, l = slot(u)
            nc.gpsimd.tensor_tensor(l, stage[:, u % STAGES, 0:unit_cols(u)], h.bitcast(F32),
                                    ALU.subtract).then_inc(lo_done, 1)

        def ready(pe, u):
            pe.wait_ge(lo_done, u + 1)

        def mm3(out, w, xh, xl, start, stop):
            wh, wl = w
            nc.tensor.matmul(out, wh, xh, start=start, stop=False)
            nc.tensor.matmul(out, wh, xl, start=False, stop=False)
            return nc.tensor.matmul(out, wl, xh, start=False, stop=stop)

        def cols(w, c, n=P):
            return w[0][:, c:c + n], w[1][:, c:c + n]

        block = ctx.enter_context(nc.Block())

        @block.sync
        def _(sp):
            def load(u):
                if u >= STAGES:
                    sp.wait_ge(lo_done, u - STAGES + 1)
                sp.dma_start(stage[:, u % STAGES, 0:unit_cols(u)], unit_src(u)).then_inc(stage_in[u % STAGES], 16)

            for i in range(4):
                b, k = i // 2, KD // 2 * (i % 2)
                sp.dma_start(xT[:, k:k + KD // 2, blk(b)], x_t[:, k:k + KD // 2, blk(b)]).then_inc(x_in[i], 16)
                if i == 1:
                    for u in range(3):
                        load(u)
            sp.dma_start(vecs[:], vecs_d).then_inc(vecs_in, 16)
            for u in range(3, 8):
                load(u)
            sp.dma_start(state[:], state_t).then_inc(state_in, 16)
            for j in range(KD):
                for u in range(8 * (j + 1), 8 * (j + 2)):
                    load(u)
                sp.wait_ge(v_done, j + 1)
                sp.dma_start(conv_out[:, j, 0:HIST], v[:, j % 2, SEQ:SEQ + HIST]).then_inc(conv_out_done, 16)
                sp.dma_start(conv_out[:, j, HIST:2 * HIST], v[:, j % 2, VCOLS - HIST:VCOLS]).then_inc(conv_out_done, 16)
            for u in range(U_AO + KD, U_KV):
                load(u)
            sp.wait_ge(ptap_done, 1)
            sp.dma_start(cc[:], cc_d).then_inc(tables_in, 16)
            sp.dma_start(ss[:], ss_d).then_inc(tables_in, 16)
            sp.dma_start(kr[ROPE:2 * ROPE, 0:T], krs_d).then_inc(tables_in, 16)
            sp.dma_start(kr[2 * ROPE:3 * ROPE, T:KEYS], ckr_t).then_inc(cache_in, 16)
            for u in range(U_KV, U_KV + 4):
                load(u)
            sp.wait_ge(yz_lo, 2 * KD)
            sp.dma_start(cf[:, :, T:KEYS], ckv_t).then_inc(cache_in, 16)
            for u in range(U_KV + 4, U_G + GU):
                load(u)
            sp.wait_ge(c_full, KL)
            sp.dma_start(c_out, cf[:, :, 0:T]).then_inc(c_stored, 16)
            sp.wait_ge(kr_done, 2)
            sp.dma_start(kr_out, kr[2 * ROPE:3 * ROPE, 0:T]).then_inc(outs_done, 16)
            for u in range(U_G + GU, U_G + 2 * GU):
                load(u)
            sp.wait_ge(p_done, len(TASKS3))
            for h in range(2 * GH):
                sp.dma_start(kT[2 * ROPE:3 * ROPE, h, :], kr[2 * ROPE:3 * ROPE, :]).then_inc(krows_in, 16)
            for g in range(NG):
                sp.wait_ge(rope_done, 2 * (g + 1))
                for i in range(GH):
                    h = GH * (g % 2) + i
                    for half in range(2):
                        sp.dma_start(qT[NOPE + 16 * half:NOPE + 16 * half + 16, h, :],
                                     rope_r[64 * half + 16 * i:64 * half + 16 * i + 16, g % 2, :]).then_inc(rope_moved, 16)
                if g:
                    first = U_G + GU * (g + 1)
                    for u in range(first, first + GU if g + 1 < NG else UNITS):
                        load(u)
            for n in range(2 * KD):
                b, i = divmod(n, KD)
                m = (0, 5, 1, 2, 6, 3, 4, 7)[i]
                if m < POOL_FINAL:
                    sp.wait_ge(y_done, POOL_FINAL * b + m + 1)
                else:
                    sp.wait_ge(y_done_pool, (KD - POOL_FINAL) * b + m - POOL_FINAL + 1)
                sp.dma_start(y_out[:, m, blk(b)], xT[:, m, blk(b)]).then_inc(outs_done, 16)
            sp.wait_ge(outs_done, 16 * (1 + 2 * KD))
            sp.wait_ge(c_stored, 16)
            sp.wait_ge(conv_out_done, 32 * KD)

        @block.scalar
        def _(act):
            def load_table(func):
                nc.scalar.activation(warm[:], ones[0:1, 0:1], func)

            act.wait_ge(const_set, 1)
            load_table(ACT.Sqrt)
            def xsquare(n):
                b, i = divmod(n, KD // 2)
                act.wait_ge(x_in[n // 2], 16)
                nc.scalar.activation(y[:, 2 * i:2 * i + 2, blk(b)], xT[:, 2 * i:2 * i + 2, blk(b)], ACT.Square).then_inc(xsq_done, 1)

            def sqrt_of(n, b=None):
                s = slice(0, T) if b is None else blk(b)
                act.wait_ge(var_done, n + 1)
                nc.scalar.activation(var_b[:, s], var_b[:, s], ACT.Sqrt).then_inc(sqrt_done, 1)

            for n in range(4):
                xsquare(n)
            hi(act, 0)
            hi(act, 1)
            sqrt_of(N_IN, 0)
            xsquare(4)
            xsquare(5)
            hi(act, 2)
            hi(act, 3)
            xsquare(6)
            xsquare(7)
            for n in range(2 * KD):
                b, k = divmod(n, KD)
                act.wait_ge(u_full, n + 1)
                nc.scalar.activation(act_hi[:, k, blk(b)], y[:, k, blk(b)], ACT.Copy).then_inc(uhi_done, 1)
                if n < 4:
                    hi(act, 4 + n)
                if n >= KD:
                    hi(act, n)
                if n == 6:
                    sqrt_of(N_IN + 1, 1)

            def ysquare(j):
                act.wait_ge(y_ready, j + 1)
                if j >= 2:
                    act.wait_ge(ystat_done, j - 1)
                nc.scalar.activation(sq[:, 2 * (j % 2):2 * (j % 2) + 2, :], two(y[:, j, :]), ACT.Square).then_inc(ysq_done, 1)

            def tap_product(j, i):
                w, after = tap_split(j)[1] + i, i + PRODS
                act.wait_ge(v_done, j + 1)
                if i >= PRODS:
                    act.wait_ge(padd_done, PADDS * j + max(1, i - PRODS))
                elif j:
                    act.wait_ge(padd_done, PADDS * (j - 1) + (after if after < POOL_TAPS else max(1, i)))
                nc.scalar.activation(prod[:, i % PRODS, :], v[:, j % 2, w:w + CCOLS], ACT.Copy,
                                     scale=vecs[:, V_DW + WIDTH * j + w:V_DW + WIDTH * j + w + 1]).then_inc(prod_done, 1)

            for j in range(KD):
                nxt = 8 * (j + 1)
                act.wait_ge(mt_done, 3 * j + 1)
                if j >= 1:
                    act.wait_ge(v_done, j)
                nc.scalar.activation(two(sig[:]), pair(2 * ((3 * j) % 2)), ACT.Sigmoid).then_inc(mt_evac, 1)

                def copy_a():
                    act.wait_ge(mt_done, 3 * j + 2)
                    nc.scalar.activation(two(a_sb[:]), pair(2 * ((3 * j + 1) % 2)), ACT.Copy).then_inc(mt_evac, 1)

                if j == 0:
                    copy_a()
                else:
                    for u in range(4):
                        hi(act, nxt + u)
                if j >= 2:
                    ysquare(j - 2)
                if j > 0:
                    copy_a()
                if j == 1:
                    for i in range(4):
                        hi(act, nxt + 4 + i)
                for i in range(WIDTH - tap_split(j)[1]):
                    if i < 4 and 2 <= j < KD - 1:
                        hi(act, nxt + 4 + i)
                    tap_product(j, i)
                    if i == 3:
                        act.wait_ge(mt_done, 3 * j + 3)
                        nc.scalar.activation(two(zs[:, j, :]), pair(2 * ((3 * j + 2) % 2)), ACT.Copy).then_inc(mt_evac, 1)
                if j == KD - 3:
                    act.wait_ge(pool_set, 2)
                    for i in range(PE_TAPS):
                        col = V_DW + WIDTH * (KD - 1) + LAST_DVE_TAPS + i
                        nc.scalar.activation(diags[i], eye, ACT.Copy, scale=vecs[:, col:col + 1]).then_inc(diag_done, 1)
            ysquare(KD - 2)
            act.wait_ge(mt_evac, 3 * KD)
            hi(act, U_AO + 4)
            for j in range(KD):
                nc.scalar.activation(zs[:, j, :], zs[:, j, :], ACT.Silu).then_inc(gate_done, 1)
            for u in range(U_AO + 5, U_AO + 7):
                hi(act, u)
            load_table(ACT.Sqrt)
            act.wait_ge(ystat_done, KD - 2)
            act.wait_ge(y_ready, KD)
            for b in range(NB):
                nc.scalar.activation(sq[:, 2 + b, :], y[:, KD - 1, blk(b)], ACT.Square).then_inc(ysq_done, 1)

            def evac_o(n):
                b, m = divmod(n, KD)
                act.wait_ge(o_done, n + 1)
                nc.scalar.activation(y[:, m, blk(b)], ps[:, n % 4, 0:HB], ACT.Square).then_inc(osq_done, 1)
                nc.scalar.activation(zs[:, m, blk(b)], ps[:, n % 4, 0:HB], ACT.Copy).then_inc(o_evac, 1)

            def split_yz(n):
                b, k = divmod(n, KD)
                act.wait_ge(yz_full, n + 1)
                nc.scalar.activation(act_hi[:, k, blk(b)], y[:, k, blk(b)], ACT.Copy).then_inc(yz_hi, 1)

            for b in range(NB):
                sqrt_of(N_LN + b, b)
            load_table(ACT.Silu)
            hi(act, U_AO + 7)
            for n in range(2 * KD):
                b, k = divmod(n, KD)
                act.wait_ge(ln_norm, n + 1)
                nc.scalar.activation(y[:, k, blk(b)], y[:, k, blk(b)], ACT.Silu, bias=vecs[:, V_BLN + k:V_BLN + k + 1],
                                     scale=vecs[:, V_GLN + k:V_GLN + k + 1]).then_inc(ln_silu, 1)
                if n >= 1:
                    split_yz(n - 1)
                if n in AO_AFTER:
                    hi(act, U_AO + KD + AO_AFTER.index(n))
                if n >= 12:
                    evac_o(n - 12)
            split_yz(2 * KD - 1)

            def hsquare(n):
                b, m = divmod(n, KD)
                act.wait_ge(h_done, n + 1)
                nc.scalar.activation(y[:, m, blk(b)], xT[:, m, blk(b)], ACT.Square).then_inc(hsq_done, 1)

            def xn_split(n):
                b, m = divmod(n, KD)
                act.wait_ge(xn_full, n + 1)
                nc.scalar.activation(act_hi[:, m, blk(b)], zs[:, m, blk(b)], ACT.Copy).then_inc(xn_hi, 1)

            def evac_p(p):
                kind, m, b = TASKS3[p]
                src = ps[:, p % 4, 0:HB]
                act.wait_ge(p_done, p + 1)
                if kind == "z":
                    nc.scalar.activation(zs[:, m, blk(b)], src, ACT.Silu).then_inc(p_evac, 1)
                elif kind == "q":
                    nc.scalar.activation(y[:, KL + m, blk(b)], src, ACT.Square).then_inc(psq_done, 1)
                    nc.scalar.activation(qa[:, m, blk(b)], src, ACT.Copy).then_inc(p_evac, 1)
                elif m < KL:
                    nc.scalar.activation(y[:, m, blk(b)], src, ACT.Square).then_inc(psq_done, 1)
                    nc.scalar.activation(cf[:, m, blk(b)], src, ACT.Copy).then_inc(p_evac, 1)
                else:
                    if b:
                        act.wait_ge(kr_done, 1)
                    nc.scalar.activation(kr_ps[:], ps[0:2 * ROPE, p % 4, 0:HB], ACT.Copy).then_inc(p_evac, 1)

            load_table(ACT.Sqrt)
            for n in range(4, 8):
                evac_o(n)
            sqrt_of(N_O[0], 0)
            for n, tiles in ((8, ()), (9, (0, 1, 2)), (10, (3, 4, 5, 6)), (11, (7,))):
                evac_o(n)
                for i in tiles:
                    hsquare(i)
            for u in range(U_KV, U_KV + 5):
                hi(act, u)
            sqrt_of(N_H[0], 0)
            evac_o(12)
            for u in range(U_KV + 5, U_KV + 7):
                hi(act, u)
            evac_o(13)
            for i in range(KD):
                xn_split(i)
            hi(act, U_KV + 7)
            evac_o(14)
            evac_o(15)
            for u in range(U_Q, U_Q + 4):
                hi(act, u)
            sqrt_of(N_O[1], 1)
            evac_p(0)
            for u in range(U_Q + 4, U_Q + 6):
                hi(act, u)
            evac_p(1)
            for i in range(2):
                hsquare(KD + 2 * i)
                hsquare(KD + 2 * i + 1)
                hi(act, U_Q + 6 + i)
            evac_p(2)
            for i in range(KD + 4, 2 * KD - 1):
                hsquare(i)
            evac_p(3)
            hsquare(2 * KD - 1)
            sqrt_of(N_H[1], 1)
            evac_p(4)
            for i in range(KD, KD + 4):
                xn_split(i)
            evac_p(5)
            for i in range(KD + 4, 2 * KD):
                xn_split(i)
            act.wait_ge(cache_in, 32)
            for k in range(KL):
                nc.scalar.activation(c_hi[:, k, T:KEYS], cf[:, k, T:KEYS], ACT.Copy).then_inc(c_hi_done, 1)
            for p in range(6, 10):
                evac_p(p)
            for p in range(10, ZTASK):
                for i in range(2):
                    hi(act, U_Z + 2 * (p - 10) + i)
                evac_p(p)
            sqrt_of(N_KV)
            sqrt_of(N_Q)
            for p in range(ZTASK, len(TASKS3)):
                evac_p(p)
                i = p - ZTASK
                if i < KD // 2:
                    hi(act, U_Z + KD + 2 * i)
                    hi(act, U_Z + KD + 2 * i + 1)
                if i >= KD:
                    hi(act, U_G + i - KD)
                if C_AT <= i < C_AT + KL:
                    k = i - C_AT
                    act.wait_ge(c_full, k + 1)
                    nc.scalar.activation(c_hi[:, k, 0:T], cf[:, k, 0:T], ACT.Copy).then_inc(c_hi_done, 1)
                if Q_AT <= i < Q_AT + KQ:
                    k = i - Q_AT
                    act.wait_ge(qn_full, k + 1)
                    nc.scalar.activation(qn_hi[:, k, :], qa[:, k, :], ACT.Copy).then_inc(qn_hi_done, 1)

            def gevac(n):
                g, i = divmod(n, NTASK)
                kind, m, half, eng = GTASKS[i]
                if eng != "act":
                    return
                bank = task_bank(n)
                act.wait_ge(g_done, n + 1)
                slot0 = GH * (g % 2) + 2 * m
                if kind == "nope":
                    for e in range(2):
                        last = nc.scalar.activation(qT[0:NOPE, slot0 + e, blk(half)], ps[64 * e:64 * e + 64, bank, 0:HB], ACT.Copy)
                elif kind == "k":
                    for e in range(2):
                        last = nc.scalar.activation(kT[0:NOPE, slot0 + e, 400 * half:400 * half + 400],
                                                    ps[64 * e:64 * e + 64, bank, 0:400], ACT.Copy)
                else:
                    rows = min(P, KEYS - P * m)
                    last = nc.scalar.activation(vt[0:rows, KT * (g % 2) + m, :], ps[0:rows, bank, 0:GH * VH], ACT.Copy)
                last.then_inc(g_evac_act, 1)

            for n in range(PROLOGUE):
                gevac(n)
            for u in range(U_G + KD, U_G + KD + 2):
                hi(act, u)

            def exps(i):
                s = i % NS
                act.wait_ge(max_done, i + 1)
                if i >= 2:
                    act.wait_ge(pt_done, i - 1)
                n, heads = (P * (s % 4 + 1), 2) if s < 8 else (SKEYS, 1)
                for e in range(heads):
                    last = nc.scalar.activation(probs[:, i % 2, e, 0:n], ps[:, 2 * (i % 2) + e, 0:n], ACT.Exp,
                                                bias=negmax[:, i % 2, e:e + 1], scale=SCALE,
                                                accum_out=rowsum[:, i % 2, e:e + 1])
                last.then_inc(exp_done, 1)

            def pt_evac(i):
                s = i % NS
                n = P * (s % 4 + 1) if s < 8 else 2 * P
                act.wait_ge(pt_done, i + 1)
                nc.scalar.activation(pT[:, 0, 0:n], ps[:, 4, 0:n], ACT.Copy).then_inc(pt_evac_act, 1)

            for i in range(STEPS):
                tasks = STEP_TASKS[i]
                if i >= 2 and i - 2 < ACT_PT:
                    pt_evac(i - 2)
                for n in tasks:
                    gevac(n)
                if i < NITEM:
                    exps(i)
                for u in AHEAD.get(i, ()):
                    hi(act, U_G + u)

            def oo_split(n):
                b, k = divmod(n, KD)
                nc.scalar.activation(o_hi[:, k, blk(b)], zs[:, k, blk(b)], ACT.Copy).then_inc(oo_hi, 1)

            def evac_f(n):
                m, b = FTASKS[n]
                act.wait_ge(f_done, n + 1)
                if m >= 6:
                    act.wait_ge(fsum_done, 1 + b)
                nc.scalar.activation(fsq[:, b, m if m < 6 else m - 4, :], ps[:, n % 4, 0:HB], ACT.Square).then_inc(fsq_done, 1)
                nc.scalar.activation(zs[:, m, blk(b)], ps[:, n % 4, 0:HB], ACT.Copy,
                                     scale=vecs[:, V_POST1 + m:V_POST1 + m + 1]).then_inc(f_evac, 1)

            act.wait_ge(att_done, NITEM)
            for n in range(2 * KD):
                oo_split(n)
            for i in range(KD):
                hi(act, U_BO + KD + i)
            for n in range(2 * KD):
                evac_f(n)
                if n == 12:
                    sqrt_of(N_F, 0)
            sqrt_of(N_F + 1, 1)

        @block.vector
        def _(dve):
            self_count = [0]

            def link(ins):
                self_count[0] += 1
                ins.then_inc(dve_self, 1)
                return self_count[0]

            nc.vector.memset(neg[:], NEG)
            nc.vector.memset(early[:, CHUNK:P], 0.0)
            nc.vector.memset(early[:, 0:CHUNK], 1.0)
            nc.vector.memset(ones[:], 1.0).then_inc(const_set, 1)

            def fold(sums, more, got, count, done, after=0):
                dve.wait_ge(got, count)
                if after:
                    dve.wait_ge(done, after)
                nc.vector.tensor_tensor(sums, sums, more, ALU.add).then_inc(done, 1)

            def variance(n, src, count, b=None):
                s = slice(0, T) if b is None else blk(b)
                dst = var_b[:, s] if b is not None else two(var_b[:])
                nc.vector.tensor_scalar(dst, src, 1.0 / count, EPS, ALU.mult, ALU.add).then_inc(var_done, 1)

            def inverse(n, dst, b=None):
                s = slice(0, T) if b is None else blk(b)
                dve.wait_ge(sqrt_done, n + 1)
                nc.vector.reciprocal(dst[:, s], var_b[:, s]).then_inc(rstd_done, 1)
                dve.wait_ge(rstd_done, n + 1)

            def xfold(b, i):
                if i < 4:
                    fold(y[:, 0:2, blk(b)], y[:, 2 * i:2 * i + 2, blk(b)], xsq_done, 4 * b + i + 1, xsum_done,
                         4 * b + i - 1 if i > 1 else 0)
                else:
                    fold(y[:, 0, blk(b)], y[:, 1, blk(b)], xsq_done, 4 * b + 4, xsum_done, 4 * b + 3)

            for i in range(1, 5):
                xfold(0, i)
            dve.wait_ge(xstat_done, 1)
            variance(N_IN, ps[:, 4, 0:HB], D, 0)
            inverse(N_IN, rstd_b, 0)

            def u_split(n):
                b, k = divmod(n, KD)
                dve.wait_ge(uhi_done, n + 1)
                nc.vector.tensor_tensor(act_lo[:, k, blk(b)], y[:, k, blk(b)], act_hi[:, k, blk(b)].bitcast(F32),
                                        ALU.subtract).then_inc(u_lo, 1)

            dve.wait_ge(vecs_in, 16)
            for n in range(2 * KD):
                b, k = divmod(n, KD)
                if n == 0:
                    xfold(1, 1)
                    xfold(1, 2)
                if n == 1:
                    xfold(1, 3)
                    xfold(1, 4)
                if n == 6:
                    dve.wait_ge(xstat_done, 2)
                    variance(N_IN + 1, ps[:, 5, 0:HB], D, 1)
                if n == KD:
                    inverse(N_IN + 1, rstd_b, 1)
                nc.vector.scalar_tensor_tensor(out=y[:, k, blk(b)], in0=xT[:, k, blk(b)],
                                               scalar=vecs[:, V_PRE0 + k:V_PRE0 + k + 1],
                                               in1=rstd_b[:, blk(b)], op0=ALU.mult, op1=ALU.mult).then_inc(u_full, 1)
                if n:
                    u_split(n - 1)
            u_split(2 * KD - 1)

            taps_issued = 0
            for j in range(KD):
                dve.wait_ge(v_done, j + 1)
                if j:
                    dve.wait_ge(y_ready, j)
                for w in range(tap_split(j)[0]):
                    dst = acc[:, w % 2, :]
                    src = v[:, j % 2, w:w + CCOLS]
                    tap = vecs[:, V_DW + WIDTH * j + w:V_DW + WIDTH * j + w + 1]
                    if w == 0:
                        ins = nc.vector.tensor_scalar(dst, src, tap, vecs[:, V_BDW + j:V_BDW + j + 1], ALU.mult, ALU.add)
                    elif w == 1:
                        ins = nc.vector.tensor_scalar(dst, src, tap, None, ALU.mult)
                    else:
                        dve.wait_ge(tap_done, taps_issued - 1)
                        ins = nc.vector.scalar_tensor_tensor(out=dst, in0=src, scalar=tap, in1=dst,
                                                             op0=ALU.mult, op1=ALU.add)
                    ins.then_inc(tap_done, 1)
                    taps_issued += 1
                dve.wait_ge(tap_done, taps_issued)
                nc.vector.tensor_tensor(acc[:, 0, :], acc[:, 0, :], acc[:, 1, :], ALU.add).then_inc(tap_done, 1)
                taps_issued += 1
                dve.wait_ge(tap_done, taps_issued)
                dve.wait_ge(padd_done, PADDS * j + WIDTH - tap_split(j)[1] - 1)
                last = j == KD - 1
                outs = (acc[:, 0, 0:SEQ], acc[:, 0, SEQ + HIST:CCOLS]) if last else (y[:, j, 0:SEQ], y[:, j, SEQ:T])
                nc.vector.tensor_tensor(outs[0], acc[:, 0, 0:SEQ], part[:, j % 2, 0:SEQ], ALU.add)
                ins = nc.vector.tensor_tensor(outs[1], acc[:, 0, SEQ + HIST:CCOLS], part[:, j % 2, SEQ + HIST:CCOLS],
                                              ALU.add)
                if last:
                    ins.then_inc(tap_done, 1)
                    taps_issued += 1
                    dve.wait_ge(tap_done, taps_issued)
                    dve.wait_ge(ptap_done, 1)
                    nc.vector.tensor_tensor(y[:, j, 0:SEQ], outs[0], ps[:, 0, 0:SEQ], ALU.add)
                    ins = nc.vector.tensor_tensor(y[:, j, SEQ:T], outs[1], ps[:, 1, 0:DEC], ALU.add)
                ins.then_inc(y_ready, 1)

            def moments(b):
                s = blk(b)
                dve.wait_ge(ymean_done, b + 1)
                n = link(nc.vector.tensor_scalar(mean_b[:, s], ps[:, 4 + b, 0:HB], 1.0 / D, None, ALU.mult))
                dve.wait_ge(dve_self, n)
                n = link(nc.vector.tensor_tensor(rstd_b[:, s], mean_b[:, s], mean_b[:, s], ALU.mult))
                dve.wait_ge(dve_self, n)
                dve.wait_ge(ystat_done, KD + b)
                n = link(nc.vector.scalar_tensor_tensor(out=var_b[:, s], in0=ps[:, 6 + b, 0:HB], scalar=1.0 / D,
                                                        in1=rstd_b[:, s], op0=ALU.mult, op1=ALU.subtract))
                dve.wait_ge(dve_self, n)
                nc.vector.tensor_scalar(var_b[:, s], var_b[:, s], 0.0, EPS, ALU.max, ALU.add).then_inc(var_done, 1)

            def centre(n):
                b, k = divmod(n, KD)
                return link(nc.vector.tensor_tensor(y[:, k, blk(b)], y[:, k, blk(b)], mean_b[:, blk(b)], ALU.subtract))

            def gate(n):
                b, k = divmod(n, KD)
                dve.wait_ge(ln_silu, n + 1)
                dve.wait_ge(gate_done, k + 1)
                nc.vector.tensor_tensor(y[:, k, blk(b)], y[:, k, blk(b)], zs[:, k, blk(b)], ALU.mult).then_inc(yz_full, 1)

            moments(0)
            moments(1)
            inverse(N_LN, rstd_b, 0)
            centred = centre(0)
            for n in range(2 * KD):
                b, k = divmod(n, KD)
                following = centre(n + 1) if n + 1 < 2 * KD else 0
                if n == KD:
                    inverse(N_LN + 1, rstd_b, 1)
                dve.wait_ge(dve_self, centred)
                nc.vector.tensor_tensor(y[:, k, blk(b)], y[:, k, blk(b)], rstd_b[:, blk(b)], ALU.mult).then_inc(ln_norm, 1)
                centred = following
                if n >= 1:
                    gate(n - 1)
            gate(2 * KD - 1)

            def residual(b, gain, evacuated, count, done, between=None):
                def scale(m):
                    dve.wait_ge(evacuated, count)
                    return link(nc.vector.scalar_tensor_tensor(
                        out=zs[:, m, blk(b)], in0=zs[:, m, blk(b)], scalar=vecs[:, gain + m:gain + m + 1],
                        in1=rstd_b[:, blk(b)], op0=ALU.mult, op1=ALU.mult))
                scaled_at = scale(0)
                for m in range(KD):
                    following = scale(m + 1) if m + 1 < KD else 0
                    dve.wait_ge(dve_self, scaled_at)
                    nc.vector.tensor_tensor(xT[:, m, blk(b)], xT[:, m, blk(b)], zs[:, m, blk(b)], ALU.add).then_inc(done, 1)
                    scaled_at = following
                    if between is not None:
                        between(m)

            def rotate_keys(b):
                dve.wait_ge(p_evac, TASKS3.index(("kv", 2, b)) + 1)
                if b == 0:
                    dve.wait_ge(tables_in, 48)
                dst = kr[2 * ROPE:3 * ROPE, blk(b)]
                tmp = var_b[2 * ROPE:3 * ROPE, blk(b)]
                nc.vector.tensor_tensor(dst, kr_ps[0:ROPE, :], cc[0:ROPE, blk(b)], ALU.mult)
                n = link(nc.vector.tensor_tensor(tmp, kr_ps[ROPE:2 * ROPE, :], kr[ROPE:2 * ROPE, blk(b)], ALU.mult))
                dve.wait_ge(dve_self, n)
                nc.vector.tensor_tensor(dst, dst, tmp, ALU.add).then_inc(kr_done, 1)

            def ofold(b, i):
                fold(y[:, 0:2, blk(b)], y[:, 2 * i:2 * i + 2, blk(b)], osq_done, KD * b + 2 * i + 2, osum_done,
                     3 * b + i - 1 if i > 1 else 0)

            def hfold(b, i):
                fold(y[:, 0:2, blk(b)], y[:, 2 * i:2 * i + 2, blk(b)], hsq_done, KD * b + 2 * i + 2, hsum_done,
                     3 * b + i - 1 if i > 1 else 0)

            def xn_rest_dve(n):
                b, m = divmod(n, KD)
                dve.wait_ge(xn_hi, n + 1)
                nc.vector.tensor_tensor(act_lo[:, m, blk(b)], zs[:, m, blk(b)], act_hi[:, m, blk(b)].bitcast(F32),
                                        ALU.subtract).then_inc(xn_lo_dve, 1)

            for u in range(U_KV, U_KV + 5):
                scale_unit(dve, u)
            for i in range(1, 4):
                ofold(0, i)
            for b in range(NB):
                dve.wait_ge(ostat_done, b + 1)
                variance(N_O[b], ps[:, 4 + b, 0:HB], D, b)
                inverse(N_O[b], rstd_b, b)

                def between(m, b=b):
                    if m == 5:
                        hfold(b, 1)
                    if m == 7:
                        hfold(b, 2)
                    if b and m < 4:
                        scale_unit(dve, U_Q + 4 + m)

                residual(b, V_POST0, o_evac, KD * (b + 1), h_done, between)
                hfold(b, 3)
                if b == 0:
                    ofold(1, 1)
                dve.wait_ge(hstat_done, b + 1)
                variance(N_H[b], ps[:, 6 + b, 0:HB], D, b)
                if b == 0:
                    scale_unit(dve, U_KV + 5)
                    scale_unit(dve, U_KV + 6)
                inverse(N_H[b], mean_b, b)
                dve.wait_ge(h_done, KD * (b + 1))
                for m in range(KD):
                    nc.vector.tensor_tensor(zs[:, m, blk(b)], xT[:, m, blk(b)], mean_b[:, blk(b)], ALU.mult).then_inc(xn_full, 1)
                    if m >= 2 and m % 2 == 0:
                        xn_rest_dve(KD * b + m - 1)
                    if b == 0 and m == 1:
                        scale_unit(dve, U_KV + 7)
                xn_rest_dve(KD * b + KD - 1)
                if b == 0:
                    ofold(1, 2)
                    ofold(1, 3)
                    for u in range(U_Q, U_Q + 4):
                        scale_unit(dve, u)

            def qfold(b):
                fold(y[:, KL:KL + 2, blk(b)], y[:, KL + 2:KL + 4, blk(b)], psq_done,
                     (KL + KQ) * (b + 1), qsum_done)

            rotate_keys(0)
            qfold(0)
            for u in range(U_Z, U_Z + 2):
                scale_unit(dve, u)
            dve.wait_ge(rstd_done, N_H[1] + 1)
            for u in range(U_Z + 2, U_Z + 5):
                scale_unit(dve, u)
            rotate_keys(1)
            for u in range(U_Z + 5, U_Z + KD):
                scale_unit(dve, u)
            qfold(1)
            for u in range(U_Z + KD, U_Z + KD + 4):
                scale_unit(dve, u)
            dve.wait_ge(kr_done, 2)
            dve.wait_ge(pstat_done, 1)
            variance(N_KV, pair(4), LORA)
            inverse(N_KV, rstd_b)
            for u in range(U_Z + KD + 4, U_Z + KD + 5):
                scale_unit(dve, u)
            dve.wait_ge(pstat_done, 2)
            variance(N_Q, pair(6), QL)
            for k in range(KL):
                nc.vector.scalar_tensor_tensor(out=cf[:, k, 0:T], in0=cf[:, k, 0:T], scalar=vecs[:, V_KVA + k:V_KVA + k + 1],
                                               in1=rstd_b[:], op0=ALU.mult, op1=ALU.mult).then_inc(c_full, 1)
            dve.wait_ge(c_full, KL)
            inverse(N_Q, rstd_b)
            for u in range(U_Z + KD + 5, U_G):
                scale_unit(dve, u)
            for k in range(KQ):
                nc.vector.scalar_tensor_tensor(out=qa[:, k, :], in0=qa[:, k, :], scalar=vecs[:, V_QA + k:V_QA + k + 1],
                                               in1=rstd_b[:], op0=ALU.mult, op1=ALU.mult).then_inc(qn_full, 1)

            def gevac(n):
                g, i = divmod(n, NTASK)
                kind, m, half, eng = GTASKS[i]
                if eng != "dve":
                    return
                bank = task_bank(n)
                dve.wait_ge(g_done, n + 1)
                if kind == "rope":
                    src = ps[:, bank, 0:HB]
                    if g >= 2 and half == 0:
                        dve.wait_ge(rope_moved, 128 * (g - 1))
                    if g or half:
                        dve.wait_ge(rope_done, 2 * g + half)
                    nc.vector.tensor_tensor(rope_a[:, 0, :], src, cc[:, blk(half)], ALU.mult)
                    nc.vector.tensor_tensor(rope_a[0:64, 1, :], src[64:128], ss[64:128, blk(half)], ALU.mult)
                    at = link(nc.vector.tensor_tensor(rope_a[64:128, 1, :], src[0:64], ss[0:64, blk(half)], ALU.mult))
                    dve.wait_ge(dve_self, at)
                    nc.vector.tensor_tensor(rope_r[:, g % 2, blk(half)], rope_a[:, 0, :], rope_a[:, 1, :],
                                            ALU.add).then_inc(rope_done, 1)
                    dve.wait_ge(rope_done, 2 * g + half + 1)
                    dve.sem_inc(g_evac_dve, 1)
                    return
                if kind == "k":
                    slot0 = GH * (g % 2) + 2 * m
                    for e in range(2):
                        last = nc.vector.tensor_copy(kT[0:NOPE, slot0 + e, 400 * half:400 * half + 400],
                                                     ps[64 * e:64 * e + 64, bank, 0:400])
                else:
                    rows = min(P, KEYS - P * m)
                    last = nc.vector.tensor_copy(vt[0:rows, KT * (g % 2) + m, :], ps[0:rows, bank, 0:GH * VH])
                last.then_inc(g_evac_dve, 1)

            def maxima(i):
                s = i % NS
                n, heads = (P * (s % 4 + 1), 2) if s < 8 else (SKEYS, 1)
                for e in range(heads):
                    dve.wait_ge(scores_done, 2 * i + (e + 1 if heads == 2 else 2))
                    at = link(nc.vector.reduce_max(rowmax[:, i % 2, e:e + 1], ps[:, 2 * (i % 2) + e, 0:n], axis=AX_X))
                if i >= 2:
                    dve.wait_ge(exp_done, i - 1)
                dve.wait_ge(dve_self, at)
                nc.vector.tensor_scalar(negmax[:, i % 2, 0:heads], rowmax[:, i % 2, 0:heads], -SCALE, None,
                                        ALU.mult).then_inc(max_done, 1)

            def pt_evac(i):
                s = i % NS
                dve.wait_ge(pt_done, i + 1)
                if i >= ACT_PT:
                    n = P * (s % 4 + 1) if s < 8 else 2 * P
                    nc.vector.tensor_copy(pT[:, 0, 0:n], ps[:, 4, 0:n])
                if s < 8:
                    n = P * (s % 4 + 1)
                    nc.vector.tensor_copy(pT[:, 1, 0:n], ps[:, 5, 0:n]).then_inc(pt_evac_dve, 1)
                else:
                    nc.vector.tensor_copy(pT[0:SKEYS - 2 * P, 1, 0:P], ps[0:SKEYS - 2 * P, 5, 0:P]).then_inc(pt_evac_dve, 1)

            def normalise(i):
                s = i % NS
                n, heads = (P * (s % 4 + 1), 2) if s < 8 else (SKEYS, 1)
                dve.wait_ge(exp_done, i + 1)
                at = link(nc.vector.reciprocal(rinv[:, i % 2, 0:heads], rowsum[:, i % 2, 0:heads]))
                dve.wait_ge(dve_self, at)
                for e in range(heads):
                    last = nc.vector.tensor_scalar(probs[:, i % 2, e, 0:n], probs[:, i % 2, e, 0:n],
                                                   rinv[:, i % 2, e:e + 1], None, ALU.mult)
                last.then_inc(prob_done, 1)

            def gated(i):
                g, s = divmod(i, NS)
                dve.wait_ge(pv_done, i + 1)
                if s < 8:
                    m, q = 2 * g + s // 4, P * (s % 4)
                    nc.vector.tensor_tensor(zs[:, m, q:q + P], ps[:, out_bank(i), 0:P], zs[:, m, q:q + P], ALU.mult).then_inc(att_done, 1)
                else:
                    dst = zs[:, 2 * g:2 * g + 2, SEQ:T]
                    nc.vector.tensor_tensor(dst, ps[:, out_bank(i), 0:2 * DEC].rearrange("p (m q) -> p m q", m=2), dst,
                                            ALU.mult).then_inc(att_done, 1)

            dve.wait_ge(c_stored, 16)
            for n in range(PROLOGUE):
                gevac(n)
            dve.wait_ge(p_evac, len(TASKS3))
            for i in range(STEPS):
                tasks = STEP_TASKS[i]
                if i >= 2:
                    pt_evac(i - 2)
                for n in tasks[:1]:
                    gevac(n)
                if 1 <= i <= NITEM:
                    normalise(i - 1)
                if i < NITEM:
                    maxima(i)
                if i >= 2:
                    gated(i - 2)
                for n in tasks[1:]:
                    gevac(n)

            for n in range(2 * KD):
                b, k = divmod(n, KD)
                dve.wait_ge(oo_hi, n + 1)
                nc.vector.tensor_tensor(o_lo[:, k, blk(b)], zs[:, k, blk(b)], o_hi[:, k, blk(b)].bitcast(F32),
                                        ALU.subtract).then_inc(oo_lo, 1)
            for b, more, count in ((0, 2, 4), (1, 2, 8), (0, 4, 10), (0, 2, 12)):
                fold(fsq[:, b, 0:2, :], fsq[:, b, more:more + 2, :], fsq_done, count, fsum_done, {10: 1, 12: 3}.get(count, 0))
            for b in range(NB):
                dve.wait_ge(fstat_done, b + 1)
                variance(N_F + b, ps[:, 4 + b, 0:HB], D, b)
                inverse(N_F + b, rstd_b, b)

                dve.wait_ge(f_evac, (12, 16)[b])
                for m in range(POOL_FINAL + 1):
                    if m < POOL_FINAL:
                        at = link(nc.vector.tensor_tensor(zs[:, m, blk(b)], zs[:, m, blk(b)], rstd_b[:, blk(b)], ALU.mult))
                    if m:
                        dve.wait_ge(dve_self, before)
                        nc.vector.tensor_tensor(xT[:, m - 1, blk(b)], xT[:, m - 1, blk(b)], zs[:, m - 1, blk(b)],
                                                ALU.add).then_inc(y_done, 1)
                    before = at
                if b == 0:
                    fold(fsq[:, 1, 0:2, :], fsq[:, 1, 4:6, :], fsq_done, 14, fsum_done, 2)

        @block.gpsimd
        def _(pool):
            nc.gpsimd.memset(v[:, :, 0:HIST], 0.0)
            nc.gpsimd.memset(eye, 0.0).then_inc(pool_set, 1)
            pool.wait_ge(pool_set, 1)
            nc.gpsimd.affine_select(out=eye, in_=eye, compare_op=ALU.not_equal, fill=1.0, base=0,
                                    pattern=[[-1, P]], channel_multiplier=1).then_inc(pool_set, 1)
            for u in range(2 * KD):
                lo(pool, u)

            pool.wait_ge(state_in, 16)
            for j in range(KD):
                nxt = 8 * (j + 1)
                last = j == KD - 1
                if 0 < j < KD - 1:
                    for u in range(4):
                        lo(pool, nxt + u)
                if j >= 2:
                    pool.wait_ge(y_ready, j - 1)
                    pool.wait_ge(conv_out_done, 32 * (j - 1))
                nc.gpsimd.tensor_copy(v[:, j % 2, HIST + SEQ:2 * HIST + SEQ], state[:, j, :])
                pool.wait_ge(mt_evac, 3 * j + 2)
                nc.gpsimd.tensor_tensor(v[:, j % 2, HIST:HIST + SEQ], a_sb[:, 0:SEQ], sig[:, 0:SEQ], ALU.mult)
                nc.gpsimd.tensor_tensor(v[:, j % 2, 2 * HIST + SEQ:VCOLS], a_sb[:, SEQ:T], sig[:, SEQ:T],
                                        ALU.mult).then_inc(v_done, 1)
                if j == 1:
                    for i in range(4):
                        lo(pool, nxt + 4 + i)
                elif j > 1 and not last:
                    lo(pool, nxt + 4)
                for i in range(1, WIDTH - tap_split(j)[1]):
                    if i < 4 and 2 <= j < KD - 1:
                        lo(pool, nxt + 4 + i)
                    pool.wait_ge(prod_done, POOL_TAPS * j + i + 1)
                    p = part[:, j % 2, :]
                    if i >= 2:
                        pool.wait_ge(padd_done, PADDS * j + i - 1)
                    nc.gpsimd.tensor_tensor(p, prod[:, i % PRODS, :], prod[:, 0, :] if i == 1 else p,
                                            ALU.add).then_inc(padd_done, 1)
            for u in range(U_AO, U_AO + KD):
                lo(pool, u)

            def rest(full, half, low, n, done, got):
                pool.wait_ge(got, n)
                nc.gpsimd.tensor_tensor(low, full, half.bitcast(F32), ALU.subtract).then_inc(done, 1)

            for n in range(2 * KD):
                b, k = divmod(n, KD)
                rest(y[:, k, blk(b)], act_hi[:, k, blk(b)], act_lo[:, k, blk(b)], n + 1, yz_lo, yz_hi)
                if n + 1 in AO_AFTER:
                    lo(pool, U_AO + KD + AO_AFTER.index(n + 1))

            def xn_rest(n):
                b, m = divmod(n, KD)
                rest(zs[:, m, blk(b)], act_hi[:, m, blk(b)], act_lo[:, m, blk(b)], n + 1, xn_lo, xn_hi)

            for u in range(U_KV, U_KV + 7):
                lo(pool, u)
            for n in range(0, KD, 2):
                xn_rest(n)
            for u in range(U_KV + 7, U_Z):
                lo(pool, u)
            for n in range(KD, 2 * KD, 2):
                xn_rest(n)
            for k in range(KL):
                rest(cf[:, k, T:KEYS], c_hi[:, k, T:KEYS], c_lo[:, k, T:KEYS], k + 1, c_lo_done, c_hi_done)
            for u in range(U_Z, U_Z + KD):
                lo(pool, u)
            for i in range(2 * KD):
                if i < KD // 2:
                    lo(pool, U_Z + KD + 2 * i)
                    lo(pool, U_Z + KD + 2 * i + 1)
                if i >= KD:
                    lo(pool, U_G + i - KD)
                if C_AT <= i < C_AT + KL:
                    k = i - C_AT
                    rest(cf[:, k, 0:T], c_hi[:, k, 0:T], c_lo[:, k, 0:T], KL + k + 1, c_lo_done, c_hi_done)
                if Q_AT <= i < Q_AT + KQ:
                    k = i - Q_AT
                    rest(qa[:, k, :], qn_hi[:, k, :], qn_lo[:, k, :], k + 1, qn_lo_done, qn_hi_done)
            pool.wait_ge(p_done, len(TASKS3))
            nc.gpsimd.memset(ident[:], 0.0).then_inc(pool_set, 1)
            pool.wait_ge(pool_set, 3)
            nc.gpsimd.affine_select(out=ident[:], in_=ident[:], compare_op=ALU.not_equal, fill=1.0, base=0,
                                    pattern=[[-1, P]], channel_multiplier=1).then_inc(pool_set, 1)
            for u in range(U_G + KD, UNITS):
                lo(pool, u)

            for b in range(NB):
                pool.wait_ge(rstd_done, N_F + b + 1)
                pool.wait_ge(f_evac, (12, 16)[b])
                for m in range(POOL_FINAL, KD):
                    nc.gpsimd.tensor_tensor(zs[:, m, blk(b)], zs[:, m, blk(b)], rstd_b[:, blk(b)],
                                            ALU.mult).then_inc(pool_self, 1)
                    if m > POOL_FINAL:
                        pool.wait_ge(pool_self, (KD - POOL_FINAL) * b + m - POOL_FINAL)
                        nc.gpsimd.tensor_tensor(xT[:, m - 1, blk(b)], xT[:, m - 1, blk(b)], zs[:, m - 1, blk(b)],
                                                ALU.add).then_inc(y_done_pool, 1)
                pool.wait_ge(pool_self, (KD - POOL_FINAL) * (b + 1))
                nc.gpsimd.tensor_tensor(xT[:, KD - 1, blk(b)], xT[:, KD - 1, blk(b)], zs[:, KD - 1, blk(b)],
                                        ALU.add).then_inc(y_done_pool, 1)

        @block.tensor
        def _(pe):
            def sums(bank, src, k, done=None):
                ins = nc.tensor.matmul(ps[:, bank, 0:HB], ones[:], src, start=k == 0, stop=k == KD - 1)
                if done is not None:
                    ins.then_inc(done, 1)

            pe.wait_ge(const_set, 1)

            def xstat(b):
                pe.wait_ge(xsum_done, 4 * (b + 1))
                nc.tensor.matmul(ps[:, 4 + b, 0:HB], ones[:], y[:, 0, blk(b)], start=True, stop=True).then_inc(xstat_done, 1)

            xstat(0)

            def ystats(j):
                last = j == KD - 1
                pe.wait_ge(y_ready, j + 1)
                for b in range(NB):
                    sums(4 + b, y[:, j, blk(b)], j, ymean_done if last else None)
                for b in range(NB):
                    pe.wait_ge(ysq_done, j + 1 + (b if last else 0))
                    sums(6 + b, sq[:, 2 * (j % 2) + b, :], j, ystat_done if b or last else None)

            for j in range(KD):
                if j == 0:
                    for b in range(NB):
                        for k in range(KD):
                            if b == 0:
                                ready(pe, k)
                                if k == 4:
                                    xstat(1)
                            pe.wait_ge(u_lo, KD * b + k + 1)
                            for t in range(2):
                                last = mm3(ps[:, 2 * t + b, 0:HB], cols(slot(k), P * t), act_hi[:, k, blk(b)],
                                           act_lo[:, k, blk(b)], k == 0, k == KD - 1)
                                if b and k == KD - 1:
                                    last.then_inc(mt_done, 1)
                for i in range(2 if j == 0 else 0, 3):
                    t = 3 * j + i
                    if t >= 2:
                        pe.wait_ge(mt_evac, t - 1)
                    for k in range(KD):
                        if i == 0:
                            ready(pe, 8 * j + k)
                        w = cols(slot(8 * j + k), P * i)
                        for b in range(NB):
                            last = mm3(ps[:, 2 * (t % 2) + b, 0:HB], w, act_hi[:, k, blk(b)], act_lo[:, k, blk(b)],
                                       k == 0, k == KD - 1)
                    last.then_inc(mt_done, 1)
                if j >= 2:
                    ystats(j - 2)

            pe.wait_ge(mt_evac, 3 * KD - 1)
            pe.wait_ge(v_done, KD)
            pe.wait_ge(diag_done, PE_TAPS)
            for i in range(PE_TAPS):
                w = LAST_DVE_TAPS + i
                first, last = i == 0, i == PE_TAPS - 1
                nc.tensor.matmul(ps[:, 0, 0:SEQ], diags[i], v[:, (KD - 1) % 2, w:w + SEQ], start=first, stop=last)
                ins = nc.tensor.matmul(ps[:, 1, 0:DEC], diags[i], v[:, (KD - 1) % 2, w + SEQ + HIST:w + CCOLS],
                                       start=first, stop=last)
            ins.then_inc(ptap_done, 1)
            ystats(KD - 2)
            ystats(KD - 1)

            def product(bank, units, m, b, kts, stats=None, fresh=None):
                for k in kts:
                    if m == 0 and b == 0:
                        ready(pe, units + k)
                    if fresh is not None:
                        fresh(k)
                    last = mm3(ps[:, bank, 0:HB], cols(slot(units + k), P * m), act_hi[:, k, blk(b)],
                               act_lo[:, k, blk(b)], k == 0, k == KD - 1)
                    if stats is not None and k == KD // 2 - 1:
                        stats()
                return last

            def square_sums(bank, src, tiles=2):
                for i in range(tiles):
                    last = nc.tensor.matmul(ps[:, bank, 0:HB], ones[:], src[:, i, :], start=i == 0, stop=i == tiles - 1)
                return last

            def ostat(b):
                pe.wait_ge(osum_done, 3 * (b + 1))
                square_sums(4 + b, y[:, 0:2, blk(b)]).then_inc(ostat_done, 1)

            def hstat(b):
                pe.wait_ge(hsum_done, 3 * (b + 1))
                square_sums(6 + b, y[:, 0:2, blk(b)]).then_inc(hstat_done, 1)

            pe.wait_ge(mt_evac, 3 * KD)
            for k in range(KD):
                pe.wait_ge(yz_lo, k + 1)
                for m in range(4):
                    last = product(m, U_AO, m, 0, [k])
                    if k == KD - 1:
                        last.then_inc(o_done, 1)
            for n in range(4, 2 * KD):
                b, m = divmod(n, KD)
                pe.wait_ge(o_evac, n - 3)
                if n == KD:
                    pe.wait_ge(yz_lo, 2 * KD)
                product(n % 4, U_AO + 8 * (m // 4), m % 4, b, range(KD),
                        {KD: lambda: ostat(0), KD + 4: lambda: hstat(0)}.get(n)).then_inc(o_done, 1)

            def cstat():
                pe.wait_ge(psq_done, 2 * KL + KQ)
                for b in range(NB):
                    last = square_sums(4 + b, y[:, 0:KL, blk(b)], KL)
                last.then_inc(pstat_done, 1)

            def qstat():
                pe.wait_ge(qsum_done, 2)
                for b in range(NB):
                    last = square_sums(6 + b, y[:, KL:KL + 2, blk(b)])
                last.then_inc(pstat_done, 1)

            for p, (kind, m, b) in enumerate(TASKS3):
                if p >= 4:
                    pe.wait_ge(p_evac, p - 3)
                else:
                    pe.wait_ge(o_evac, 13 + p)
                units, col = {"kv": (U_KV, m), "q": (U_Q, m), "z": (U_Z + 8 * (m // 4), m % 4)}[kind]
                if kind == "kv" and m == KL:
                    for k in range(KD):
                        last = mm3(ps[0:2 * ROPE, p % 4, 0:HB], cols(slot(U_KV + k), LORA, 2 * ROPE),
                                   act_hi[:, k, blk(b)], act_lo[:, k, blk(b)], k == 0, k == KD - 1)
                    last.then_inc(p_done, 1)
                    continue

                def xn_ready(k, b=b):
                    pe.wait_ge(xn_lo_dve if k % 2 else xn_lo, KD // 2 * b + k // 2 + 1)

                stats = {0: lambda: ostat(1), 4: lambda: hstat(1), 10: lambda: cstat(), ZTASK: lambda: qstat()}.get(p)
                product(p % 4, units, col, b, range(KD), stats,
                        xn_ready if (kind, m) == ("kv", 0) else None).then_inc(p_done, 1)

            def wait_evacs(n):
                if n:
                    pe.wait_ge(g_evac_act, evacs("act", n - 1))
                    pe.wait_ge(g_evac_dve, evacs("dve", n - 1))

            def gtask(n):
                g, i = divmod(n, NTASK)
                kind, m, half, _ = GTASKS[i]
                bank = task_bank(n)
                prev = n - 4 if n < PROLOGUE else n - 2
                if prev >= 0:
                    eng = GTASKS[prev % NTASK][3]
                    pe.wait_ge(g_evac_act if eng == "act" else g_evac_dve, evacs(eng, prev))
                base = U_G + GU * g
                if i == 0:
                    ready(pe, base + KQ - 1)
                    if g == 0:
                        pe.wait_ge(qn_lo_done, KQ)
                if kind == "k" and m == half == 0:
                    ready(pe, base + GU - 1)
                    if g == 0:
                        pe.wait_ge(c_lo_done, 2 * KL)
                if kind in ("rope", "nope"):
                    for k in range(KQ):
                        last = mm3(ps[:, bank, 0:HB], cols(slot(base + k), P * m), qn_hi[:, k, blk(half)],
                                   qn_lo[:, k, blk(half)], k == 0, k == KQ - 1)
                elif kind == "k":
                    keys = slice(400 * half, 400 * half + 400)
                    for k in range(KL):
                        last = mm3(ps[:, bank, 0:400], cols(slot(base + KQ + k), P * m), c_hi[:, k, keys],
                                   c_lo[:, k, keys], k == 0, k == KL - 1)
                else:
                    rows = min(P, KEYS - P * m)
                    keys = slice(P * m, P * m + rows)
                    for k in range(KL):
                        wh, wl = cols(slot(base + KQ + k), GH * NOPE, GH * VH)
                        out = ps[0:rows, bank, 0:GH * VH]
                        nc.tensor.matmul(out, c_hi[:, k, keys], wh, start=k == 0, stop=False)
                        nc.tensor.matmul(out, c_hi[:, k, keys], wl, start=False, stop=False)
                        last = nc.tensor.matmul(out, c_lo[:, k, keys], wh, start=False, stop=k == KL - 1)
                last.then_inc(g_done, 1)

            for n in range(PROLOGUE):
                gtask(n)

            def scores(i):
                g, s = divmod(i, NS)
                if i >= 2:
                    pe.wait_ge(exp_done, i - 1)
                if i == 0:
                    pe.wait_ge(p_evac, len(TASKS3))
                    pe.wait_ge(krows_in, 16 * 2 * GH)
                wait_evacs(tasks_needed(i))
                if s == 0:
                    pe.wait_ge(rope_moved, 128 * (g + 1))
                if s < 8:
                    q, n = P * (s % 4), P * (s % 4 + 1)
                    for e in range(2):
                        h = GH * (g % 2) + 2 * (s // 4) + e
                        bank = 2 * (i % 2) + e
                        if e == 1 and i >= 3:
                            pe.wait_ge(att_done, i - 2)
                        nc.tensor.matmul(ps[:, bank, 0:n], qT[0:NOPE + ROPE, h, q:q + P], kT[0:NOPE + ROPE, h, 0:n],
                                         start=True, stop=True)
                        nc.tensor.matmul(ps[:, bank, n - CHUNK:n], early[:], neg[:], start=False, stop=True,
                                         skip_group_check=True).then_inc(scores_done, 1)
                else:
                    for e in range(GH):
                        h = GH * (g % 2) + e
                        last = nc.tensor.matmul(ps[DEC * e:DEC * e + DEC, 2 * (i % 2), 0:SKEYS],
                                                qT[0:NOPE + ROPE, h, SEQ:T], kT[0:NOPE + ROPE, h, SEQ:KEYS],
                                                start=True, stop=True)
                    last.then_inc(scores_done, 2)

            def transposes(i):
                s = i % NS
                pe.wait_ge(prob_done, i + 1)
                if i == 0:
                    wait_evacs(PROLOGUE)
                if i >= 1:
                    pe.wait_ge(pt_evac_act, min(i, ACT_PT))
                    pe.wait_ge(pt_evac_dve, i)
                if s < 8:
                    for e in range(2):
                        for t in range(s % 4 + 1):
                            last = nc.tensor.transpose(ps[:, 4 + e, P * t:P * t + P], probs[:, i % 2, e, P * t:P * t + P], ident[:])
                else:
                    for t in range(3):
                        n = min(P, SKEYS - P * t)
                        last = nc.tensor.transpose(ps[0:n, 4 + t // 2, P * (t % 2):P * (t % 2) + P],
                                                   probs[:, i % 2, 0, P * t:P * t + n], ident[:])
                last.then_inc(pt_done, 1)

            def values(i):
                g, s = divmod(i, NS)
                pe.wait_ge(pt_evac_act, min(i + 1, ACT_PT))
                pe.wait_ge(pt_evac_dve, i + 1)
                if i + 1 < NITEM:
                    pe.wait_ge(exp_done, i + 2)
                v0 = KT * (g % 2)
                if s < 8:
                    for t in range(s % 4 + 1):
                        for e in range(2):
                            col = VH * (2 * (s // 4) + e)
                            last = nc.tensor.matmul(ps[64 * e:64 * e + 64, out_bank(i), 0:P], vt[:, v0 + t, col:col + VH],
                                                    pT[:, e, P * t:P * t + P], start=t == 0, stop=t == s % 4)
                else:
                    for m in range(2):
                        for t in range(3):
                            n = min(P, SKEYS - P * t)
                            for e in range(2):
                                h = 2 * m + e
                                last = nc.tensor.matmul(ps[64 * e:64 * e + 64, out_bank(i), DEC * m:DEC * m + DEC],
                                                        vt[0:n, v0 + 4 + t, VH * h:VH * h + VH],
                                                        pT[0:n, t // 2, P * (t % 2) + DEC * h:P * (t % 2) + DEC * h + DEC],
                                                        start=t == 0, stop=t == 2)
                last.then_inc(pv_done, 1)

            pe.wait_ge(pool_set, 4)
            for i in range(STEPS):
                tasks = STEP_TASKS[i]
                if i >= 2:
                    transposes(i - 2)
                for n in tasks[:1]:
                    gtask(n)
                if i < NITEM:
                    scores(i)
                if i >= 2:
                    values(i - 2)
                for n in tasks[1:]:
                    gtask(n)

            def fstat(b):
                pe.wait_ge(fsum_done, (4, 5)[b])
                slots = (0, 1) if b == 0 else (0, 1, 2, 3)
                for i in slots:
                    if i >= 2:
                        pe.wait_ge(fsq_done, 13 + i)
                    last = nc.tensor.matmul(ps[:, 4 + b, 0:HB], ones[:], fsq[:, b, i, :], start=i == 0, stop=i == slots[-1])
                last.then_inc(fstat_done, 1)

            def fproduct(n, kts):
                m, b = FTASKS[n]
                for k in kts:
                    last = mm3(ps[:, n % 4, 0:HB], cols(slot(U_BO + 8 * (m // 4) + k), P * (m % 4)), o_hi[:, k, blk(b)],
                               o_lo[:, k, blk(b)], k == 0, k == KD - 1)
                return last

            ready(pe, U_BO + KD - 1)
            for k in range(KD):
                pe.wait_ge(oo_lo, k + 1)
                for n in range(4):
                    last = fproduct(n, [k])
                    if k == KD - 1:
                        last.then_inc(f_done, 1)
            for n in range(4, 2 * KD):
                pe.wait_ge(f_evac, n - 3)
                if n == 4:
                    pe.wait_ge(oo_lo, 2 * KD)
                if n == 8:
                    ready(pe, UNITS - 1)
                fproduct(n, range(KD)).then_inc(f_done, 1)
                if n == 12:
                    fstat(0)
            fstat(1)


def kernel(x_prompt, x_sample, state_conv, cache_kv_latent, cache_k_rope,
           g_pre, g_post, w_a_in, w_a_dw, b_a_dw, g_a_ln, b_a_ln, w_a_out,
           g_kv_in, w_kv_a, g_kv_a, w_kv_b, w_b_in, g_q_a, w_q_b, w_b_out):
    import numpy as np
    import concourse.bacc as bacc
    from concourse import mybir as mb
    from concourse.bass_utils import run_bass_kernel_spmd

    f = lambda a: np.asarray(a)

    def tiles(a):
        return f(a).reshape(-1, P, a.shape[-1])

    def columns(a):
        return f(a).reshape(-1, P).T

    def rows(a):
        return f(a).T.reshape(-1, P, a.shape[0]).transpose(1, 0, 2)

    x = np.concatenate([f(x_prompt)[0], f(x_sample)[0]], axis=0)
    win = tiles(w_a_in[0]).reshape(KD, P, 3, KD, P)
    win = win[:, :, [1, 0, 2]].transpose(3, 0, 1, 2, 4).reshape(KD * KD, P, 3 * P)

    def chunks(a, n=512):
        t = tiles(a)
        return t.reshape(t.shape[0], P, -1, n).transpose(2, 0, 1, 3).reshape(-1, P, n)

    wkv = tiles(w_kv_a)
    half = ROPE // 2
    wkv = np.concatenate([wkv, wkv[..., LORA + half:], wkv[..., LORA:LORA + half]], axis=-1)
    wqb = tiles(w_q_b[0]).reshape(KQ, P, NG, GH, NOPE + ROPE)
    nope = wqb[..., :NOPE].reshape(KQ, P, NG, GH * NOPE)
    rope = wqb[..., NOPE:].reshape(KQ, P, NG, GH, 2, half).transpose(0, 1, 2, 4, 3, 5).reshape(KQ, P, NG, GH * ROPE)
    wqb = np.concatenate([nope, rope], axis=-1).transpose(2, 0, 1, 3).reshape(NG * KQ, P, 3 * P)
    wkb = tiles(w_kv_b).reshape(KL, P, NG, GH, 2, NOPE).transpose(2, 0, 1, 4, 3, 5).reshape(NG * KL, P, 2 * GH * NOPE)

    vec = np.concatenate(
        [columns(g_pre[0]), columns(g_pre[1]), columns(g_post[0]), columns(g_post[1]),
         f(w_a_dw)[0].T.reshape(KD, P, WIDTH).transpose(1, 0, 2).reshape(P, KD * WIDTH),
         columns(b_a_dw[0]), columns(g_a_ln[0]), columns(b_a_ln[0]), columns(g_kv_in), columns(g_kv_a),
         columns(g_q_a[0])], axis=1)

    pos = np.concatenate([np.arange(SEQ), PAST + np.arange(DEC)]).astype(np.float32)
    inv = (np.float32(10000.0) ** (-np.arange(half, dtype=np.float32) / np.float32(half))).astype(np.float32)
    ang = inv[:, None] * pos[None, :]
    cos, sin = np.cos(ang).astype(np.float32), np.sin(ang).astype(np.float32)
    cc = np.tile(cos, (8, 1))
    ss = np.concatenate([np.tile(sin, (4, 1)), -np.tile(sin, (4, 1))], axis=0)
    krs = np.concatenate([-sin, sin], axis=0)

    arrays = {
        "x_t": rows(x), "state_t": rows(f(state_conv)[0, 0]), "ckv_t": rows(f(cache_kv_latent)[0]),
        "ckr_t": f(cache_k_rope)[0].T, "w_in": win, "w_ao": chunks(w_a_out[0]), "w_kv": wkv,
        "w_bi": chunks(w_b_in[0]), "w_qb": wqb, "w_kb": wkb, "w_bo": chunks(w_b_out[0]),
        "vecs_d": vec, "cc_d": cc, "ss_d": ss, "krs_d": krs,
    }
    arrays = {k: np.ascontiguousarray(a) for k, a in arrays.items()}
    outs = {"y_out": (P, KD, T), "conv_out": (P, KD, 2 * HIST), "c_out": (P, KL, T), "kr_out": (ROPE, T)}

    nc = bacc.Bacc("TRN2", target_bir_lowering=False, num_devices=1)
    args = [nc.dram_tensor(k, a.shape, mb.dt.from_np(a.dtype), kind="ExternalInput").ap() for k, a in arrays.items()]
    args += [nc.dram_tensor(k, s, mb.dt.float32, kind="ExternalOutput").ap() for k, s in outs.items()]
    build(nc, *args)
    r = run_bass_kernel_spmd(nc, [arrays], core_ids=[0]).results[0]

    def tokens(a):
        a = np.asarray(a)
        return np.ascontiguousarray(a.transpose(2, 1, 0).reshape(a.shape[2], -1))

    yt, ct, cv, krt = tokens(r["y_out"]), tokens(r["c_out"]), tokens(r["conv_out"]), np.asarray(r["kr_out"]).T
    return (yt[None, :SEQ], yt[None, SEQ:], cv[None, None, :HIST], ct[None, :SEQ], np.ascontiguousarray(krt[None, :SEQ]),
            cv[None, None, HIST:], ct[None, SEQ:], np.ascontiguousarray(krt[None, SEQ:]))
```
